# Optimizing a Trainium2 kernel written in Bass

```python
import math
import jax
import jax.numpy as jnp
from jax import lax
import numpy as np

D_MODEL = 1024
BATCH = 1
SEQ = 512
DEPTH = 1
DEC_BATCH = 8
DEC_SEQ = 4
PAST_LEN = 2048
PAGE_SIZE = 128

MIX_WIDTH = D_MODEL
A_HEAD_DIM = 64
A_HEADS = MIX_WIDTH // 2 // A_HEAD_DIM
DILATED_BRANCHES = ((128, 1), (512, 4), (2048, 16))
MAX_WINDOW = 2048
BAND_BLOCK = 128
ROPE_THETA = 10000.0
B_KEY_DIM = 128
B_VAL_DIM = 128
B_HEADS = MIX_WIDTH // 2 // B_VAL_DIM
CONV_WIDTH = 4
DELTA_CHUNK = 64
B_QKV = B_HEADS * (2 * B_KEY_DIM + B_VAL_DIM)
SPLITS = (A_HEADS * A_HEAD_DIM,) * 3 + (B_HEADS * B_KEY_DIM, B_HEADS * B_KEY_DIM, B_HEADS * B_VAL_DIM, B_HEADS * B_VAL_DIM, B_HEADS, B_HEADS)
SPLIT_POINTS = tuple(sum(SPLITS[:i + 1]) for i in range(len(SPLITS) - 1))
IN_WIDTH = sum(SPLITS)
PEER_HEADS = 8
PEER_KEYS = 128
PEER_EXPERTS = PEER_KEYS * PEER_KEYS
PEER_QUERY_DIM = 256
PEER_TOPK = 16
PEER_BLOCK = 256
EPS = 1e-6

kernel_name = 'hybrid_dilated_attn_gdn_peer_step'

def rms_norm(x, w):
    x32 = x.astype(jnp.float32)
    y = x32 * lax.rsqrt(jnp.mean(x32 * x32, axis=-1, keepdims=True) + EPS)
    return (y * w.astype(jnp.float32)).astype(x.dtype)

def l2_normalize(x):
    x32 = x.astype(jnp.float32)
    return x32 * lax.rsqrt(jnp.sum(x32 * x32, axis=-1, keepdims=True) + EPS)

def rope(x, pos):
    half = x.shape[-1] // 2
    inv_freq = ROPE_THETA ** (-jnp.arange(half, dtype=jnp.float32) / half)
    ang = pos.astype(jnp.float32)[:, None] * inv_freq[None, :]
    cos = jnp.cos(ang)[None, :, None, :]
    sin = jnp.sin(ang)[None, :, None, :]
    x32 = x.astype(jnp.float32)
    x1, x2 = x32[..., :half], x32[..., half:]
    return jnp.concatenate([x1 * cos - x2 * sin, x2 * cos + x1 * sin], axis=-1).astype(x.dtype)

def masked_softmax(scores, mask):
    scores = jnp.where(mask, scores, -jnp.inf)
    mx = jnp.max(scores, axis=-1, keepdims=True)
    p = jnp.exp(scores - mx)
    l = jnp.sum(p, axis=-1, keepdims=True)
    return p / l, (mx + jnp.log(l))[..., 0]

def dilated_branch_prompt(q, k, v, window, dilation):
    b, s, h, dh = q.shape
    n_back = window // dilation
    m = -(-s // dilation)
    mp = -(-m // BAND_BLOCK) * BAND_BLOCK
    nb = mp // BAND_BLOCK

    def by_residue(t):
        t = jnp.pad(t, ((0, 0), (0, m * dilation - s), (0, 0), (0, 0)))
        t = t.reshape(b, m, dilation, h, dh).transpose(0, 2, 1, 3, 4)
        t = jnp.pad(t, ((0, 0), (0, 0), (0, mp - m), (0, 0), (0, 0)))
        return t.reshape(b, dilation, nb, BAND_BLOCK, h, dh)

    def band(t):
        prev = jnp.pad(t, ((0, 0), (0, 0), (1, 0), (0, 0), (0, 0), (0, 0)))[:, :, :-1]
        return jnp.concatenate([prev, t], axis=3)

    qb = by_residue(q)
    kk = band(by_residue(k))
    vv = band(by_residue(v))
    scores = jnp.einsum('brnqhe,brnkhe->brnhqk', qb, kk) / math.sqrt(dh)
    qi = jnp.arange(BAND_BLOCK)[:, None]
    kj = jnp.arange(2 * BAND_BLOCK)[None, :]
    dist = BAND_BLOCK + qi - kj
    in_band = (dist >= 0) & (dist <= n_back)
    has_prev = (jnp.arange(nb) > 0)[:, None, None] | (kj >= BAND_BLOCK)[None]
    mask = (in_band[None] & has_prev)[None, None, :, None]
    probs, lse = masked_softmax(scores, mask)
    out = jnp.einsum('brnhqk,brnkhe->brnqhe', probs, vv)
    lse = jnp.swapaxes(lse, 3, 4)

    def back(t):
        t = t.reshape((b, dilation, mp) + t.shape[4:])[:, :, :m]
        return jnp.moveaxis(t, 1, 2).reshape((b, m * dilation) + t.shape[3:])[:, :s]

    return back(out), back(lse)

def dilated_branch_sample(q, kc, vc, window, dilation):
    b, l, h, dh = q.shape
    w_len = kc.shape[1] - l
    n_back = window // dilation
    idx = w_len + jnp.arange(l)[:, None] - dilation * jnp.arange(n_back + 1)[None, :]
    valid = idx >= 0
    idx = jnp.maximum(idx, 0)
    kg = kc[:, idx].astype(jnp.float32)
    vg = vc[:, idx].astype(jnp.float32)
    scores = jnp.einsum('blhe,blnhe->blhn', q, kg) / math.sqrt(dh)
    probs, lse = masked_softmax(scores, valid[None, :, None, :])
    out = jnp.einsum('blhn,blnhe->blhe', probs, vg)
    return out, lse

def merge_branches(outs, lses):
    w = jax.nn.softmax(jnp.stack(lses), axis=0)
    return jnp.sum(w[..., None] * jnp.stack(outs), axis=0)

def short_conv(x_ext, conv_w):
    y = lax.conv_general_dilated(x_ext, conv_w[:, None, :].astype(x_ext.dtype), window_strides=(1,), padding='VALID', dimension_numbers=('NWC', 'WIO', 'NWC'), feature_group_count=x_ext.shape[-1])
    return jax.nn.silu(y)

def gated_delta_rule(q, k, v, g, beta, s0):
    b, t, h, _ = q.shape
    dv = v.shape[-1]
    c = DELTA_CHUNK
    nc = -(-t // c)
    pad = nc * c - t

    def chunks(x):
        x = jnp.pad(x, ((0, 0), (0, pad)) + ((0, 0),) * (x.ndim - 2))
        x = x.reshape((b, nc, c) + x.shape[2:])
        return jnp.moveaxis(x, 3, 1)

    qc, kc, vc, gc, bc = chunks(q), chunks(k), chunks(v), chunks(g), chunks(beta)
    gcum = jnp.cumsum(gc, axis=-1)
    ii = jnp.arange(c)[:, None]
    jj = jnp.arange(c)[None, :]
    causal = ii >= jj
    strict = ii > jj
    decay = jnp.exp(jnp.where(causal, gcum[..., :, None] - gcum[..., None, :], -jnp.inf))
    kb = kc * bc[..., None]
    lower = jnp.where(strict, jnp.einsum('bhnid,bhnjd->bhnij', kb, kc) * decay, 0.0)
    a_mat = jnp.eye(c, dtype=jnp.float32) + lower
    rhs = jnp.concatenate([vc * bc[..., None], kb * jnp.exp(gcum)[..., None]], axis=-1)
    sol = lax.linalg.triangular_solve(a_mat, rhs, left_side=True, lower=True, unit_diagonal=True)
    u, w = sol[..., :dv], sol[..., dv:]
    intra = jnp.where(causal, jnp.einsum('bhnid,bhnjd->bhnij', qc, kc) * decay, 0.0)
    q_dec = qc * jnp.exp(gcum)[..., None]
    k_dec = kc * jnp.exp(gcum[..., -1:] - gcum)[..., None]
    chunk_decay = jnp.exp(gcum[..., -1])
    xs = (jnp.moveaxis(q_dec, 2, 0), jnp.moveaxis(k_dec, 2, 0), jnp.moveaxis(u, 2, 0), jnp.moveaxis(w, 2, 0), jnp.moveaxis(intra, 2, 0), jnp.moveaxis(chunk_decay, 2, 0))

    def step(state, inp):
        qd, kd, uc, wc, att, cd = inp
        v_new = uc - jnp.einsum('bhck,bhkv->bhcv', wc, state)
        out = jnp.einsum('bhck,bhkv->bhcv', qd, state) + jnp.einsum('bhij,bhjv->bhiv', att, v_new)
        state = state * cd[..., None, None] + jnp.einsum('bhck,bhcv->bhkv', kd, v_new)
        return state, out

    s_fin, outs = lax.scan(step, s0, xs)
    o = jnp.moveaxis(outs, 0, 2).reshape(b, h, nc * c, dv)[:, :, :t]
    return jnp.moveaxis(o, 1, 2), s_fin

def peer(xn, w_pq, sub_keys, expert_u, expert_v):
    n_tok, d = xn.shape
    n_blk = -(-n_tok // PEER_BLOCK)
    xb = jnp.pad(xn, ((0, n_blk * PEER_BLOCK - n_tok), (0, 0))).reshape(n_blk, PEER_BLOCK, d)
    half = PEER_QUERY_DIM // 2

    def block(xt):
        qh = (xt @ w_pq).astype(jnp.float32).reshape(PEER_BLOCK, PEER_HEADS, 2, half)
        sub = jnp.einsum('thcd,ckd->thck', qh, sub_keys.astype(jnp.float32))
        top_s, top_i = lax.top_k(sub, PEER_TOPK)
        cand = (top_s[:, :, 0, :, None] + top_s[:, :, 1, None, :]).reshape(PEER_BLOCK, PEER_HEADS, PEER_TOPK * PEER_TOPK)
        best_s, best_c = lax.top_k(cand, PEER_TOPK)
        i1 = jnp.take_along_axis(top_i[:, :, 0], best_c // PEER_TOPK, axis=-1)
        i2 = jnp.take_along_axis(top_i[:, :, 1], best_c % PEER_TOPK, axis=-1)
        experts = i1 * PEER_KEYS + i2
        gate = jax.nn.softmax(best_s, axis=-1)
        pre = jnp.einsum('td,thkd->thk', xt, expert_u[experts]).astype(jnp.float32)
        act = jax.nn.gelu(pre, approximate=False)
        return jnp.einsum('thk,thkd->td', (gate * act).astype(xt.dtype), expert_v[experts])

    return lax.map(block, xb).reshape(n_blk * PEER_BLOCK, d)[:n_tok]

def decoder_layer(x, pos, k_past, v_past, conv_buf, s0, norm_mix_w, w_in, q_norm_w, k_norm_w, conv_w, a_log, dt_bias, delta_norm_w, w_out, norm_ffn_w, w_pq, sub_keys, expert_u, expert_v):
    b, t, _ = x.shape
    xn = rms_norm(x, norm_mix_w)
    aq, ak, av, bq, bk, bv, bz, bb, ba = jnp.split(xn @ w_in, SPLIT_POINTS, axis=-1)

    q = rope(rms_norm(aq.reshape(b, t, A_HEADS, A_HEAD_DIM), q_norm_w), pos)
    k = rope(rms_norm(ak.reshape(b, t, A_HEADS, A_HEAD_DIM), k_norm_w), pos)
    v = av.reshape(b, t, A_HEADS, A_HEAD_DIM)
    q32 = q.astype(jnp.float32)
    if k_past is None:
        k32, v32 = k.astype(jnp.float32), v.astype(jnp.float32)
        branches = [dilated_branch_prompt(q32, k32, v32, wnd, dil) for wnd, dil in DILATED_BRANCHES]
        win = min(MAX_WINDOW, t)
        k_buf, v_buf = k[:, t - win:], v[:, t - win:]
    else:
        kc = jnp.concatenate([k_past, k.astype(k_past.dtype)], axis=1)
        vc = jnp.concatenate([v_past, v.astype(v_past.dtype)], axis=1)
        branches = [dilated_branch_sample(q32, kc, vc, wnd, dil) for wnd, dil in DILATED_BRANCHES]
        win = k_past.shape[1]
        k_buf, v_buf = kc[:, kc.shape[1] - win:], vc[:, vc.shape[1] - win:]
    a_out = merge_branches([o for o, _ in branches], [l for _, l in branches])
    a_out = a_out.reshape(b, t, A_HEADS * A_HEAD_DIM).astype(x.dtype)

    raw = jnp.concatenate([bq, bk, bv], axis=-1)
    ext = jnp.concatenate([conv_buf.astype(raw.dtype), raw], axis=1)
    conv_state = ext[:, ext.shape[1] - (CONV_WIDTH - 1):]
    cq, ck, cv = jnp.split(short_conv(ext, conv_w), (B_HEADS * B_KEY_DIM, 2 * B_HEADS * B_KEY_DIM), axis=-1)
    dq = l2_normalize(cq.reshape(b, t, B_HEADS, B_KEY_DIM)) * (B_KEY_DIM ** -0.5)
    dk = l2_normalize(ck.reshape(b, t, B_HEADS, B_KEY_DIM))
    dv = cv.reshape(b, t, B_HEADS, B_VAL_DIM).astype(jnp.float32)
    beta = jax.nn.sigmoid(bb.astype(jnp.float32))
    g = -jnp.exp(a_log.astype(jnp.float32)) * jax.nn.softplus(ba.astype(jnp.float32) + dt_bias.astype(jnp.float32))
    o, s_fin = gated_delta_rule(dq, dk, dv, g, beta, s0.astype(jnp.float32))
    o = rms_norm(o, delta_norm_w) * jax.nn.silu(bz.reshape(b, t, B_HEADS, B_VAL_DIM).astype(jnp.float32))
    b_out = o.reshape(b, t, B_HEADS * B_VAL_DIM).astype(x.dtype)

    h = x + jnp.concatenate([a_out, b_out], axis=-1) @ w_out
    hn = rms_norm(h, norm_ffn_w)
    y = h + peer(hn.reshape(b * t, -1), w_pq, sub_keys, expert_u, expert_v).reshape(b, t, -1)
    return y, k_buf, v_buf, conv_state, s_fin.astype(s0.dtype)

def setup_inputs(seed: int = 0) -> dict:
    key = jax.random.key(seed)
    ks = jax.random.split(key, 24)
    win_buf = min(MAX_WINDOW, PAST_LEN)

    def nrm(k, shape, scale):
        return jax.random.normal(k, shape, jnp.float32) * scale

    dt = jnp.exp(jax.random.uniform(ks[9], (DEPTH, B_HEADS), jnp.float32, math.log(1e-3), math.log(1e-1)))
    return {
        'x_prompt': nrm(ks[0], (BATCH, SEQ, D_MODEL), 1.0),
        'x_sample': nrm(ks[1], (DEC_BATCH, DEC_SEQ, D_MODEL), 1.0),
        'cache_k_win': nrm(ks[2], (DEPTH, DEC_BATCH, win_buf, A_HEADS, A_HEAD_DIM), 1.0),
        'cache_v_win': nrm(ks[3], (DEPTH, DEC_BATCH, win_buf, A_HEADS, A_HEAD_DIM), 1.0),
        'state_conv': nrm(ks[4], (DEPTH, DEC_BATCH, CONV_WIDTH - 1, B_QKV), 1.0),
        'state_delta': nrm(ks[5], (DEPTH, DEC_BATCH, B_HEADS, B_KEY_DIM, B_VAL_DIM), 0.05),
        'norm_mix_w': 1.0 + nrm(ks[6], (DEPTH, D_MODEL), 0.02),
        'w_in': nrm(ks[7], (DEPTH, D_MODEL, IN_WIDTH), D_MODEL ** -0.5),
        'q_norm_w': 1.0 + nrm(ks[8], (DEPTH, A_HEAD_DIM), 0.02),
        'k_norm_w': 1.0 + nrm(ks[10], (DEPTH, A_HEAD_DIM), 0.02),
        'conv_w': nrm(ks[11], (DEPTH, CONV_WIDTH, B_QKV), CONV_WIDTH ** -0.5),
        'a_log': jnp.log(jax.random.uniform(ks[12], (DEPTH, B_HEADS), jnp.float32, 1.0, 16.0)),
        'dt_bias': dt + jnp.log(-jnp.expm1(-dt)),
        'delta_norm_w': 1.0 + nrm(ks[13], (DEPTH, B_VAL_DIM), 0.02),
        'w_out': nrm(ks[14], (DEPTH, MIX_WIDTH, D_MODEL), MIX_WIDTH ** -0.5),
        'norm_ffn_w': 1.0 + nrm(ks[15], (DEPTH, D_MODEL), 0.02),
        'w_pq': nrm(ks[16], (DEPTH, D_MODEL, PEER_HEADS * PEER_QUERY_DIM), D_MODEL ** -0.5),
        'sub_keys': nrm(ks[17], (DEPTH, 2, PEER_KEYS, PEER_QUERY_DIM // 2), (PEER_QUERY_DIM // 2) ** -0.5),
        'expert_u': nrm(ks[18], (DEPTH, PEER_EXPERTS, D_MODEL), D_MODEL ** -0.5),
        'expert_v': nrm(ks[19], (DEPTH, PEER_EXPERTS, D_MODEL), PEER_HEADS ** -0.5),
    }

def reference(x_prompt, x_sample, cache_k_win, cache_v_win, state_conv, state_delta, norm_mix_w, w_in, q_norm_w, k_norm_w, conv_w, a_log, dt_bias, delta_norm_w, w_out, norm_ffn_w, w_pq, sub_keys, expert_u, expert_v):
    bp, sp, _ = x_prompt.shape
    pos_prompt = jnp.arange(sp)
    pos_sample = PAST_LEN + jnp.arange(x_sample.shape[1])
    yp, ys = x_prompt, x_sample
    kp_l, vp_l, cp_l, dp_l, ks_l, vs_l, cs_l, ds_l = [], [], [], [], [], [], [], []
    for layer in range(DEPTH):
        weights = (norm_mix_w[layer], w_in[layer], q_norm_w[layer], k_norm_w[layer], conv_w[layer], a_log[layer], dt_bias[layer], delta_norm_w[layer], w_out[layer], norm_ffn_w[layer], w_pq[layer], sub_keys[layer], expert_u[layer], expert_v[layer])
        conv0 = jnp.zeros((bp, CONV_WIDTH - 1, B_QKV), x_prompt.dtype)
        s_zero = jnp.zeros((bp, B_HEADS, B_KEY_DIM, B_VAL_DIM), jnp.float32)
        yp, kb, vb, cb, sb = decoder_layer(yp, pos_prompt, None, None, conv0, s_zero, *weights)
        kp_l.append(kb)
        vp_l.append(vb)
        cp_l.append(cb)
        dp_l.append(sb)
        ys, kb, vb, cb, sb = decoder_layer(ys, pos_sample, cache_k_win[layer], cache_v_win[layer], state_conv[layer], state_delta[layer], *weights)
        ks_l.append(kb)
        vs_l.append(vb)
        cs_l.append(cb)
        ds_l.append(sb)
    k_win_prompt, v_win_prompt = jnp.stack(kp_l), jnp.stack(vp_l)
    conv_prompt, delta_prompt = jnp.stack(cp_l), jnp.stack(dp_l)
    k_win_sample, v_win_sample = jnp.stack(ks_l), jnp.stack(vs_l)
    conv_sample, delta_sample = jnp.stack(cs_l), jnp.stack(ds_l)
    return (yp, ys, k_win_prompt, v_win_prompt, conv_prompt, delta_prompt, k_win_sample, v_win_sample, conv_sample, delta_sample)


_drawn_inputs = setup_inputs


def setup_inputs(seed=0):
    import zlib

    import numpy as np

    out = dict(_drawn_inputs(seed))
    spreads = {}
    factors = {'q_norm_w': 57.838, 'delta_norm_w': 8.776, 'norm_ffn_w': 10.502}
    for name, (base, spread) in spreads.items():
        noise = np.random.default_rng([zlib.crc32(name.encode()), seed]).standard_normal(out[name].shape)
        drawn = base * np.exp(spread * noise) if base else spread * noise
        out[name] = jnp.asarray(drawn.astype(out[name].dtype))
    for name, factor in factors.items():
        out[name] = (out[name] * factor).astype(out[name].dtype)
    return out
```

```python
from contextlib import ExitStack

import numpy as np

import concourse.bass as bass
from concourse import mybir

F32 = mybir.dt.float32
F32R = mybir.dt.float32r
U32 = mybir.dt.uint32
ALU = mybir.AluOpType
ACT = mybir.ActivationFunctionType
AX = mybir.AxisListType

P = 128
D = 1024
CH = D // P
SEQ, NB, NL = 512, 8, 4
TOK = SEQ + NB * NL
TILES = [(t * P, P) for t in range(SEQ // P)] + [(SEQ, NB * NL)]
NT = len(TILES)
HALF = TOK // 2
AH, AD = 8, 64
PAIRS = AH // 2
BH, BD = 4, 128
PAST = 2048
CONV = 4
EPS = 1e-6
NEG = -1e30
WC = 256
OLD_TILES, NEW_TILES = 3, 4
KTILES = OLD_TILES + NEW_TILES
CACHED = KTILES * P
PH, PK, TOPK = 8, 128, 16
EXPERTS = PK * PK
LEVELS = 7
GT = 68
GBLOCKS = TOK // GT


def position_tables():
    half = AD // 2
    inv = np.float32(10000.0) ** (-np.arange(half, dtype=np.float32) / np.float32(half))
    pos = np.concatenate([np.arange(SEQ), np.tile(PAST + np.arange(NL), NB)]).astype(np.float32)
    ang = (pos[:, None] * inv[None, :].astype(np.float32)).astype(np.float32).astype(np.float64)
    cos, sin = np.cos(ang), np.sin(ang)
    out = np.zeros((2, NT * P, AD), np.float32)
    out[0, :TOK] = np.concatenate([cos, cos], 1)
    out[1, :TOK] = np.concatenate([-sin, sin], 1)
    return out.reshape(2, NT, P, AD).transpose(2, 0, 1, 3).copy()


def log_count(dist):
    count = np.zeros(dist.shape)
    for window, dil in ((128, 1), (512, 4), (2048, 16)):
        count += (dist >= 0) & (dist <= window) & (dist % dil == 0)
    return np.where(count > 0, np.log(np.maximum(count, 1)), NEG).astype(np.float32)


def prompt_log_counts():
    q, k = np.arange(P)[:, None], np.arange(P)[None, :]
    return np.concatenate([log_count(d * P + q - k) for d in (3, 2, 1, 0)], 1)


def sample_log_counts():
    p = np.arange(P)
    pos = [(j * 32 + p // 4) * 16 + p % 4 for j in range(OLD_TILES)]
    pos += [PAST - NEW_TILES * P + j * P + p for j in range(NEW_TILES)]
    pos = np.concatenate(pos)
    rows = PAST + np.tile(np.arange(NL), AH)
    cached = log_count(rows[:, None] - pos[None, :])
    own = log_count(np.arange(NL)[:, None] - np.arange(NL)[None, :])
    new = np.full((AH * NL, NB, NB * NL), NEG, np.float32)
    for b in range(NB):
        new[:, b, b * NL:(b + 1) * NL] = np.tile(own, (AH, 1))
    return np.concatenate([cached, new.reshape(AH * NL, -1)], 1)


def square_tables():
    i = np.arange(P)
    j, c = i[:, None], i[None, :]
    out = [j == c, np.ones((P, P)), j <= c, (j <= c) & (j // NL == c // NL), j // NL == c // NL,
           np.broadcast_to(c, (P, P))]
    for lv in range(LEVELS):
        s = 1 << lv
        out.append((j // (2 * s) == c // (2 * s)) & ((c // s) % 2 == 1) & ((j // s) % 2 == 0))
    return np.stack(out, 1).astype(np.float32)


IDENT, ONES, CUM_P, CUM_S, BLK_S, ASC, LEVEL0 = range(7)
NSQ = LEVEL0 + LEVELS


class Chain:

    def __init__(self, eng, sem):
        self.eng, self.sem, self.n = eng, sem, 0

    def mark(self, ins):
        ins.then_inc(self.sem, 1)
        self.n += 1

    def join(self):
        self.eng.wait_ge(self.sem, self.n)

    def link(self, ins):
        self.mark(ins)
        self.join()


def rows(n):
    w = TILES[n][1]
    return slice(P - w, P)


def token_columns(n):
    t0, w = TILES[n]
    return slice(t0 + w - P, t0 + w)


def bc(ap, axis, count):
    ap = ap.unsqueeze(axis)
    shape = list(ap.shape)
    shape[axis] = count
    return ap.broadcast_to(shape)


def hybrid_step(nc, x_p, x_s, kc, vc, conv_state, s0, nmix, win, wg8, qkw, convw, alog, dtb, dnw, wout, nffn,
                wpq, skt, eu, ev, pos_t, lnc_p, lnc_s, squares,
                y_p, y_s, k_p, v_p, conv_out, s_p, k_s, v_s, s_s, gates_dram):
    with ExitStack() as ctx:
        def sem(name):
            return ctx.enter_context(nc.semaphore(name))

        base = 16512
        top = [0]

        def at(name, offset, shape, dt=F32):
            size = int(np.prod(shape[1:])) * 4
            top[0] = max(top[0], offset + size)
            assert offset + size <= 212800, name
            return nc.alloc_sbuf_tensor_at(name, shape, dt, offset=base + offset)

        def region(offset):
            pos = [offset]

            def put(name, shape, dt=F32):
                t = at(name, pos[0], shape, dt)
                pos[0] += -(-int(np.prod(shape[1:])) * 4 // 32) * 32
                return t
            put.pos = pos
            return put

        put = region(0)
        sq = put("sq", [P, NSQ, P])
        nmix_b = put("nmix_b", [P, D])
        lncp = put("lncp", [P, 4 * P])
        lncs = put("lncs", [NB * NL, CACHED + NB * NB * NL])
        pos = put("pos", [P, 2, NT, AD])
        cw = put("cw", [P, NT, 2, AD])
        sw = put("sw", [P, NT, 2, AD])
        qkw_b = put("qkw_b", [P, 2, 2, AD])
        convw_t = put("convw_t", [P, 3 * BH, CONV])
        dnw_b = put("dnw_b", [P, BD])
        gconst = put("gconst", [P, 2, BH])
        g8 = put("g8", [P, NT, 2 * BH])
        gz = put("gz", [P, NT, BH])
        gl = put("gl", [P, NT, BH])
        gate_g = put("gate_g", [P, NT, BH])
        beta = put("beta", [P, NT, BH])
        nega = put("nega", [P, BH])
        stat = put("stat", [P, 8, NT])
        ropes = put("ropes", [P, NT, 16])
        wg8_raw = put("wg8_raw", [P, CH, 8])
        wg8_hi = put("wg8_hi", [P, CH, 8], F32R)
        wg8_lo = put("wg8_lo", [P, CH, 8], F32R)
        cst = put("cst", [P, 3 * BH, NB, 3])
        cso = put("cso", [P, 3 * BH, (NB + 1) * 3])
        smax = put("smax", [P, 2, 4])
        sstat = put("sstat", [NB * NL, 2, 8])
        R_X = put.pos[0]
        R_XN = R_X + 20480
        R_W = R_XN + 2 * CH * TOK * 4
        R_AQ = R_W + 40960
        R_AV = R_AQ + 12 * TOK * 4
        R_BZ = R_AV + NT * 512 * 4
        R_QK = R_BZ + NT * 512 * 4
        R_E = R_QK + 8 * TOK * 4

        ident, ones, asc = sq[:, IDENT, :], sq[:, ONES, :], sq[:, ASC, :]
        X = at("X", R_X, [P, NT, D])
        xs = at("xs", R_BZ, [P, 2, D])
        xn_hi = at("xn_hi", R_XN, [P, CH, TOK], F32R)
        xn_lo = at("xn_lo", R_XN + CH * TOK * 4, [P, CH, TOK], F32R)
        w_raw = at("w_raw", R_W, [P, CH, WC])
        w_hi = at("w_hi", R_W + 8192, [P, 2, CH, WC], F32R)
        w_lo = at("w_lo", R_W + 24576, [P, 2, CH, WC], F32R)
        qk = at("qk", R_AQ, [P, NT, 2 * AH * AD])
        co = at("co", R_AQ, [P, 3 * BH, TOK])
        av = at("av", R_AV, [P, NT, AH * AD])
        bz = at("bz", R_BZ, [P, NT, BH * BD])
        qkt = at("qkt", R_QK, [P, 2 * PAIRS, TOK])
        tmp1 = at("tmp1", R_E, [P, 16 * AD])
        tmp2 = at("tmp2", R_E + 4096, [P, 16 * AD])
        ext = at("ext", R_E, [P, 2, 3 + SEQ + NB * (3 + NL) + 1])
        cy = at("cy", R_E + 2 * 572 * 4 + 32, [P, 2, TOK])
        put = region(R_XN)
        l2s = put("l2s", [P, 2, TOK])
        l2r = put("l2r", [P, 2, TOK])
        cat = at("cat", R_X, [P, CH, TOK])
        sm = at("sm", R_E, [P, 2, 4 * P])
        pt = at("pt", R_E + 4096, [P, 2, 4, P])
        put = region(R_XN)

        def slots(name):
            return [put(f"{name}{s}", [P, BH, P]) for s in range(2)]
        eg, qd, lt, it, kd, kbg, vb, xt, xi, yv, ml, uu, wt = (
            slots(n) for n in ("eg", "qd", "lt", "it", "kd", "kbg", "vb", "xt", "xi", "yv", "ml", "uu", "wt"))
        vm = at("vm", R_XN + 2048, [P, NB, BD])
        vnt = put("vnt", [P, 3, BH, NB * NL])
        s_cur = put("s_cur", [P, BH, BD])
        gcol = put("gcol", [P, 2, 4, BH])
        ost = put("ost", [P, 2, 2, BH])
        ss0 = at("ss0", R_W + 40960 - 16384, [P, NB, BH, BD])
        assert put.pos[0] <= R_W + 40960 - 16384
        put = region(R_XN)
        ks = [put(f"ks{s}", [P, KTILES, AH * AD]) for s in range(2)]
        vs = [put(f"vs{s}", [P, KTILES, AH * AD]) for s in range(2)]
        kt = put("kt", [P, PAIRS, CACHED])
        assert put.pos[0] <= R_W + 40960
        sss = at("sss", R_E, [NB * NL, CACHED + NB * NL])
        pts = at("pts", R_E + 4096, [P, KTILES + 1, NB * NL])
        qbd = at("qbd", R_E + 4096 + 1024, [P, NB, PAIRS, NB * NL])

        cat_hi = at("cat_hi", R_AQ, [P, CH, TOK], F32R)
        cat_lo = at("cat_lo", R_AQ + CH * TOK * 4, [P, CH, TOK], F32R)
        hn_hi = at("hn_hi", R_AQ, [P, CH, TOK], F32R)
        hn_lo = at("hn_lo", R_AQ + CH * TOK * 4, [P, CH, TOK], F32R)
        R_B = R_AQ + 2 * CH * TOK * 4
        put = region(R_B)
        qt = put("qt", [P, 2 * PH, TOK])
        put = region(R_XN)
        hs = put("hs", [P, 2, D])
        cand = put("cand", [P, PH, TOPK, TOPK])
        eq = put("eq", [P, PH, TOPK, TOPK])
        tv = put("tv", [P, 2 * PH, TOPK])
        ti = put("ti", [P, 2 * PH, TOPK], U32)
        tif = put("tif", [P, 2 * PH, TOPK])
        bv = put("bv", [P, PH, TOPK])
        bi = put("bi", [P, PH, TOPK], U32)
        bhl = put("bhl", [P, 2, PH, TOPK], U32)
        bhlf = put("bhlf", [P, 2, PH, TOPK])
        picks = put("picks", [P, 3, PH * TOPK])
        gsum = put("gsum", [P, 2, PH])
        assert put.pos[0] <= R_W
        put = region(R_W)
        picks_t = put("picks_t", [P, 3, TOK])
        one1 = [put(f"one1_{s}", [P, 4, PK]) for s in range(2)]
        one2 = [put(f"one2_{s}", [P, 4, PK]) for s in range(2)]
        cols_s = put("cols_s", [P, 2, 3, GT])
        skt_s = put("skt_s", [P, 2, PK])
        sub_s = [put(f"sub_s{s}", [P, 2 * PH, PK]) for s in range(2)]
        assert put.pos[0] <= R_AQ
        gst = [at("gst0", R_XN, [P, PK, GT]), at("gst1", R_B, [P, PK, GT])]
        put = region(R_XN)
        u_raw = [put(f"u_raw{s}", [P, CH, P]) for s in range(2)]
        u_hi = [put(f"u_hi{s}", [P, CH, P], F32R) for s in range(2)]
        u_lo = [put(f"u_lo{s}", [P, CH, P], F32R) for s in range(2)]
        v_raw = [put(f"v_raw{s}", [P, D]) for s in range(2)]
        v_hi = [put(f"v_hi{s}", [P, D], F32R) for s in range(4)]
        v_lo = [put(f"v_lo{s}", [P, D], F32R) for s in range(4)]
        gin = [put(f"gin{s}", [P, GBLOCKS, 2, GT]) for s in range(2)]
        assert put.pos[0] <= R_AQ
        put = region(R_B)
        a_hi = [put(f"a_hi{s}", [P, TOK], F32R) for s in range(4)]
        a_lo = [put(f"a_lo{s}", [P, TOK], F32R) for s in range(4)]
        act_g = [put(f"act_g{s}", [P, TOK]) for s in range(2)]
        y_t = put("y_t", [P, CH, TOK])

        bank = [ctx.enter_context(nc.psum_tensor(f"bank{i}", [P, 512], F32)) for i in range(8)]

        def quad(b, w=P, n=P):
            return bank[b][0:n, 0:4 * w].rearrange("p (h c) -> p h c", h=4)

        block = ctx.enter_context(nc.Block())

        NW1 = 14
        order1 = [0, 1, 2, 3, 4, 5, 12, 13, 6, 7, 8, 9, 10, 11]

        x_in = [sem(f"x_in{t}") for t in range(NT)]
        consts_in, small_in = sem("consts_in"), sem("small_in")
        ssq_ready, rstd_ready, xs_ready, xs_turned = sem("ssq_ready"), sem("rstd_ready"), sem("xs_ready"), sem("xs_turned")
        var_ready = sem("var_ready")
        xn_hi_ready, xn_lo_ready = sem("xn_hi_ready"), sem("xn_lo_ready")
        w_in, w_hi_ready, w_lo_ready, w_used = sem("w_in"), sem("w_hi_ready"), sem("w_lo_ready"), sem("w_used")
        g8_split = sem("g8_split")
        proj_ready, proj_evac = sem("proj_ready"), sem("proj_evac")
        rope_var, rope_rs, rope_done = sem("rope_var"), sem("rope_rs"), sem("rope_done")
        qk_turned, qkt_ready = sem("qk_turned"), sem("qkt_ready")
        kv_out = sem("kv_out")
        ext_ready, ext_state, conv_done, cso_done, silu_done = (
            sem("ext_ready"), sem("ext_state"), sem("conv_done"), sem("cso_done"), sem("silu_done"))
        l2_sq, l2_sum, l2_inv, l2_rt, l2_done = sem("l2_sq"), sem("l2_sum"), sem("l2_inv"), sem("l2_rt"), sem("l2_done")
        gates_v, gates_e = sem("gates_v"), sem("gates_e")
        conv_out_sem = sem("conv_out_sem")
        dve_chain, act_chain, pool_chain = sem("dve_chain"), sem("act_chain"), sem("pool_chain")
        s_scores, s_masked, s_exp, s_norm, s_turned, s_pt, s_out, s_cat = (
            sem("s_scores"), sem("s_masked"), sem("s_exp"), sem("s_norm"), sem("s_turned"), sem("s_pt"),
            sem("s_out"), sem("s_cat"))
        extra = {}

        def S_(name):
            if name not in extra:
                extra[name] = sem(name)
            return extra[name]

        NCONST = 3

        UNITS = [(i, h) for i in range(SEQ // P) for h in range(AH)]

        def pe_attend(pe):
            pe.wait_ge(l2_inv, 2 * BH)

            def scores(u):
                i, h = UNITS[u]
                if u >= 4:
                    pe.wait_ge(s_masked, u - 3)
                r = slice(AD * (h % 2), AD * (h % 2) + AD)
                nc.tensor.matmul(bank[2 + u % 4][:, 0:(i + 1) * P], qkt[r, h // 2, i * P:(i + 1) * P],
                                 qkt[r, PAIRS + h // 2, 0:(i + 1) * P], start=True, stop=True).then_inc(s_scores, 1)

            def turn(u):
                i, h = UNITS[u]
                pe.wait_ge(s_norm, u + 1)
                if u >= 2:
                    pe.wait_ge(s_pt, u - 1)
                for j in range(i + 1):
                    last = nc.tensor.transpose(quad(u % 2)[:, j, :], sm[:, u % 2, j * P:(j + 1) * P], ident)
                last.then_inc(s_turned, 1)

            def values(u):
                i, h = UNITS[u]
                pe.wait_ge(s_pt, u + 1)
                if u >= 4:
                    pe.wait_ge(s_cat, u // 2 - 1)
                r = slice(AD * (h % 2), AD * (h % 2) + AD)
                for j in range(i + 1):
                    last = nc.tensor.matmul(bank[6 + (u // 2) % 2][r, 0:P], av[:, j, h * AD:(h + 1) * AD], pt[:, u % 2, j, :],
                                            start=j == 0, stop=j == i)
                last.then_inc(s_out, 1)

            for u in range(3):
                scores(u)
            for u in range(len(UNITS)):
                turn(u)
                if u:
                    values(u - 1)
                if u + 3 < len(UNITS):
                    scores(u + 3)
            values(len(UNITS) - 1)

        def dve_attend(dve, chain):
            dve.wait_ge(silu_done, 3 * BH)
            dve.wait_ge(cso_done, 3 * BH)

            def mask(u):
                i, h = UNITS[u]
                n = (i + 1) * P
                dve.wait_ge(s_scores, u + 1)
                if u >= 2:
                    dve.wait_ge(s_turned, u - 1)
                chain.link(nc.vector.tensor_tensor_reduce(
                    out=sm[:, u % 2, 0:n], in0=bank[2 + u % 4][:, 0:n], in1=lncp[:, 4 * P - n:4 * P], scale=1.0,
                    scalar=NEG, op0=ALU.add, op1=ALU.max, accum_out=smax[:, u % 2, 0:1]))
                nc.vector.tensor_scalar(smax[:, u % 2, 1:2], smax[:, u % 2, 0:1], -1.0, None, ALU.mult).then_inc(s_masked, 1)

            mask(0)
            for u in range(len(UNITS)):
                if u + 1 < len(UNITS):
                    mask(u + 1)
                n = (UNITS[u][0] + 1) * P
                dve.wait_ge(s_exp, u + 1)
                chain.link(nc.vector.reciprocal(smax[:, u % 2, 3:4], smax[:, u % 2, 2:3]))
                nc.vector.tensor_scalar(sm[:, u % 2, 0:n], sm[:, u % 2, 0:n], smax[:, u % 2, 3:4], None, ALU.mult).then_inc(s_norm, 1)

        def act_attend(act, chain):
            def turned(u):
                i, h = UNITS[u]
                act.wait_ge(s_turned, u + 1)
                if u >= 2:
                    act.wait_ge(s_out, u - 1)
                nc.scalar.activation(pt[:, u % 2, 0:i + 1, :], quad(u % 2)[:, 0:i + 1, :], ACT.Copy).then_inc(s_pt, 1)

            def pair(v):
                i = UNITS[2 * v][0]
                act.wait_ge(s_out, 2 * v + 2)
                nc.scalar.activation(cat[:, v % PAIRS, i * P:(i + 1) * P], bank[6 + v % 2][:, 0:P], ACT.Copy).then_inc(s_cat, 1)

            for u in range(len(UNITS)):
                n = (UNITS[u][0] + 1) * P
                act.wait_ge(s_masked, u + 1)
                nc.scalar.activation(sm[:, u % 2, 0:n], sm[:, u % 2, 0:n], ACT.Exp, bias=smax[:, u % 2, 1:2],
                                     accum_out=smax[:, u % 2, 2:3]).then_inc(s_exp, 1)
                if u:
                    turned(u - 1)
                if u >= 3 and u % 2:
                    pair(u // 2 - 1)
            turned(len(UNITS) - 1)
            pair(len(UNITS) // 2 - 1)

        GROUPS = [(0, 1), (2, 3), (4,)]
        names = ("gg rows kk tok eg gd dt dec sc front x0 x0t xi ml y yc xy xu uw uwc ws vn os s o ovar ort og ot cat "
                 "s_pe s_act s_dve vm st su")
        dl = {n: S_("delta_" + n) for n in names.split()}

        def cum(n):
            return sq[:, CUM_P if n < NT - 1 else CUM_S, :]

        def total(n):
            return sq[:, ONES if n < NT - 1 else BLK_S, :]

        def levels(n):
            return LEVELS if n < NT - 1 else 2

        def level_steps(group):
            return [(lv, n) for lv in range(1, levels(group[0])) for n in group]

        step_no = {}
        for g_ in GROUPS:
            for st_ in level_steps(g_):
                step_no[st_] = len(step_no)

        def sub(t, w, cols=None):
            return t[0:w, :, 0:(w if cols is None else cols)]

        def pe_delta(pe):
            pe.wait_ge(s_cat, len(UNITS) // 2)
            pe.wait_ge(gates_v, 3)
            pe.wait_ge(l2_done, 2 * BH)
            for group in GROUPS:
                for n in group:
                    (t0, w), s = TILES[n], n % 2
                    cols = slice(t0, t0 + w)
                    if n == group[0] and n:
                        pe.wait_ge(dl["cat"], n)
                        pe.wait_ge(dl["s"], n)
                    elif n:
                        pe.wait_ge(dl["front"], n)
                        pe.wait_ge(dl["eg"], n)
                    pe.wait_ge(dl["gg"], n + 1)
                    nc.tensor.matmul(bank[6][0:w, 0:4], cum(n)[0:w, 0:w], gate_g[0:w, n, :], start=True, stop=True)
                    nc.tensor.matmul(bank[6][0:w, 4:8], total(n)[0:w, 0:w], gate_g[0:w, n, :], start=True, stop=True)
                    nc.tensor.matmul(quad(0, w), ones[0:w, :], sub(lt[s], w), start=True, stop=True)
                    nc.tensor.matmul(quad(1, w), ones[0:w, :], sub(it[s], w), start=True, stop=True).then_inc(dl["rows"], 1)
                    for h in range(BH):
                        nc.tensor.matmul(quad(2, w, w)[:, h, :], co[:, BH + h, cols], co[:, BH + h, cols], start=True, stop=True)
                        last = nc.tensor.matmul(quad(3, w, w)[:, h, :], co[:, BH + h, cols], co[:, h, cols], start=True, stop=True)
                    last.then_inc(dl["kk"], 1)
                    for h in range(BH):
                        for b, c in ((4, BH + h), (5, 2 * BH + h)):
                            if w == P:
                                last = nc.tensor.transpose(quad(b)[:, h, :], co[:, c, cols], ident)
                            else:
                                last = nc.tensor.matmul(quad(b)[0:w, h, :], co[:, c, cols], ident, start=True, stop=True)
                    last.then_inc(dl["tok"], 1)
                for n in group:
                    w, s = TILES[n][1], n % 2
                    pe.wait_ge(dl["x0"], n + 1)
                    if n:
                        pe.wait_ge(dl["xi"], n)
                    for h in range(BH):
                        if w == P:
                            last = nc.tensor.transpose(quad(7)[:, h, :], xt[s][:, h, :], ident)
                        else:
                            last = nc.tensor.matmul(quad(7, w, w)[:, h, :], xt[s][0:w, h, 0:w], ident[0:w, 0:w], start=True, stop=True)
                    last.then_inc(dl["x0t"], 1)
                pe.wait_ge(dl["front"], group[-1] + 1)
                for lv, n in level_steps(group):
                    w, s, q = TILES[n][1], n % 2, step_no[lv, n]
                    pe.wait_ge(dl["ml"], q + 1)
                    if lv == 1:
                        pe.wait_ge(dl["xi"], n + 1)
                    else:
                        pe.wait_ge(dl["xu"], step_no[lv - 1, n] + 1)
                    for h in range(BH):
                        last = nc.tensor.matmul(quad(s, w, w)[:, h, :], ml[s][0:w, h, 0:w], xi[s][0:w, h, 0:w], start=True, stop=True)
                    last.then_inc(dl["y"], 1)
                    if n != group[-1]:
                        continue
                    for m in group:
                        s, q = m % 2, step_no[lv, m]
                        pe.wait_ge(dl["yc"], q + 1)
                        for h in range(BH):
                            if lv < levels(m) - 1:
                                nc.tensor.matmul(quad(2 + s, w, w)[:, h, :], xt[s][0:w, h, 0:w], yv[s][0:w, h, 0:w], start=True, stop=True)
                            last = nc.tensor.matmul(quad(4 + s, w, w)[:, h, :], yv[s][0:w, h, 0:w], xt[s][0:w, h, 0:w], start=True, stop=True)
                        last.then_inc(dl["xy"], 1)
                for n in group:
                    w, s = TILES[n][1], n % 2
                    pe.wait_ge(dl["xu"], step_no[levels(n) - 1, n] + 1)
                    if n:
                        pe.wait_ge(dl["uwc"], n)
                    for h in range(BH):
                        if n < NT - 1:
                            nc.tensor.matmul(quad(6)[:, h, :], xt[s][:, h, :], vb[s][:, h, :], start=True, stop=True)
                        else:
                            nc.tensor.matmul(quad(6, w)[:, h, :], vb[s][0:w, h, :], xt[s][0:w, h, 0:w], start=True, stop=True)
                        last = nc.tensor.matmul(quad(7, w)[:, h, :], kbg[s][0:w, h, :], xt[s][0:w, h, 0:w], start=True, stop=True)
                    last.then_inc(dl["uw"], 1)
                if group[0] < NT - 1:
                    for n in group:
                        s = n % 2
                        pe.wait_ge(dl["uwc"], n + 1)
                        if n:
                            pe.wait_ge(dl["s"], n)
                            for h in range(BH):
                                last = nc.tensor.matmul(quad(0)[:, h, :], wt[s][:, h, :], s_cur[:, h, :], start=True, stop=True)
                            last.then_inc(dl["ws"], 1)
                            pe.wait_ge(dl["vn"], n)
                            pe.wait_ge(dl["o"], n)
                        vn = ml[s] if n else uu[s]
                        for h in range(BH):
                            if n:
                                nc.tensor.matmul(quad(1)[:, h, :], qd[s][:, h, :], s_cur[:, h, :], start=True, stop=False)
                            nc.tensor.matmul(quad(1)[:, h, :], it[s][:, h, :], vn[:, h, :], start=n == 0, stop=True)
                            last = nc.tensor.matmul(quad(2)[:, h, :], kd[s][:, h, :], vn[:, h, :], start=True, stop=True)
                        last.then_inc(dl["os"], 1)
                else:
                    pe_delta_sample(pe)
                for n in group:
                    w, s = TILES[n][1], n % 2
                    pe.wait_ge(dl["og"], n + 1)
                    if n:
                        pe.wait_ge(dl["cat"], n)
                    for h in range(BH):
                        last = nc.tensor.transpose(quad(3, w)[:, h, :], yv[s][0:w, h, :], ident[0:w, 0:w])
                    last.then_inc(dl["ot"], 1)

        def pe_delta_sample(pe):
            w, s = NB * NL, 0
            pe.wait_ge(dl["uwc"], NT)
            pe.wait_ge(S_("states_in"), 16)
            for h in range(BH):
                for b in range(NB):
                    c = slice(b * NL, (b + 1) * NL)
                    nc.tensor.matmul(quad(0, w)[:, h, c], ss0[:, b, h, :], wt[s][:, h, c], start=True, stop=True)
                    last = nc.tensor.matmul(quad(1, w)[:, h, c], ss0[:, b, h, :], qd[s][:, h, c], start=True, stop=True)
            last.then_inc(dl["s_pe"], 1)
            pe.wait_ge(dl["s_dve"], 1)
            for h in range(BH):
                last = nc.tensor.matmul(quad(2)[0:w, h, :], vnt[:, 0, h, :], ident, start=True, stop=True)
            last.then_inc(dl["s_pe"], 1)
            pe.wait_ge(dl["s_act"], 2)
            for h in range(BH):
                last = nc.tensor.matmul(quad(3, w)[:, h, :], ml[s][0:w, h, :], it[s][0:w, h, 0:w], start=True, stop=True)
            last.then_inc(dl["s_pe"], 1)
            pe.wait_ge(dl["s_dve"], 2)
            for h in range(BH):
                last = nc.tensor.matmul(quad(4)[0:w, h, :], vnt[:, 2, h, :], ident, start=True, stop=True)
            last.then_inc(dl["s_pe"], 1)
            for h in range(BH):
                pe.wait_ge(dl["vm"], h + 1)
                if h:
                    pe.wait_ge(dl["su"], h)
                for b2 in range(2):
                    last = nc.tensor.matmul(quad(6 + b2), kd[s][0:w, h, :], vm[0:w, 4 * b2:4 * b2 + 4, :], start=True, stop=True)
                last.then_inc(dl["st"], 1)

        def act_delta(act, chain):
            act.wait_ge(l2_done, 2 * BH)
            for group in GROUPS:
                for n in group:
                    w, s = TILES[n][1], n % 2
                    act.wait_ge(dl["rows"], n + 1)
                    nc.scalar.activation(eg[s][:, :, 0:w], quad(0, w), ACT.Exp).then_inc(dl["eg"], 1)
                    act.wait_ge(dl["gd"], n + 1)
                    nc.scalar.activation(gcol[0:w, s, 1:3, :], gcol[0:w, s, 1:3, :], ACT.Exp).then_inc(dl["sc"], 1)
                    act.wait_ge(dl["dt"], n + 1)
                    nc.scalar.activation(sub(lt[s], w), sub(lt[s], w), ACT.Exp).then_inc(dl["dec"], 1)
                for n in group:
                    w, s = TILES[n][1], n % 2
                    act.wait_ge(dl["x0t"], n + 1)
                    nc.scalar.activation(sub(xi[s], w), quad(7, w, w), ACT.Copy).then_inc(dl["xi"], 1)
                for lv, n in level_steps(group):
                    w, s, q = TILES[n][1], n % 2, step_no[lv, n]
                    act.wait_ge(dl["y"], q + 1)
                    nc.scalar.activation(sub(yv[s], w), quad(s, w, w), ACT.Copy).then_inc(dl["yc"], 1)
                for n in group:
                    w, s = TILES[n][1], n % 2
                    act.wait_ge(dl["uw"], n + 1)
                    if n < NT - 1:
                        chain.mark(nc.scalar.activation(uu[s][:], quad(6), ACT.Copy))
                    else:
                        chain.mark(nc.scalar.activation(uu[s][:, :, 0:w], quad(6, w), ACT.Copy))
                    chain.link(nc.scalar.activation(wt[s][:, :, 0:w], quad(7, w), ACT.Copy))
                    act.sem_inc(dl["uwc"], 1)
                if group[0] < NT - 1:
                    for n in group:
                        act.wait_ge(dl["os"], n + 1)
                        nc.scalar.activation(yv[n % 2][:], quad(1), ACT.Copy).then_inc(dl["o"], 1)
                else:
                    w, s = NB * NL, 0
                    act.wait_ge(dl["s_pe"], 1)
                    nc.scalar.activation(vnt[:, 1], quad(1, w), ACT.Copy).then_inc(dl["s_act"], 1)
                    act.wait_ge(dl["s_pe"], 2)
                    nc.scalar.activation(ml[s][0:w], quad(2)[0:w], ACT.Copy).then_inc(dl["s_act"], 1)
                    act.wait_ge(dl["s_pe"], 4)
                    nc.scalar.activation(yv[s][0:w], quad(4)[0:w], ACT.Copy).then_inc(dl["o"], 1)
                for n in group:
                    act.wait_ge(dl["ovar"], n + 1)
                    nc.scalar.activation(ost[:, n % 2, 1, :], ost[:, n % 2, 1, :], ACT.Sqrt).then_inc(dl["ort"], 1)
                for n in group:
                    t0, w = TILES[n]
                    act.wait_ge(dl["ot"], n + 1)
                    nc.scalar.activation(cat[:, PAIRS:, t0:t0 + w], quad(3, w), ACT.Copy).then_inc(dl["cat"], 1)

        def dve_delta(dve, chain):
            tt = nc.vector.tensor_tensor
            chain.link(nc.vector.memset(ost[:], 1.0))
            for group in GROUPS:
                for n in group:
                    w, s = TILES[n][1], n % 2
                    chain.mark(tt(out=sub(lt[s], w), in0=bc(cum(n)[0:w, 0:w], 1, BH), in1=bc(gate_g[0:w, n, :], 2, w), op=ALU.mult))
                    chain.link(tt(out=sub(it[s], w), in0=bc(ident[0:w, 0:w], 1, BH), in1=bc(beta[0:w, n, :], 2, w), op=ALU.mult))
                    dve.sem_inc(dl["gg"], 1)
                for n in group:
                    (t0, w), s = TILES[n], n % 2
                    dve.wait_ge(dl["rows"], n + 1)
                    chain.link(nc.vector.tensor_copy(gcol[0:w, s, 0, :], bank[6][0:w, 0:4]))
                    chain.mark(nc.vector.tensor_copy(gcol[0:w, s, 2, :], bank[6][0:w, 0:4]))
                    chain.link(tt(out=gcol[0:w, s, 1, :], in0=bank[6][0:w, 4:8], in1=gcol[0:w, s, 0, :], op=ALU.subtract))
                    dve.sem_inc(dl["gd"], 1)
                    dve.wait_ge(dl["eg"], n + 1)
                    for h in range(BH):
                        chain.mark(nc.vector.tensor_scalar(lt[s][0:w, h, 0:w], quad(0, w, w)[:, h, :], gcol[0:w, s, 0, h:h + 1],
                                                           0.0, ALU.subtract, ALU.min))
                    chain.join()
                    dve.sem_inc(dl["dt"], 1)
                    chain.mark(tt(out=qd[s][:, :, 0:w], in0=co[:, 0:BH, t0:t0 + w], in1=eg[s][:, :, 0:w], op=ALU.mult))
                    dve.wait_ge(dl["sc"], n + 1)
                    chain.link(tt(out=gcol[0:w, s, 3, :], in0=beta[0:w, n, :], in1=gcol[0:w, s, 2, :], op=ALU.mult))
                    dve.wait_ge(dl["dec"], n + 1)
                    dve.wait_ge(dl["kk"], n + 1)
                    chain.link(tt(out=sub(it[s], w), in0=quad(3, w, w), in1=sub(lt[s], w), op=ALU.mult))
                    chain.mark(tt(out=sub(it[s], w), in0=sub(it[s], w), in1=bc(cum(n)[0:w, 0:w], 1, BH), op=ALU.mult))
                    chain.link(tt(out=sub(lt[s], w), in0=quad(2, w, w), in1=sub(lt[s], w), op=ALU.mult))
                    chain.link(tt(out=sub(lt[s], w), in0=sub(lt[s], w), in1=quad(1, w, w), op=ALU.mult))
                    chain.link(tt(out=sub(ml[s], w), in0=sub(lt[s], w), in1=bc(sq[0:w, LEVEL0, 0:w], 1, BH), op=ALU.mult))
                    chain.link(tt(out=sub(xt[s], w), in0=bc(ident[0:w, 0:w], 1, BH), in1=sub(ml[s], w), op=ALU.subtract))
                    dve.sem_inc(dl["x0"], 1)
                    dve.wait_ge(dl["tok"], n + 1)
                    chain.mark(tt(out=kd[s][0:w], in0=quad(4)[0:w], in1=bc(gcol[0:w, s, 1, :], 2, BD), op=ALU.mult))
                    chain.mark(tt(out=kbg[s][0:w], in0=quad(4)[0:w], in1=bc(gcol[0:w, s, 3, :], 2, BD), op=ALU.mult))
                    chain.link(tt(out=vb[s][0:w], in0=quad(5)[0:w], in1=bc(beta[0:w, n, :], 2, BD), op=ALU.mult))
                    dve.sem_inc(dl["front"], 1)
                for lv, n in level_steps(group):
                    w, s, q = TILES[n][1], n % 2, step_no[lv, n]
                    dve.wait_ge(dl["xy"], q + 1)
                    if lv < levels(n) - 1:
                        chain.mark(tt(out=sub(xi[s], w), in0=sub(xi[s], w), in1=quad(2 + s, w, w), op=ALU.subtract))
                    chain.link(tt(out=sub(xt[s], w), in0=sub(xt[s], w), in1=quad(4 + s, w, w), op=ALU.subtract))
                    dve.sem_inc(dl["xu"], 1)
                if group[0] < NT - 1:
                    for n in group:
                        s = n % 2
                        if n:
                            dve.wait_ge(dl["ws"], n)
                            tt(out=ml[s][:], in0=uu[s][:], in1=quad(0), op=ALU.subtract).then_inc(dl["vn"], 1)
                        dve.wait_ge(dl["os"], n + 1)
                        if n:
                            for h in range(BH):
                                chain.mark(nc.vector.scalar_tensor_tensor(out=s_cur[:, h, :], in0=s_cur[:, h, :], scalar=eg[s][:, h, P - 1:P],
                                                                          in1=quad(2)[:, h, :], op0=ALU.mult, op1=ALU.add))
                            chain.join()
                        else:
                            chain.link(nc.vector.tensor_copy(s_cur[:], quad(2)))
                        dve.sem_inc(dl["s"], 1)
                else:
                    w, s = NB * NL, 0
                    dve.wait_ge(dl["s_pe"], 1)
                    tt(out=vnt[:, 0], in0=uu[s][:, :, 0:w], in1=quad(0, w), op=ALU.subtract).then_inc(dl["s_dve"], 1)
                    dve.wait_ge(dl["s_act"], 1)
                    dve.wait_ge(dl["s_pe"], 3)
                    tt(out=vnt[:, 2], in0=vnt[:, 1], in1=quad(3, w), op=ALU.add).then_inc(dl["s_dve"], 1)
                    for h in range(BH):
                        if h:
                            dve.wait_ge(dl["st"], h)
                        tt(out=vm[0:w], in0=bc(ml[s][0:w, h, :], 1, NB), in1=bc(sq[0:w, BLK_S, 0:w:NL], 2, BD), op=ALU.mult).then_inc(dl["vm"], 1)
                        chain.link(tt(out=ss0[:, :, h, :], in0=ss0[:, :, h, :], in1=bc(eg[s][:, h, NL - 1:w:NL], 2, BD), op=ALU.mult))
                        dve.wait_ge(dl["st"], h + 1)
                        for b2 in range(2):
                            chain.mark(tt(out=ss0[:, 4 * b2:4 * b2 + 4, h, :], in0=ss0[:, 4 * b2:4 * b2 + 4, h, :], in1=quad(6 + b2), op=ALU.add))
                        chain.join()
                        dve.sem_inc(dl["su"], 1)
                for n in group:
                    w, s = TILES[n][1], n % 2
                    dve.wait_ge(dl["o"], n + 1)
                    chain.link(tt(out=xi[s][0:w], in0=yv[s][0:w], in1=yv[s][0:w], op=ALU.mult))
                    chain.link(nc.vector.tensor_reduce(ost[0:w, s, 0, :], xi[s][0:w], axis=AX.X, op=ALU.add))
                    chain.link(nc.vector.tensor_scalar(ost[0:w, s, 1, :], ost[0:w, s, 0, :], 1.0 / BD, EPS, ALU.mult, ALU.add))
                    nc.vector.reciprocal(ost[0:w, s, 1, :], ost[0:w, s, 1, :]).then_inc(dl["ovar"], 1)
                for n in group:
                    w, s = TILES[n][1], n % 2
                    dve.wait_ge(dl["ort"], n + 1)
                    chain.link(tt(out=yv[s][0:w], in0=yv[s][0:w], in1=bc(ost[0:w, s, 1, :], 2, BD), op=ALU.mult))
                    tt(out=yv[s][0:w], in0=yv[s][0:w], in1=bz[0:w, n, :].rearrange("p (h e) -> p h e", h=BH), op=ALU.mult).then_inc(dl["og"], 1)

        def pool_mix(pool, chain):
            for group in GROUPS:
                for lv, n in level_steps(group):
                    w, s = TILES[n][1], n % 2
                    if lv == 1:
                        pool.wait_ge(dl["x0"], n + 1)
                    else:
                        pool.wait_ge(dl["y"], step_no[lv - 1, n] + 1)
                    nc.gpsimd.tensor_tensor(out=sub(ml[s], w), in0=sub(lt[s], w), in1=bc(sq[0:w, LEVEL0 + lv, 0:w], 1, BH),
                                            op=ALU.mult).then_inc(dl["ml"], 1)
            pool_sample(pool, chain)

        def sp_delta(sp):
            sp.wait_ge(l2_done, 2 * BH)
            sp.dma_start(ss0[:], s0.rearrange("b h k v -> k (b h) v")).then_inc(S_("states_in"), 16)
            sp.wait_ge(dl["s"], NT - 1)
            sp.dma_start(s_p.rearrange("h k v -> k h v"), s_cur[:]).then_inc(S_("states_out"), 16)
            sp.wait_ge(dl["su"], BH)
            sp.dma_start(s_s.rearrange("b h k v -> k (b h) v"), ss0[:]).then_inc(S_("states_out"), 16)

        QROWS = NB * NL
        kv_in = [S_(f"cached_in{s}") for s in range(2)]
        sa = {n: S_("sample_" + n) for n in "q kt0 kt1 kta ktv scores masked exp norm turned pt out os used".split()}

        def sp_sample(sp):
            sp.wait_ge(S_("states_out"), 32)
            sp.wait_ge(dl["cat"], NT)
            for b in range(NB):
                s = b % 2
                if b >= 2:
                    sp.wait_ge(sa["used"], b - 1)
                for dst, cache in ((ks[s], kc), (vs[s], vc)):
                    groups = cache[b].rearrange("(j g s) c -> j g s c", g=32, s=16)
                    for j in range(OLD_TILES):
                        sp.dma_start(dst[:, j, :], groups[j, :, 0:4, :]).then_inc(kv_in[s], 16)
                    sp.dma_start(dst[:, OLD_TILES:, :],
                                 cache[b, PAST - NEW_TILES * P:PAST, :].rearrange("(j p) c -> p j c", p=P)).then_inc(kv_in[s], 16)

        def pe_sample(pe):
            pe.wait_ge(dl["cat"], NT)
            pe.wait_ge(dl["su"], BH)

            def turn_keys(b):
                s = b % 2
                pe.wait_ge(kv_in[s], 16 * 8 * (b // 2 + 1))
                for p in range(PAIRS):
                    q = b * PAIRS + p
                    if q:
                        pe.wait_ge(sa["kta"], q)
                    for j in range(4):
                        last = nc.tensor.transpose(quad(0)[:, j, :], ks[s][:, j, p * P:(p + 1) * P], ident)
                    last.then_inc(sa["kt0"], 1)
                    if q:
                        pe.wait_ge(sa["ktv"], q)
                    for j in range(4, KTILES):
                        last = nc.tensor.transpose(quad(1)[:, j - 4, :], ks[s][:, j, p * P:(p + 1) * P], ident)
                    last.then_inc(sa["kt1"], 1)

            turn_keys(0)
            pe.wait_ge(sa["q"], 1)
            for b in range(NB):
                s = b % 2
                pe.wait_ge(sa["kta"], PAIRS * (b + 1))
                pe.wait_ge(sa["ktv"], PAIRS * (b + 1))
                if b:
                    pe.wait_ge(sa["masked"], b)
                for p in range(PAIRS):
                    nc.tensor.matmul(bank[2][0:QROWS, :], qbd[:, b, p, :], kt[:, p, 0:512], start=p == 0, stop=p == PAIRS - 1)
                for p in range(PAIRS):
                    nc.tensor.matmul(bank[3][0:QROWS, 0:CACHED - 512], qbd[:, b, p, :], kt[:, p, 512:CACHED], start=p == 0, stop=p == PAIRS - 1)
                for p in range(PAIRS):
                    last = nc.tensor.matmul(bank[3][0:QROWS, CACHED - 512:CACHED - 512 + QROWS], qbd[:, b, p, :], qkt[:, PAIRS + p, SEQ:TOK],
                                            start=p == 0, stop=p == PAIRS - 1)
                last.then_inc(sa["scores"], 1)
                if b + 1 < NB:
                    turn_keys(b + 1)
                pe.wait_ge(sa["norm"], b + 1)
                if b:
                    pe.wait_ge(sa["pt"], b)
                pts_bank = bank[4][:, 0:(KTILES + 1) * QROWS].rearrange("p (j q) -> p j q", q=QROWS)
                for j in range(KTILES):
                    nc.tensor.transpose(pts_bank[:, j, :], sss[:, j * P:(j + 1) * P], ident[0:QROWS, 0:QROWS])
                nc.tensor.matmul(pts_bank[0:QROWS, KTILES, :], sss[:, CACHED:CACHED + QROWS], ident[0:QROWS, 0:QROWS],
                                 start=True, stop=True).then_inc(sa["turned"], 1)
                pe.wait_ge(sa["pt"], b + 1)
                if b:
                    pe.wait_ge(sa["os"], b)
                for p in range(PAIRS):
                    out = bank[5][:, 8 * p:8 * p + 8]
                    for j in range(KTILES):
                        nc.tensor.matmul(out, vs[s][:, j, p * P:(p + 1) * P], pts[:, j, 8 * p:8 * p + 8], start=j == 0, stop=False)
                    last = nc.tensor.matmul(out, av[0:QROWS, NT - 1, p * P:(p + 1) * P], pts[0:QROWS, KTILES, 8 * p:8 * p + 8],
                                            start=False, stop=True)
                last.then_inc(sa["out"], 1)
                pe.wait_ge(sa["out"], b + 1)
                pe.sem_inc(sa["used"], 1)

        def dve_sample(dve, chain):
            chain.link(nc.vector.memset(qbd[:], 0.0))
            for h in range(AH):
                r = slice(AD * (h % 2), AD * (h % 2) + AD)
                chain.mark(nc.vector.tensor_copy(qbd[r, :, h // 2, h * NL:(h + 1) * NL],
                                                 qkt[r, h // 2, SEQ:TOK].rearrange("p (b l) -> p b l", b=NB)))
            chain.join()
            dve.sem_inc(sa["q"], 1)

            def keys(b):
                if b:
                    dve.wait_ge(sa["scores"], b)
                for p in range(PAIRS):
                    dve.wait_ge(sa["kt1"], b * PAIRS + p + 1)
                    nc.vector.tensor_copy(kt[:, p, 512:CACHED], bank[1][:, 0:CACHED - 512]).then_inc(sa["ktv"], 1)

            keys(0)
            for b in range(NB):
                s = b % 2
                dve.wait_ge(sa["scores"], b + 1)
                if b:
                    dve.wait_ge(sa["turned"], b)
                m = 512
                parts = ((0, bank[2][0:QROWS, :], lncs[:, 0:m]),
                         (m, bank[3][0:QROWS, 0:CACHED - m], lncs[:, m:CACHED]),
                         (CACHED, bank[3][0:QROWS, CACHED - m:CACHED - m + QROWS], lncs[:, CACHED + b * QROWS:CACHED + (b + 1) * QROWS]))
                for x, (c0, src, lnc) in enumerate(parts):
                    chain.mark(nc.vector.tensor_tensor_reduce(
                        out=sss[:, c0:c0 + src.shape[1]], in0=src, in1=lnc, scale=1.0, scalar=NEG, op0=ALU.add, op1=ALU.max,
                        accum_out=sstat[:, s, x:x + 1]))
                chain.join()
                nc.vector.tensor_reduce(sstat[:, s, 3:4], sstat[:, s, 0:3], axis=AX.X, op=ALU.max, negate=True).then_inc(sa["masked"], 1)
                if b + 1 < NB:
                    keys(b + 1)
                dve.wait_ge(sa["exp"], b + 1)
                chain.link(nc.vector.reciprocal(sstat[:, s, 5:6], sstat[:, s, 4:5]))
                nc.vector.tensor_scalar(sss[:], sss[:], sstat[:, s, 5:6], None, ALU.mult).then_inc(sa["norm"], 1)

        def act_sample(act, chain):
            def keys(b):
                if b:
                    act.wait_ge(sa["scores"], b)
                for p in range(PAIRS):
                    act.wait_ge(sa["kt0"], b * PAIRS + p + 1)
                    nc.scalar.activation(kt[:, p, 0:512], bank[0][:], ACT.Copy).then_inc(sa["kta"], 1)

            keys(0)
            for b in range(NB):
                s = b % 2
                act.wait_ge(sa["masked"], b + 1)
                nc.scalar.activation(sss[:], sss[:], ACT.Exp, bias=sstat[:, s, 3:4], accum_out=sstat[:, s, 4:5]).then_inc(sa["exp"], 1)
                if b + 1 < NB:
                    keys(b + 1)
                act.wait_ge(sa["turned"], b + 1)
                if b:
                    act.wait_ge(sa["out"], b)
                pts_bank = bank[4][:, 0:(KTILES + 1) * QROWS].rearrange("p (j q) -> p j q", q=QROWS)
                chain.mark(nc.scalar.activation(pts[:, 0:KTILES, :], pts_bank[:, 0:KTILES, :], ACT.Copy))
                chain.link(nc.scalar.activation(pts[0:QROWS, KTILES, :], pts_bank[0:QROWS, KTILES, :], ACT.Copy))
                act.sem_inc(sa["pt"], 1)
                act.wait_ge(sa["out"], b + 1)
                c = slice(SEQ + b * NL, SEQ + (b + 1) * NL)
                o4 = bank[5][:, 0:8 * PAIRS].rearrange("p (i q) -> p i q", q=8)
                chain.mark(nc.scalar.activation(cat[0:AD, 0:PAIRS, c], o4[0:AD, :, 0:NL], ACT.Copy))
                chain.link(nc.scalar.activation(cat[AD:P, 0:PAIRS, c], o4[AD:P, :, NL:2 * NL], ACT.Copy))
                act.sem_inc(sa["os"], 1)

        def pool_sample(pool, chain):
            pool_ffn(pool, chain)

        NW_OUT, NW_PQ = 4, 8
        NW2 = NW1 + NW_OUT
        NW3 = NW2 + NW_PQ
        ff = {n: S_("ffn_" + n) for n in (
            "cat_hi cat_lo x_in norm_in h_used ssq var rstd hs turned hi lo pq pq_evac sub sub_evac sub_free "
            "top_exp top_expd picks picks_turned picks_t cols ones1 gate_mm gate_bank staged").split()}
        gate_out = [S_("gate_out0"), S_("gate_out1")]
        QUADS = GT // 4

        def sp_ffn(sp):
            sp.wait_ge(sa["used"], NB)
            for k in range(NW1, NW3):
                sp.wait_ge(w_hi_ready, k)
                sp.wait_ge(w_lo_ready, k)
                src = wout[k - NW1] if k < NW2 else wpq[k - NW2]
                sp.dma_start(w_raw[:], src).then_inc(w_in, 16)
                if k == NW1:
                    sp.wait_ge(ff["cat_hi"], 2)
                    sp.wait_ge(ff["cat_lo"], 2)
                    for t in range(NT):
                        x = x_p[t * P:(t + 1) * P, :] if t < NT - 1 else x_s
                        sp.dma_start(X[0:TILES[t][1], t, :], x).then_inc(ff["x_in"], 16)
                    sp.dma_start(nmix_b[:], nffn.partition_broadcast(P)).then_inc(ff["norm_in"], 16)
            sp.wait_ge(w_used, NW3)
            sp.dma_start(skt_s[:], skt).then_inc(ff["norm_in"], 16)
            with sp.Fori(0, GBLOCKS // 2) as i:
                for s in range(2):
                    sp.wait_ge(ff["staged"], 2 * i + s + 1)
                    sp.dma_start(gates_dram[bass.ds(2 * i + s, 1)].rearrange("o p a t -> p (o a t)"), gst[s][:]).then_inc(gate_out[s], 16)
            for s in range(2):
                sp.wait_ge(gate_out[s], 16 * (GBLOCKS // 2) + 16)
            sp_dense(sp)

        def pe_ffn(pe, product):
            pe.wait_ge(ff["cat_lo"], 2)
            pe.wait_ge(sa["os"], NB)
            uses = 0
            for k in range(NW1, NW2):
                pe.wait_ge(w_lo_ready, k + 1)
                for t in range(NT):
                    if uses >= 4:
                        pe.wait_ge(ff["h_used"], uses - 3)
                    tok = token_columns(t)
                    product(bank[2 + uses % 4][:, 0:WC],
                            [(cat_hi[:, c, tok], cat_lo[:, c, tok], w_hi[:, k % 2, c, :], w_lo[:, k % 2, c, :])
                             for c in range(CH)]).then_inc(proj_ready, 1)
                    uses += 1
                pe.wait_ge(proj_ready, READY1 + uses)
                pe.sem_inc(w_used, 1)
            for m in range(2 * NT):
                t0, w = TILES[m // 2]
                pe.wait_ge(ff["hs"], m // 2 + 1)
                if m >= 2:
                    pe.wait_ge(ff["lo"], m - 1)
                for j in range(4):
                    c = 4 * (m % 2) + j
                    last = nc.tensor.transpose(quad(m % 2, w)[:, j, :], hs[0:w, (m // 2) % 2, c * P:(c + 1) * P], ident[0:w, 0:w])
                last.then_inc(ff["turned"], 1)
            pe.wait_ge(ff["lo"], 2 * NT)
            pe.wait_ge(ff["h_used"], NW_OUT * NT)
            uses = 0
            for c in range(2 * PH):
                k = NW2 + c // 2
                pe.wait_ge(w_lo_ready, k + 1)
                wcols = slice((c % 2) * P, (c % 2) * P + P)
                for h in range(2):
                    if uses >= 4:
                        pe.wait_ge(ff["pq_evac"], uses - 3)
                    cols = slice(h * HALF, (h + 1) * HALF)
                    product(bank[2 + uses % 4][:, 0:HALF],
                            [(w_hi[:, k % 2, i, wcols], w_lo[:, k % 2, i, wcols], hn_hi[:, i, cols], hn_lo[:, i, cols])
                             for i in range(CH)]).then_inc(ff["pq"], 1)
                    uses += 1
                if c % 2:
                    pe.wait_ge(ff["pq"], uses)
                    pe.sem_inc(w_used, 1)
            pe.wait_ge(ff["pq_evac"], uses)
            pe.wait_ge(ff["norm_in"], 32)

            def half_scores(t):
                t0, w = TILES[t]
                for g in range(4):
                    q = 4 * t + g
                    if q >= 2:
                        pe.wait_ge(ff["sub_evac"], q - 1)
                    for j in range(4):
                        c = 4 * g + j
                        last = nc.tensor.matmul(quad(g % 2)[0:w, j, :], qt[:, c, t0:t0 + w], skt_s[:, c % 2, :], start=True, stop=True)
                    last.then_inc(ff["sub"], 1)

            half_scores(0)
            half_scores(1)
            for t, (t0, w) in enumerate(TILES):
                pe.wait_ge(ff["picks"], t + 1)
                if t:
                    pe.wait_ge(ff["picks_t"], t)
                for j in range(3):
                    last = nc.tensor.transpose(bank[6][:, j * P:j * P + w], picks[0:w, j, :], ident[0:w, 0:w])
                last.then_inc(ff["picks_turned"], 1)
                if t + 2 < NT:
                    half_scores(t + 2)
            with pe.Fori(0, GBLOCKS // 2) as i:
                for n in range(2 * QUADS):
                    pe.wait_ge(ff["ones1"], i * (2 * QUADS) + n + 1)
                    pe.wait_ge(ff["gate_bank"], i * (2 * QUADS) + n + 1)
                    for j in range(4):
                        last = nc.tensor.matmul(quad(2 + n % 2)[:, j, :], one2[n % 2][:, j, :], one1[n % 2][:, j, :], start=True, stop=True)
                    last.then_inc(ff["gate_mm"], 1)
            pe_dense(pe, product)

        def act_ffn(act, chain):
            act.wait_ge(sa["used"], NB)
            for h in range(2):
                nc.scalar.activation(cat_hi[:, 4 * h:4 * h + 4, :], cat[:, 4 * h:4 * h + 4, :], ACT.Copy).then_inc(ff["cat_hi"], 1)

            def split_hi(k):
                act.wait_ge(w_in, 16 * (k + 1))
                act.wait_ge(w_used, k - 1)
                nc.scalar.activation(w_hi[:, k % 2], w_raw[:], ACT.Copy).then_inc(w_hi_ready, 1)

            for k in range(NW1, NW2 + 2):
                split_hi(k)
            for t, (t0, w) in enumerate(TILES):
                act.wait_ge(ff["h_used"], (NW_OUT - 1) * NT + t + 1)
                if t:
                    act.wait_ge(ff["ssq"], t)
                nc.scalar.activation(tmp1[0:w, :], X[0:w, t, :], ACT.Square, accum_out=stat[0:w, 2, t:t + 1]).then_inc(ff["ssq"], 1)
            act.wait_ge(ff["var"], 1)
            nc.scalar.activation(stat[:, 3, :], stat[:, 3, :], ACT.Sqrt).then_inc(ff["rstd"], 1)
            for m in range(2 * NT):
                t0, w = TILES[m // 2]
                act.wait_ge(ff["turned"], m + 1)
                nc.scalar.activation(hn_hi[:, 4 * (m % 2):4 * (m % 2) + 4, t0:t0 + w], quad(m % 2, w), ACT.Copy).then_inc(ff["hi"], 1)
            uses = 0
            for c in range(2 * PH):
                for h in range(2):
                    act.wait_ge(ff["pq"], uses + 1)
                    nc.scalar.activation(qt[:, c, h * HALF:(h + 1) * HALF], bank[2 + uses % 4][:, 0:HALF], ACT.Copy).then_inc(ff["pq_evac"], 1)
                    uses += 1
                if c % 2 and NW2 + c // 2 + 2 < NW3:
                    split_hi(NW2 + c // 2 + 2)

            def scores_out(t):
                w = TILES[t][1]
                if t >= 2:
                    act.wait_ge(ff["sub_free"], t - 1)
                for g in range(4):
                    act.wait_ge(ff["sub"], 4 * t + g + 1)
                    nc.scalar.activation(sub_s[t % 2][0:w, 4 * g:4 * g + 4, :], quad(g % 2)[0:w], ACT.Copy).then_inc(ff["sub_evac"], 1)
            scores_out(0)
            for t, (t0, w) in enumerate(TILES):
                if t + 1 < NT:
                    scores_out(t + 1)
                act.wait_ge(ff["top_exp"], t + 1)
                nc.scalar.activation(bv[0:w], bv[0:w], ACT.Exp).then_inc(ff["top_expd"], 1)
            act.sem_inc(ff["gate_bank"], 2)
            with act.Fori(0, GBLOCKS // 2) as i:
                for s in range(2):
                    act.wait_ge(gate_out[s], 16 * i + 16)
                    for n in range(QUADS):
                        q = s * QUADS + n
                        act.wait_ge(ff["gate_mm"], i * (2 * QUADS) + (q + 1 + 2))
                        nc.scalar.activation(gst[s][:, :, 4 * n:4 * n + 4], quad(2 + q % 2).rearrange("p t a -> p a t"), ACT.Copy)\
                            .then_inc(ff["gate_bank"], 1)
                    act.wait_ge(ff["gate_bank"], i * (2 * QUADS) + (2 + (s + 1) * QUADS))
                    act.sem_inc(ff["staged"], 1)
            act_dense(act, chain)

        def dve_ffn(dve, chain):
            tt, ts = nc.vector.tensor_tensor, nc.vector.tensor_scalar
            for h in range(2):
                dve.wait_ge(ff["cat_hi"], h + 1)
                tt(out=cat_lo[:, 4 * h:4 * h + 4, :], in0=cat[:, 4 * h:4 * h + 4, :], in1=cat_hi[:, 4 * h:4 * h + 4, :].bitcast(F32),
                   op=ALU.subtract).then_inc(ff["cat_lo"], 1)
            dve.wait_ge(ff["x_in"], 16 * NT)
            uses = 0
            for k in range(NW_OUT):
                for t, (t0, w) in enumerate(TILES):
                    dve.wait_ge(proj_ready, READY1 + uses + 1)
                    x = X[0:w, t, k * WC:(k + 1) * WC]
                    tt(out=x, in0=x, in1=bank[2 + uses % 4][rows(t), 0:WC], op=ALU.add).then_inc(ff["h_used"], 1)
                    uses += 1
            dve.wait_ge(ff["ssq"], NT)
            chain.link(ts(stat[:, 3, :], stat[:, 2, :], 1.0 / D, EPS, ALU.mult, ALU.add))
            nc.vector.reciprocal(stat[:, 3, :], stat[:, 3, :]).then_inc(ff["var"], 1)
            dve.wait_ge(ff["rstd"], 1)
            dve.wait_ge(ff["norm_in"], 16)

            def scale_tokens(t):
                w = TILES[t][1]
                if t >= 2:
                    dve.wait_ge(ff["turned"], 2 * (t - 1))
                nc.vector.scalar_tensor_tensor(out=hs[0:w, t % 2, :], in0=X[0:w, t, :], scalar=stat[0:w, 3, t:t + 1],
                                               in1=nmix_b[0:w, :], op0=ALU.mult, op1=ALU.mult).then_inc(ff["hs"], 1)
            scale_tokens(0)
            for m in range(2 * NT):
                t0, w = TILES[m // 2]
                if m % 2 == 0 and m // 2 + 1 < NT:
                    scale_tokens(m // 2 + 1)
                hi = hn_hi[:, 4 * (m % 2):4 * (m % 2) + 4, t0:t0 + w].bitcast(F32)
                dve.wait_ge(ff["hi"], m + 1)
                tt(out=hn_lo[:, 4 * (m % 2):4 * (m % 2) + 4, t0:t0 + w], in0=quad(m % 2, w), in1=hi, op=ALU.subtract).then_inc(ff["lo"], 1)

            def top16(w, vals, idx, src, n):
                for j in range(n):
                    chain.mark(nc.vector.max(vals(j)[:, 0:8], src(j)))
                chain.join()
                for j in range(n):
                    chain.mark(nc.vector.max_index(idx(j)[:, 0:8], vals(j)[:, 0:8], src(j)))
                chain.join()
                for j in range(n):
                    chain.mark(nc.vector.match_replace(src(j), vals(j)[:, 0:8], src(j), NEG))
                chain.join()
                for j in range(n):
                    chain.mark(nc.vector.max(vals(j)[:, 8:16], src(j)))
                chain.join()
                for j in range(n):
                    chain.mark(nc.vector.max_index(idx(j)[:, 8:16], vals(j)[:, 8:16], src(j)))
                chain.join()

            for t, (t0, w) in enumerate(TILES):
                sub_t = sub_s[t % 2]
                dve.wait_ge(ff["sub_evac"], 4 * (t + 1))
                top16(w, lambda j: tv[0:w, j, :], lambda j: ti[0:w, j, :], lambda j: sub_t[0:w, j, :], 2 * PH)
                dve.sem_inc(ff["sub_free"], 1)
                chain.mark(nc.vector.tensor_copy(tif[0:w], ti[0:w]))
                tv4 = tv[0:w].rearrange("p (h c) k -> p h c k", c=2)
                chain.link(tt(out=cand[0:w], in0=bc(tv4[:, :, 0, :], 3, TOPK), in1=bc(tv4[:, :, 1, :], 2, TOPK), op=ALU.add))
                top16(w, lambda j: bv[0:w, j, :], lambda j: bi[0:w, j, :],
                      lambda j: cand[0:w, j].rearrange("p a b -> p (a b)"), PH)
                chain.mark(nc.vector.tensor_copy(gsum[0:w, 0, :], bv[0:w, :, 0]))
                chain.mark(ts(bhl[0:w, 0], bi[0:w], 4, None, ALU.logical_shift_right))
                chain.link(ts(bhl[0:w, 1], bi[0:w], TOPK - 1, None, ALU.bitwise_and))
                tt(out=bv[0:w], in0=bv[0:w], in1=bc(gsum[0:w, 0, :], 2, TOPK), op=ALU.subtract).then_inc(ff["top_exp"], 1)
                chain.link(nc.vector.tensor_copy(bhlf[0:w], bhl[0:w]))
                if t:
                    dve.wait_ge(ff["picks_turned"], t)
                tif4 = tif[0:w].rearrange("p (h c) k -> p h c k", c=2)
                eq3 = eq[0:w].rearrange("p h k a -> p (h k) a")
                for c in range(2):
                    chain.link(tt(out=eq3, in0=bc(bhlf[0:w, c].rearrange("p h k -> p (h k)"), 2, TOPK),
                                  in1=bc(asc[0:w, 0:TOPK], 1, PH * TOPK), op=ALU.is_equal))
                    chain.link(tt(out=eq[0:w], in0=eq[0:w], in1=bc(tif4[:, :, c, :], 2, TOPK), op=ALU.mult))
                    chain.link(nc.vector.tensor_reduce(picks[0:w, c, :], eq3, axis=AX.X, op=ALU.add))
                dve.wait_ge(ff["top_expd"], t + 1)
                chain.link(nc.vector.tensor_reduce(gsum[0:w, 0, :], bv[0:w], axis=AX.X, op=ALU.add))
                chain.link(nc.vector.reciprocal(gsum[0:w, 1, :], gsum[0:w, 0, :]))
                tt(out=picks[0:w, 2, :].rearrange("p (h k) -> p h k", k=TOPK), in0=bv[0:w], in1=bc(gsum[0:w, 1, :], 2, TOPK),
                   op=ALU.mult).then_inc(ff["picks"], 1)
                dve.wait_ge(ff["picks"], t + 1)
                dve.wait_ge(ff["picks_turned"], t + 1)
                for j in range(3):
                    chain.mark(nc.vector.tensor_copy(picks_t[:, j, t0:t0 + w], bank[6][:, j * P:j * P + w]))
                chain.join()
                dve.sem_inc(ff["picks_t"], 1)
            with dve.Fori(0, GBLOCKS // 2) as i:
                for s in range(2):
                    nc.vector.tensor_copy(cols_s[:, s], picks_t[:, :, bass.ds((2 * i + s) * GT, GT)]).then_inc(ff["cols"], 1)
                    dve.wait_ge(ff["cols"], 2 * i + s + 1)
                    for n in range(QUADS):
                        q = s * QUADS + n
                        dve.wait_ge(ff["gate_mm"], i * (2 * QUADS) + (q + 1))
                        for j in range(4):
                            c = 4 * n + j
                            ts(one1[q % 2][:, j, :], asc, cols_s[:, s, 0, c:c + 1], cols_s[:, s, 2, c:c + 1], ALU.is_equal, ALU.mult)
                            last = ts(one2[q % 2][:, j, :], asc, cols_s[:, s, 1, c:c + 1], None, ALU.is_equal)
                        last.then_inc(ff["ones1"], 1)
            dve_dense(dve, chain)

        def pool_ffn(pool, chain):
            for k in range(NW1, NW3):
                pool.wait_ge(w_hi_ready, k + 1)
                pool.wait_ge(w_used, k - 1)
                nc.gpsimd.tensor_tensor(out=w_lo[:, k % 2], in0=w_raw[:], in1=w_hi[:, k % 2].bitcast(F32),
                                        op=ALU.subtract).then_inc(w_lo_ready, 1)
            pool.sem_inc(ff["gate_mm"], 2)
            for s in range(2):
                pool.sem_inc(gate_out[s], 16)
            pool_dense(pool, chain)

        READY1 = 9 * NT + 2 * 3 * BH

        dn = {n: S_("dense_" + n) for n in "uhi ulo vhi vlo pre gelu mul ahi alo acc outs yturn yadd".split()}
        u_in = [S_(f"u_in{s}") for s in range(2)]
        v_in = [S_(f"v_in{s}") for s in range(2)]
        g_in = [S_(f"g_in{s}") for s in range(2)]
        y_out, cache_out, y_free = S_("y_out"), S_("cache_out"), S_("y_free")
        NE = PK
        ITERS = NE // 4 - 1
        ROWS = 64
        OUT_TILES = 2 * CH

        def one(e):
            return bass.ds(e, 1)

        def sp_dense(sp):
            def load_u(e, s):
                sp.dma_start(u_raw[s][:], eu[one(e)].rearrange("o p c n -> p (o c) n")).then_inc(u_in[s], 16)

            def load_v(e, s):
                sp.dma_start(v_raw[s][:], ev[one(e)].rearrange("o p n -> p (o n)")).then_inc(v_in[s], 16)

            def load_g(g, s):
                sp.dma_start(gin[s][:], gates_dram[:, :, bass.ds(2 * g, 2), :].rearrange("b p a t -> p b (a t)")).then_inc(g_in[s], 16)

            for s in range(2):
                load_u(s, s)
                load_v(s, s)
                load_g(s, s)
            with sp.Fori(0, ITERS) as i:
                for j in range(2, 6):
                    sp.wait_ge(dn["ulo"], i * 4 + (j - 1))
                    load_u(i * 4 + j, j % 2)
                    sp.wait_ge(dn["vlo"], i * 4 + (j - 1))
                    load_v(i * 4 + j, j % 2)
                    if j % 2 and j < 4:
                        sp.wait_ge(dn["mul"], i * 4 + 2)
                        load_g(i * 2 + 2, 0)
                    elif j % 2:
                        sp.wait_ge(dn["mul"], i * 4 + 4)
                        load_g(i * 2 + 3, 1)
            for j in range(2):
                sp.wait_ge(dn["ulo"], NE - 3 + j)
                sp.wait_ge(dn["vlo"], NE - 3 + j)
                load_u(NE - 2 + j, j)
                load_v(NE - 2 + j, j)
            for t, (t0, w) in enumerate(TILES):
                sp.wait_ge(dn["yadd"], 2 * (t + 1))
                dst = y_p[t0:t0 + w, :] if t < NT - 1 else y_s
                sp.dma_start(dst, X[0:w, t, :]).then_inc(y_out, 16)
            sp.wait_ge(y_out, 16 * NT)
            sp.wait_ge(kv_out, 16 * (2 * (NT - 1) + 2 * NB))
            sp.wait_ge(conv_out_sem, 16)
            sp.wait_ge(S_("states_out"), 32)
            sp.wait_ge(cache_out, 16 * 2 * (ITERS + 1))

        def pe_dense(pe, product):
            def pre(e, s):
                pe.wait_ge(dn["ulo"], e + 1)
                pe.wait_ge(dn["gelu"], 2 * e - 2) if not isinstance(e, int) or e >= 2 else None
                for h in range(2):
                    cols = slice(h * HALF, (h + 1) * HALF)
                    last = product(bank[2 * s + h][:, 0:HALF],
                                   [(u_hi[s][:, c, :], u_lo[s][:, c, :], hn_hi[:, c, cols], hn_lo[:, c, cols]) for c in range(CH)])
                    last.then_inc(dn["pre"], 1)

            def outs(g, s):
                pe.wait_ge(dn["alo"], 2 * g + 2)
                pe.wait_ge(dn["vlo"], 2 * g + 2)
                for d in range(CH):
                    for h in range(2):
                        x = 2 * d + h
                        cols, dc = slice(h * HALF, (h + 1) * HALF), slice(d * P, (d + 1) * P)
                        pe.wait_ge(dn["acc"], OUT_TILES * g + (x + 1))
                        product(bank[4 + x % 4][:, 0:HALF],
                                [(v_hi[2 * s + j][:, dc], v_lo[2 * s + j][:, dc], a_hi[2 * s + j][:, cols], a_lo[2 * s + j][:, cols])
                                 for j in range(2)]).then_inc(dn["outs"], 1)

            pe.wait_ge(ff["gate_bank"], (GBLOCKS // 2) * 2 * QUADS + 2)
            pe.sem_inc(dn["outs"], OUT_TILES)
            pre(0, 0)
            pre(1, 1)
            with pe.Fori(0, ITERS) as i:
                pre(i * 4 + 2, 0)
                pre(i * 4 + 3, 1)
                outs(i * 2, 0)
                pre(i * 4 + 4, 0)
                pre(i * 4 + 5, 1)
                outs(i * 2 + 1, 1)
            pre(NE - 2, 0)
            pre(NE - 1, 1)
            outs(NE // 2 - 2, 0)
            outs(NE // 2 - 1, 1)
            pe.wait_ge(dn["acc"], 4 + OUT_TILES * NE // 2)
            for m in range(2 * NT):
                t0, w = TILES[m // 2]
                if m >= 2:
                    pe.wait_ge(dn["yadd"], m - 1)
                for j in range(4):
                    c = 4 * (m % 2) + j
                    if w == P:
                        last = nc.tensor.transpose(quad(m % 2)[:, j, :], y_t[:, c, t0:t0 + w], ident)
                    else:
                        last = nc.tensor.matmul(quad(m % 2)[0:w, j, :], y_t[:, c, t0:t0 + w], ident, start=True, stop=True)
                last.then_inc(dn["yturn"], 1)

        def act_dense(act, chain):
            def split_u(e, s):
                act.wait_ge(u_in[s], 8 * (e - s) + 16)
                if not isinstance(e, int) or e >= 2:
                    act.wait_ge(dn["pre"], 2 * e - 2)
                nc.scalar.activation(u_hi[s][:], u_raw[s][:], ACT.Copy).then_inc(dn["uhi"], 1)

            def step(e, j, more=True):
                s = j % 2
                if more:
                    split_u(e + 1, 1 - s)
                act.wait_ge(v_in[s], 8 * (e - s) + 16)
                if not isinstance(e, int) or e >= 4:
                    act.wait_ge(dn["outs"], OUT_TILES // 2 * (e - s))
                nc.scalar.activation(v_hi[j][:], v_raw[s][:], ACT.Copy).then_inc(dn["vhi"], 1)
                if not isinstance(e, int) or e >= 2:
                    act.wait_ge(dn["alo"], e - 1)
                for h in range(2):
                    act.wait_ge(dn["pre"], 2 * e + (h + 1))
                    nc.scalar.activation(act_g[s][:, h * HALF:(h + 1) * HALF], bank[2 * s + h][:, 0:HALF], ACT.Gelu).then_inc(dn["gelu"], 1)
                act.wait_ge(dn["mul"], e + 1)
                nc.scalar.activation(a_hi[j][:], act_g[s][:], ACT.Copy).then_inc(dn["ahi"], 1)

            def copy_cache(row0, n):
                for dst, src in ((k_s, kc), (v_s, vc)):
                    act.dma_start(dst[:, bass.ds(row0, n), :], src[:, bass.ds(row0 + NL, n), :]).then_inc(cache_out, 16)

            act.wait_ge(gate_out[0], 16 * (GBLOCKS // 2) + 16)
            act.wait_ge(gate_out[1], 16 * (GBLOCKS // 2) + 16)
            split_u(0, 0)
            step(0, 0)
            step(1, 1, more=True)
            with act.Fori(0, ITERS) as i:
                copy_cache(i * ROWS, ROWS)
                for j in range(2, 6):
                    step(i * 4 + j, j % 4)
            copy_cache(ITERS * ROWS, PAST - NL - ITERS * ROWS)
            step(NE - 2, 2)
            step(NE - 1, 3, more=False)

        def dve_dense(dve, chain):
            tt = nc.vector.tensor_tensor

            def weigh(e, j):
                s, g = j % 2, (j // 2) % 2
                if j % 2 == 0:
                    dve.wait_ge(g_in[g], 8 * (e - j % 4) // 2 + 16) if isinstance(e, int) else None
                dve.wait_ge(dn["gelu"], 2 * e + 2)
                t3 = act_g[s][:].rearrange("p (b t) -> p b t", b=GBLOCKS)
                tt(out=t3, in0=t3, in1=gin[g][:, :, j % 2, :], op=ALU.mult).then_inc(dn["mul"], 1)
                dve.wait_ge(dn["ahi"], e + 1)
                tt(out=a_lo[j][:], in0=act_g[s][:], in1=a_hi[j][:].bitcast(F32), op=ALU.subtract).then_inc(dn["alo"], 1)

            def accumulate(g):
                for x in range(OUT_TILES):
                    y = y_t[:, x // 2, (x % 2) * HALF:(x % 2 + 1) * HALF]
                    dve.wait_ge(dn["outs"], OUT_TILES * g + (OUT_TILES + x + 1))
                    tt(out=y, in0=y, in1=bank[4 + x % 4][:, 0:HALF], op=ALU.add).then_inc(dn["acc"], 1)

            dve.wait_ge(gate_out[1], 16 * (GBLOCKS // 2) + 16)
            chain.link(nc.vector.memset(y_t[:], 0.0))
            dve.sem_inc(dn["acc"], 4)
            dve.wait_ge(g_in[0], 16)
            weigh(0, 0)
            weigh(1, 1)
            with dve.Fori(0, ITERS) as i:
                dve.wait_ge(g_in[1], 16 * i + 16)
                weigh(i * 4 + 2, 2)
                weigh(i * 4 + 3, 3)
                accumulate(i * 2)
                dve.wait_ge(g_in[0], 16 * i + 32)
                weigh(i * 4 + 4, 0)
                weigh(i * 4 + 5, 1)
                accumulate(i * 2 + 1)
            dve.wait_ge(g_in[1], 16 * ITERS + 16)
            weigh(NE - 2, 2)
            weigh(NE - 1, 3)
            accumulate(NE // 2 - 2)
            accumulate(NE // 2 - 1)
            dve.wait_ge(dn["acc"], 4 + OUT_TILES * NE // 2)
            for m in range(2 * NT):
                t0, w = TILES[m // 2]
                dve.wait_ge(dn["yturn"], m + 1)
                x = X[0:w, m // 2, 512 * (m % 2):512 * (m % 2 + 1)].rearrange("p (j d) -> p j d", j=4)
                tt(out=x, in0=x, in1=quad(m % 2)[0:w], op=ALU.add).then_inc(dn["yadd"], 1)

        def pool_dense(pool, chain):
            def lo_u(e, s):
                pool.wait_ge(dn["uhi"], e + 1)
                nc.gpsimd.tensor_tensor(out=u_lo[s][:], in0=u_raw[s][:], in1=u_hi[s][:].bitcast(F32), op=ALU.subtract).then_inc(dn["ulo"], 1)

            def lo_v(e, j):
                pool.wait_ge(dn["vhi"], e + 1)
                nc.gpsimd.tensor_tensor(out=v_lo[j][:], in0=v_raw[j % 2][:], in1=v_hi[j][:].bitcast(F32), op=ALU.subtract).then_inc(dn["vlo"], 1)

            lo_u(0, 0)
            for e in range(2):
                lo_u(e + 1, 1 - e)
                lo_v(e, e)
            with pool.Fori(0, ITERS) as i:
                for j in range(2, 6):
                    lo_u(i * 4 + (j + 1), (j + 1) % 2)
                    lo_v(i * 4 + j, j % 4)
            lo_u(NE - 1, 1)
            lo_v(NE - 2, 2)
            lo_v(NE - 1, 3)

        def sp_windows(sp):
            for t, (t0, w) in enumerate(TILES):
                sp.wait_ge(rope_done, t + 1)
                sp.wait_ge(proj_evac, 5 * NT + t + 1)
                if t < NT - 1:
                    sp.dma_start(k_p[t0:t0 + w, :], qk[0:w, t, 512:1024]).then_inc(kv_out, 16)
                    sp.dma_start(v_p[t0:t0 + w, :], av[0:w, t, :]).then_inc(kv_out, 16)
                else:
                    for dst, src in ((k_s, qk[0:w, t, 512:1024]), (v_s, av[0:w, t, :])):
                        for b in range(NB):
                            sp.dma_start(dst[b, PAST - NL:PAST, :], src[b * NL:(b + 1) * NL]).then_inc(kv_out, 16)

        def sp_mix(sp):
            sp.wait_ge(cso_done, 3 * BH)
            sp.dma_start(conv_out, cso[:]).then_inc(conv_out_sem, 16)
            sp_delta(sp)
            sp_sample(sp)
            sp_ffn(sp)

        @block.sync
        def _(sp):
            for t in range(NT):
                src = x_p[t * P:(t + 1) * P, :] if t < NT - 1 else x_s
                sp.dma_start(X[0:TILES[t][1], t, :], src).then_inc(x_in[t], 16)
                if t == 0:
                    sp.dma_start(nmix_b[:], nmix.partition_broadcast(P)).then_inc(consts_in, 16)
                    sp.dma_start(sq[:], squares).then_inc(consts_in, 16)
                    sp.dma_start(wg8_raw[:], wg8).then_inc(consts_in, 16)
            for k in range(NW1):
                if k:
                    sp.wait_ge(w_hi_ready, k)
                    sp.wait_ge(w_lo_ready, k)
                sp.dma_start(w_raw[:], win[order1[k]]).then_inc(w_in, 16)
                if k == 9:
                    sp_windows(sp)
                if k == 0:
                    for dst, src in ((pos[:], pos_t), (qkw_b[:], qkw.partition_broadcast(P)), (convw_t[:], convw),
                                     (dnw_b[:], dnw.partition_broadcast(P)), (gconst[:, 0, :], alog.partition_broadcast(P)),
                                     (gconst[:, 1, :], dtb.partition_broadcast(P)), (cst[:], conv_state),
                                     (lncp[:], lnc_p), (lncs[:], lnc_s)):
                        sp.dma_start(dst, src).then_inc(small_in, 16)
            sp_mix(sp)

        @block.scalar
        def _(act):
            chain = Chain(act, act_chain)
            act.wait_ge(dve_chain, 1)
            for t, (t0, w) in enumerate(TILES):
                act.wait_ge(x_in[t], 16)
                chain.link(nc.scalar.activation(tmp1[0:w, :], X[0:w, t, :], ACT.Square, accum_out=stat[0:w, 0, t:t + 1]))
                act.sem_inc(ssq_ready, 1)
            act.wait_ge(var_ready, 1)
            nc.scalar.activation(stat[:, 1, :], stat[:, 1, :], ACT.Sqrt).then_inc(rstd_ready, 1)

            def split_hi(k):
                act.wait_ge(w_in, 16 * (k + 1))
                if k >= 2:
                    act.wait_ge(w_used, k - 1)
                nc.scalar.activation(w_hi[:, k % 2], w_raw[:], ACT.Copy).then_inc(w_hi_ready, 1)

            split_hi(0)
            for m in range(2 * NT):
                t0, w = TILES[m // 2]
                act.wait_ge(xs_turned, m + 1)
                nc.scalar.activation(xn_hi[:, 4 * (m % 2):4 * (m % 2) + 4, t0:t0 + w], quad(m % 2, w), ACT.Copy)\
                    .then_inc(xn_hi_ready, 1)
            split_hi(1)
            uses = 0
            for k in range(8):
                for t, (t0, w) in enumerate(TILES):
                    act.wait_ge(proj_ready, uses + 1)
                    src = bank[2 + uses % 4][rows(t), 0:WC]
                    if k < 4:
                        dst = qk[0:w, t, k * WC:(k + 1) * WC]
                    elif k < 6:
                        dst = av[0:w, t, (k - 4) * WC:(k - 3) * WC]
                    else:
                        dst = bz[0:w, t, (k - 6) * WC:(k - 5) * WC]
                    nc.scalar.activation(dst, src, ACT.Silu if k >= 6 else ACT.Copy).then_inc(proj_evac, 1)
                    uses += 1
                split_hi(k + 2)
                if k == 4:
                    act.wait_ge(rope_var, NT)
                    nc.scalar.activation(ropes[:], ropes[:], ACT.Sqrt).then_inc(rope_rs, 1)
            for t, (t0, w) in enumerate(TILES):
                act.wait_ge(proj_ready, uses + 1)
                nc.scalar.activation(g8[0:w, t, :], bank[2 + uses % 4][rows(t), 0:8], ACT.Copy).then_inc(proj_evac, 1)
                uses += 1
            E0 = 3 + SEQ

            def silu(c):
                act.wait_ge(conv_done, c + 1)
                if c == 0:
                    act.wait_ge(qk_turned, 2 * NT)
                    act.wait_ge(kv_out, 16 * (2 * (NT - 1) + 2 * NB))
                nc.scalar.activation(co[:, c, :], cy[:, c % 2, :], ACT.Silu).then_inc(silu_done, 1)

            for c in range(3 * BH):
                if c == 0:
                    act.wait_ge(rope_done, NT)
                    act.wait_ge(qkt_ready, 2 * NT)
                if c >= 2:
                    act.wait_ge(conv_done, c - 1)
                    act.wait_ge(cso_done, c - 1)
                slot = ext[:, c % 2, :]
                act.wait_ge(proj_ready, uses + 1)
                nc.scalar.activation(slot[:, 3:3 + HALF], bank[2 + uses % 4][:, 0:HALF], ACT.Copy).then_inc(proj_evac, 1)
                uses += 1
                act.wait_ge(proj_ready, uses + 1)
                b = bank[2 + uses % 4]
                chain.mark(nc.scalar.activation(slot[:, 3 + HALF:3 + SEQ], b[:, 0:SEQ - HALF], ACT.Copy))
                nc.scalar.activation(slot[:, E0:E0 + NB * 7].rearrange("p (b j) -> p b j", b=NB)[:, :, 3:7],
                                     b[:, SEQ - HALF:HALF].rearrange("p (b j) -> p b j", b=NB), ACT.Copy)\
                    .then_inc(proj_evac, 1)
                chain.join()
                act.wait_ge(proj_evac, uses + 1)
                act.sem_inc(ext_ready, 1)
                uses += 1
                if c % 2 and 8 + c // 2 + 2 < NW1:
                    split_hi(8 + c // 2 + 2)
                if c:
                    silu(c - 1)
            silu(3 * BH - 1)
            act.wait_ge(gates_v, 1)
            chain.mark(nc.scalar.activation(beta[:], g8[:, :, 0:BH], ACT.Sigmoid))
            chain.mark(nc.scalar.activation(nega[:], gconst[:, 0, :], ACT.Exp))
            chain.link(nc.scalar.activation(gl[:], gl[:], ACT.Exp, scale=-1.0))
            act.sem_inc(gates_e, 1)
            act.wait_ge(gates_v, 2)
            chain.link(nc.scalar.activation(gl[:], gl[:], ACT.Ln))
            act.sem_inc(gates_e, 1)
            for c in range(2 * BH):
                act.wait_ge(l2_inv, c + 1)
                nc.scalar.activation(l2r[:, c % 2, :], l2r[:, c % 2, :], ACT.Sqrt,
                                     scale=1.0 / BD if c < BH else 1.0).then_inc(l2_rt, 1)
            act_attend(act, chain)
            act_delta(act, chain)
            act_sample(act, chain)
            act_ffn(act, chain)

        @block.vector
        def _(dve):
            chain = Chain(dve, dve_chain)
            chain.mark(nc.vector.memset(stat[:], 1.0))
            nc.vector.memset(ropes[:], 1.0).then_inc(rope_var, 0) if False else chain.mark(nc.vector.memset(ropes[:], 1.0))
            chain.mark(nc.vector.memset(g8[:], 0.0))
            dve.wait_ge(ssq_ready, NT)
            chain.link(nc.vector.tensor_scalar(stat[:, 1, :], stat[:, 0, :], 1.0 / D, EPS, ALU.mult, ALU.add))
            nc.vector.reciprocal(stat[:, 1, :], stat[:, 1, :]).then_inc(var_ready, 1)
            dve.wait_ge(rstd_ready, 1)
            dve.wait_ge(consts_in, 16 * NCONST)

            def scale_tokens(t):
                t0, w = TILES[t]
                if t >= 2:
                    dve.wait_ge(xs_turned, 2 * (t - 1))
                nc.vector.scalar_tensor_tensor(out=xs[0:w, t % 2, :], in0=X[0:w, t, :], scalar=stat[0:w, 1, t:t + 1],
                                               in1=nmix_b[0:w, :], op0=ALU.mult, op1=ALU.mult).then_inc(xs_ready, 1)
            scale_tokens(0)
            for m in range(2 * NT):
                t0, w = TILES[m // 2]
                if m % 2 == 0 and m // 2 + 1 < NT:
                    scale_tokens(m // 2 + 1)
                hi = xn_hi[:, 4 * (m % 2):4 * (m % 2) + 4, t0:t0 + w].bitcast(F32)
                dve.wait_ge(xn_hi_ready, m + 1)
                nc.vector.tensor_tensor(out=xn_lo[:, 4 * (m % 2):4 * (m % 2) + 4, t0:t0 + w], in0=quad(m % 2, w),
                                        in1=hi, op=ALU.subtract).then_inc(xn_lo_ready, 1)
            dve.wait_ge(small_in, 16 * 9)
            for j in range(2):
                chain.mark(nc.vector.tensor_tensor(out=cw[:, :, j, :], in0=pos[:, 0], in1=bc(qkw_b[:, j, 0, :], 1, NT), op=ALU.mult))
                chain.mark(nc.vector.tensor_tensor(out=sw[:, :, j, :], in0=pos[:, 1], in1=bc(qkw_b[:, j, 1, :], 1, NT), op=ALU.mult))
            chain.join()
            for t, (t0, w) in enumerate(TILES):
                dve.wait_ge(proj_evac, 3 * NT + t + 1)
                chain.link(nc.vector.tensor_tensor(out=tmp1[0:w, :], in0=qk[0:w, t, :], in1=qk[0:w, t, :], op=ALU.mult))
                chain.link(nc.vector.tensor_reduce(ropes[0:w, t, :], tmp1[0:w, :].rearrange("p (h e) -> p h e", e=AD),
                                                   axis=AX.X, op=ALU.add))
                chain.link(nc.vector.tensor_scalar(ropes[0:w, t, :], ropes[0:w, t, :], 1.0 / AD, EPS, ALU.mult, ALU.add))
                nc.vector.reciprocal(ropes[0:w, t, :], ropes[0:w, t, :]).then_inc(rope_var, 1)
            dve.wait_ge(rope_rs, 1)
            chain.link(nc.vector.tensor_scalar(ropes[:, :, 0:8], ropes[:, :, 0:8], AD ** -0.5, None, ALU.mult))
            for t, (t0, w) in enumerate(TILES):
                q4 = qk[0:w, t, :].rearrange("p (j h e) -> p j h e", j=2, e=AD)
                q3 = qk[0:w, t, :].rearrange("p (h e) -> p h e", e=AD)
                t4 = tmp1[0:w, :].rearrange("p (j h e) -> p j h e", j=2, e=AD)
                u4 = tmp2[0:w, :].rearrange("p (j h e) -> p j h e", j=2, e=AD)
                chain.link(nc.vector.tensor_tensor(out=q3, in0=q3, in1=bc(ropes[0:w, t, :], 2, AD), op=ALU.mult))
                H = AD // 2
                chain.mark(nc.vector.tensor_tensor(out=t4, in0=q4, in1=bc(cw[0:w, t], 2, AH), op=ALU.mult))
                chain.mark(nc.vector.tensor_tensor(out=u4[:, :, :, 0:H], in0=q4[:, :, :, H:AD], in1=bc(sw[0:w, t, :, 0:H], 2, AH), op=ALU.mult))
                chain.link(nc.vector.tensor_tensor(out=u4[:, :, :, H:AD], in0=q4[:, :, :, 0:H], in1=bc(sw[0:w, t, :, H:AD], 2, AH), op=ALU.mult))
                nc.vector.tensor_tensor(out=qk[0:w, t, :], in0=tmp1[0:w, :], in1=tmp2[0:w, :], op=ALU.add).then_inc(rope_done, 1)
                if t < NT - 1:
                    dve.wait_ge(rope_done, t + 1)
            for m in range(2 * NT):
                t0, w = TILES[m // 2]
                dve.wait_ge(qk_turned, m + 1)
                nc.vector.tensor_copy(qkt[:, 4 * (m % 2):4 * (m % 2) + 4, t0:t0 + w], quad(m % 2, w)).then_inc(qkt_ready, 1)
            dve.wait_ge(proj_evac, 8 * NT)
            bz4 = bz[:, 0:NT - 1, :].rearrange("p t (h e) -> p (t h) e", e=BD)
            chain.mark(nc.vector.tensor_tensor(out=bz4, in0=bz4, in1=bc(dnw_b[:], 1, (NT - 1) * BH), op=ALU.mult))
            bz1 = bz[0:NB * NL, NT - 1, :].rearrange("p (h e) -> p h e", e=BD)
            chain.mark(nc.vector.tensor_tensor(out=bz1, in0=bz1, in1=bc(dnw_b[0:NB * NL], 1, BH), op=ALU.mult))
            dve.wait_ge(qkt_ready, 2 * NT)
            E0 = 3 + SEQ
            for s in range(2):
                chain.link(nc.vector.memset(ext[:, s, 0:3], 0.0))
            for c in range(3 * BH):
                dve.wait_ge(ext_ready, c + 1)
                dve.wait_ge(ext_state, c + 1)
                if c >= 2:
                    dve.wait_ge(silu_done, c - 1)
                slot = ext[:, c % 2, :]
                es = slot[:, E0:E0 + NB * 7].rearrange("p (b j) -> p b j", b=NB)
                yp_, ys_ = cy[:, c % 2, 0:SEQ], cy[:, c % 2, SEQ:TOK].rearrange("p (b j) -> p b j", b=NB)
                chain.mark(nc.vector.tensor_scalar(yp_, slot[:, 0:SEQ], convw_t[:, c, 0:1], None, ALU.mult))
                chain.link(nc.vector.tensor_scalar(ys_, es[:, :, 0:NL], convw_t[:, c, 0:1], None, ALU.mult))
                for j in range(1, CONV):
                    chain.mark(nc.vector.scalar_tensor_tensor(out=yp_, in0=slot[:, j:j + SEQ], scalar=convw_t[:, c, j:j + 1],
                                                              in1=yp_, op0=ALU.mult, op1=ALU.add))
                    chain.link(nc.vector.scalar_tensor_tensor(out=ys_, in0=es[:, :, j:j + NL], scalar=convw_t[:, c, j:j + 1],
                                                              in1=ys_, op0=ALU.mult, op1=ALU.add))
                dve.sem_inc(conv_done, 1)
            dve.wait_ge(proj_evac, 9 * NT)
            chain.link(nc.vector.tensor_tensor(out=gz[:], in0=g8[:, :, BH:2 * BH], in1=bc(gconst[:, 1, :], 1, NT), op=ALU.add))
            chain.link(nc.vector.scalar_tensor_tensor(out=gl[:], in0=gz[:], scalar=-1.0, in1=gz[:], op0=ALU.mult, op1=ALU.max))
            dve.sem_inc(gates_v, 1)
            chain.mark(nc.vector.tensor_scalar(gz[:], gz[:], 0.0, None, ALU.max))
            dve.wait_ge(gates_e, 1)
            chain.link(nc.vector.tensor_scalar(gl[:], gl[:], 1.0, None, ALU.add))
            dve.sem_inc(gates_v, 1)
            dve.wait_ge(gates_e, 2)
            chain.link(nc.vector.tensor_tensor(out=gl[:], in0=gl[:], in1=gz[:], op=ALU.add))
            chain.link(nc.vector.scalar_tensor_tensor(out=gate_g[:], in0=gl[:], scalar=-1.0, in1=bc(nega[:], 1, NT), op0=ALU.mult, op1=ALU.mult))
            dve.sem_inc(gates_v, 1)
            dve.wait_ge(w_used, NW1)

            def l2_square(c):
                dve.wait_ge(silu_done, c + 1)
                if c >= 2:
                    dve.wait_ge(l2_sum, c - 1)
                nc.vector.tensor_tensor(out=l2s[:, c % 2, :], in0=co[:, c, :], in1=co[:, c, :], op=ALU.mult).then_inc(l2_sq, 1)

            def l2_scale(c):
                dve.wait_ge(l2_rt, c + 1)
                nc.vector.tensor_tensor(out=co[:, c, :], in0=co[:, c, :], in1=l2r[:, c % 2, :], op=ALU.mult).then_inc(l2_done, 1)
            l2_square(0)
            for c in range(2 * BH):
                if c + 1 < 2 * BH:
                    l2_square(c + 1)
                if c >= 2:
                    dve.wait_ge(l2_done, c - 1)
                dve.wait_ge(l2_sum, c + 1)
                for h in range(2):
                    cols = slice(h * HALF, (h + 1) * HALF)
                    chain.mark(nc.vector.tensor_scalar(l2r[:, c % 2, cols], bank[2 * (c % 2) + h][:, 0:HALF], EPS, None, ALU.add))
                chain.join()
                nc.vector.reciprocal(l2r[:, c % 2, :], l2r[:, c % 2, :]).then_inc(l2_inv, 1)
                if c:
                    l2_scale(c - 1)
            l2_scale(2 * BH - 1)
            dve_attend(dve, chain)
            dve_delta(dve, chain)
            dve_sample(dve, chain)
            dve_ffn(dve, chain)

        @block.gpsimd
        def _(pool):
            chain = Chain(pool, pool_chain)

            def split_lo(k):
                pool.wait_ge(w_hi_ready, k + 1)
                if k >= 2:
                    pool.wait_ge(w_used, k - 1)
                nc.gpsimd.tensor_tensor(out=w_lo[:, k % 2], in0=w_raw[:], in1=w_hi[:, k % 2].bitcast(F32),
                                        op=ALU.subtract).then_inc(w_lo_ready, 1)
            pool.wait_ge(consts_in, 16 * NCONST)
            chain.link(nc.gpsimd.tensor_copy(wg8_hi[:], wg8_raw[:]))
            nc.gpsimd.tensor_tensor(out=wg8_lo[:], in0=wg8_raw[:], in1=wg8_hi[:].bitcast(F32), op=ALU.subtract).then_inc(g8_split, 1)
            split_lo(0)
            split_lo(1)
            for k in range(8):
                split_lo(k + 2)
            pool.wait_ge(small_in, 16 * 9)
            pool.wait_ge(rope_done, NT)
            E0 = 3 + SEQ
            for c in range(3 * BH):
                slot = ext[:, c % 2, :]
                es = slot[:, E0:E0 + NB * 7].rearrange("p (b j) -> p b j", b=NB)
                if c >= 2:
                    pool.wait_ge(conv_done, c - 1)
                nc.gpsimd.tensor_copy(es[:, :, 0:3], cst[:, c]).then_inc(ext_state, 1)
                pool.wait_ge(ext_ready, c + 1)
                chain.mark(nc.gpsimd.tensor_copy(cso[:, c, 0:3], slot[:, SEQ:SEQ + 3]))
                chain.link(nc.gpsimd.tensor_copy(cso[:, c, 3:27].rearrange("p (b j) -> p b j", b=NB), es[:, :, 4:7]))
                pool.sem_inc(cso_done, 1)
                if c % 2 and 8 + c // 2 + 2 < NW1:
                    split_lo(8 + c // 2 + 2)
            pool_mix(pool, chain)

        @block.tensor
        def _(pe):
            def product(out, pairs):
                n = len(pairs)
                for i, (ah, al, bh, bl) in enumerate(pairs):
                    nc.tensor.matmul(out, ah, bh, start=i == 0, stop=False)
                    nc.tensor.matmul(out, ah, bl, start=False, stop=False)
                    last = nc.tensor.matmul(out, al, bh, start=False, stop=i == n - 1)
                return last

            pe.wait_ge(consts_in, 16 * NCONST)
            for m in range(2 * NT):
                t0, w = TILES[m // 2]
                pe.wait_ge(xs_ready, m // 2 + 1)
                if m >= 2:
                    pe.wait_ge(xn_lo_ready, m - 1)
                for j in range(4):
                    c = 4 * (m % 2) + j
                    last = nc.tensor.transpose(quad(m % 2, w)[:, j, :], xs[0:w, (m // 2) % 2, c * P:(c + 1) * P], ident[0:w, 0:w])
                last.then_inc(xs_turned, 1)
            pe.wait_ge(xn_lo_ready, 2 * NT)
            uses = 0
            for k in range(8):
                pe.wait_ge(w_lo_ready, k + 1)
                for t in range(NT):
                    if uses >= 4:
                        pe.wait_ge(proj_evac, uses - 3)
                    tok = token_columns(t)
                    last = product(bank[2 + uses % 4][:, 0:WC],
                                   [(xn_hi[:, c, tok], xn_lo[:, c, tok], w_hi[:, k % 2, c, :], w_lo[:, k % 2, c, :])
                                    for c in range(CH)])
                    last.then_inc(proj_ready, 1)
                    uses += 1
                pe.wait_ge(proj_ready, uses)
                pe.sem_inc(w_used, 1)
            pe.wait_ge(g8_split, 1)
            for t in range(NT):
                pe.wait_ge(proj_evac, uses - 3)
                tok = token_columns(t)
                product(bank[2 + uses % 4][:, 0:8],
                        [(xn_hi[:, c, tok], xn_lo[:, c, tok], wg8_hi[:, c, :], wg8_lo[:, c, :])
                         for c in range(CH)]).then_inc(proj_ready, 1)
                uses += 1
            for m in range(2 * NT):
                t0, w = TILES[m // 2]
                pe.wait_ge(rope_done, m // 2 + 1)
                if m >= 2:
                    pe.wait_ge(qkt_ready, m - 1)
                for j in range(4):
                    c = 4 * (m % 2) + j
                    last = nc.tensor.transpose(quad(m % 2, w)[:, j, :], qk[0:w, m // 2, c * P:(c + 1) * P], ident[0:w, 0:w])
                last.then_inc(qk_turned, 1)
            for c in range(3 * BH):
                k = 8 + c // 2
                pe.wait_ge(w_lo_ready, k + 1)
                wcols = slice((c % 2) * P, (c % 2) * P + P)
                for h in range(2):
                    pe.wait_ge(proj_evac, uses - 3)
                    cols = slice(h * HALF, (h + 1) * HALF)
                    product(bank[2 + uses % 4][:, 0:HALF],
                            [(w_hi[:, k % 2, i, wcols], w_lo[:, k % 2, i, wcols], xn_hi[:, i, cols], xn_lo[:, i, cols])
                             for i in range(CH)]).then_inc(proj_ready, 1)
                    uses += 1
                if c % 2:
                    pe.wait_ge(proj_ready, uses)
                    pe.sem_inc(w_used, 1)
            pe.wait_ge(proj_evac, uses)
            for c in range(2 * BH):
                pe.wait_ge(l2_sq, c + 1)
                if c >= 2:
                    pe.wait_ge(l2_inv, c - 1)
                for h in range(2):
                    last = nc.tensor.matmul(bank[2 * (c % 2) + h][:, 0:HALF], ones, l2s[:, c % 2, h * HALF:(h + 1) * HALF],
                                            start=True, stop=True)
                last.then_inc(l2_sum, 1)
            pe_attend(pe)
            pe_delta(pe)
            pe_sample(pe)
            pe_ffn(pe, product)


def kernel(**inputs):
    import concourse.bacc as bacc
    from concourse.bass_utils import run_bass_kernel_spmd as run

    a = {k: np.asarray(v) for k, v in inputs.items()}

    def tiles(w, cols):
        d, n = w.shape
        return np.ascontiguousarray(w.reshape(CH, P, n // cols, cols).transpose(2, 1, 0, 3))

    w_in = a["w_in"][0]
    main = 14 * WC
    qkw = np.stack([a["q_norm_w"][0], a["k_norm_w"][0]])
    qkw = np.stack([qkw, np.roll(qkw, AD // 2, axis=1)], 1)
    arrays = {
        "x_p": a["x_prompt"].reshape(SEQ, D),
        "x_s": a["x_sample"].reshape(NB * NL, D),
        "kc": a["cache_k_win"].reshape(NB, PAST, AH * AD),
        "vc": a["cache_v_win"].reshape(NB, PAST, AH * AD),
        "conv_state": a["state_conv"][0].transpose(2, 0, 1).reshape(3 * BH, P, NB, 3).transpose(1, 0, 2, 3),
        "s0": a["state_delta"].reshape(NB, BH, BD, BD),
        "nmix": a["norm_mix_w"].reshape(D),
        "win": tiles(w_in[:, :main], WC),
        "wg8": tiles(w_in[:, main:], 8)[0],
        "qkw": qkw,
        "convw": a["conv_w"][0].reshape(CONV, 3 * BH, P).transpose(2, 1, 0),
        "alog": a["a_log"].reshape(BH),
        "dtb": a["dt_bias"].reshape(BH),
        "dnw": a["delta_norm_w"].reshape(BD),
        "wout": tiles(a["w_out"][0], WC),
        "nffn": a["norm_ffn_w"].reshape(D),
        "wpq": tiles(a["w_pq"][0], WC),
        "skt": a["sub_keys"][0].transpose(2, 0, 1),
        "eu": tiles(a["expert_u"][0].T, P),
        "ev": a["expert_v"][0].reshape(PK, PK, D),
        "pos_t": position_tables(),
        "lnc_p": prompt_log_counts(),
        "lnc_s": sample_log_counts(),
        "squares": square_tables(),
    }
    outs = {
        "y_p": (SEQ, D), "y_s": (NB * NL, D), "k_p": (SEQ, AH * AD), "v_p": (SEQ, AH * AD),
        "conv_out": (P, 3 * BH, (NB + 1) * 3), "s_p": (BH, BD, BD),
        "k_s": (NB, PAST, AH * AD), "v_s": (NB, PAST, AH * AD), "s_s": (NB, BH, BD, BD),
    }
    nc = bacc.Bacc("TRN2", target_bir_lowering=False, num_devices=1)
    args = []
    for name, v in arrays.items():
        arrays[name] = np.ascontiguousarray(v)
        args.append(nc.dram_tensor(name, v.shape, F32, kind="ExternalInput").ap())
    for name, shape in outs.items():
        args.append(nc.dram_tensor(name, shape, F32, kind="ExternalOutput").ap())
    args.append(nc.dram_tensor("gates_dram", (GBLOCKS, P, PK, GT), F32, kind="Internal").ap())
    hybrid_step(nc, *args)
    r = run(nc, [arrays], core_ids=[0]).results[0]
    conv = r["conv_out"].transpose(1, 0, 2).reshape(3 * BH * P, NB + 1, 3).transpose(1, 2, 0)
    return (
        r["y_p"].reshape(1, SEQ, D), r["y_s"].reshape(NB, NL, D),
        r["k_p"].reshape(1, 1, SEQ, AH, AD), r["v_p"].reshape(1, 1, SEQ, AH, AD),
        np.ascontiguousarray(conv[0:1])[None], r["s_p"][None, None],
        r["k_s"].reshape(1, NB, PAST, AH, AD), r["v_s"].reshape(1, NB, PAST, AH, AD),
        np.ascontiguousarray(conv[1:])[None], r["s_s"][None],
    )
```

```python
from contextlib import ExitStack

import numpy as np

import concourse.bass as bass
from concourse import mybir

F32 = mybir.dt.float32
F32R = mybir.dt.float32r
U32 = mybir.dt.uint32
ALU = mybir.AluOpType
ACT = mybir.ActivationFunctionType
AX = mybir.AxisListType

P = 128
D = 1024
CH = D // P
SEQ, NB, NL = 512, 8, 4
TOK = SEQ + NB * NL
TILES = [(t * P, P) for t in range(SEQ // P)] + [(SEQ, NB * NL)]
NT = len(TILES)
HALF = TOK // 2
AH, AD = 8, 64
PAIRS = AH // 2
BH, BD = 4, 128
PAST = 2048
CONV = 4
EPS = 1e-6
NEG = -1e30
WC = 256
OLD_TILES, NEW_TILES = 3, 4
KTILES = OLD_TILES + NEW_TILES
CACHED = KTILES * P
PH, PK, TOPK = 8, 128, 16
EXPERTS = PK * PK
LEVELS = 7
GT = 68
GBLOCKS = TOK // GT
GB = 4
HOT = 4
AHEAD = PK // 2


def position_tables():
    half = AD // 2
    inv = np.float32(10000.0) ** (-np.arange(half, dtype=np.float32) / np.float32(half))
    pos = np.concatenate([np.arange(SEQ), np.tile(PAST + np.arange(NL), NB)]).astype(np.float32)
    ang = (pos[:, None] * inv[None, :].astype(np.float32)).astype(np.float32).astype(np.float64)
    cos, sin = np.cos(ang), np.sin(ang)
    out = np.zeros((2, NT * P, AD), np.float32)
    out[0, :TOK] = np.concatenate([cos, cos], 1)
    out[1, :TOK] = np.concatenate([-sin, sin], 1)
    return out.reshape(2, NT, P, AD).transpose(2, 0, 1, 3).copy()


def log_count(dist):
    count = np.zeros(dist.shape)
    for window, dil in ((128, 1), (512, 4), (2048, 16)):
        count += (dist >= 0) & (dist <= window) & (dist % dil == 0)
    return np.where(count > 0, np.log(np.maximum(count, 1)), NEG).astype(np.float32)


def prompt_log_counts():
    q, k = np.arange(P)[:, None], np.arange(P)[None, :]
    return np.concatenate([log_count(d * P + q - k) for d in (3, 2, 1, 0)], 1)


def sample_log_counts():
    p = np.arange(P)
    pos = [(j * 32 + p // 4) * 16 + p % 4 for j in range(OLD_TILES)]
    pos += [PAST - NEW_TILES * P + j * P + p for j in range(NEW_TILES)]
    pos = np.concatenate(pos)
    rows = PAST + np.tile(np.arange(NL), AH)
    cached = log_count(rows[:, None] - pos[None, :])
    own = log_count(np.arange(NL)[:, None] - np.arange(NL)[None, :])
    new = np.full((AH * NL, NB, NB * NL), NEG, np.float32)
    for b in range(NB):
        new[:, b, b * NL:(b + 1) * NL] = np.tile(own, (AH, 1))
    return np.concatenate([cached, new.reshape(AH * NL, -1)], 1)


def square_tables():
    i = np.arange(P)
    j, c = i[:, None], i[None, :]
    out = [j == c, np.ones((P, P)), j <= c, (j <= c) & (j // NL == c // NL), j // NL == c // NL,
           np.broadcast_to(c, (P, P))]
    for lv in range(LEVELS):
        s = 1 << lv
        out.append((j // (2 * s) == c // (2 * s)) & ((c // s) % 2 == 1) & ((j // s) % 2 == 0))
    return np.stack(out, 1).astype(np.float32)


IDENT, ONES, CUM_P, CUM_S, BLK_S, ASC, LEVEL0 = range(7)
NSQ = LEVEL0 + LEVELS


class Chain:

    def __init__(self, eng, sem):
        self.eng, self.sem, self.n = eng, sem, 0

    def mark(self, ins):
        ins.then_inc(self.sem, 1)
        self.n += 1

    def join(self):
        self.eng.wait_ge(self.sem, self.n)

    def link(self, ins):
        self.mark(ins)
        self.join()


def rows(n):
    w = TILES[n][1]
    return slice(P - w, P)


def token_columns(n):
    t0, w = TILES[n]
    return slice(t0 + w - P, t0 + w)


def bc(ap, axis, count):
    ap = ap.unsqueeze(axis)
    shape = list(ap.shape)
    shape[axis] = count
    return ap.broadcast_to(shape)


def hybrid_step(nc, x_p, x_s, kc, vc, conv_state, s0, nmix, win, wg8, qkw, convw, alog, dtb, dnw, wout, nffn,
                wpq, skt, eu, ev, pos_t, lnc_p, lnc_s, squares,
                y_p, y_s, k_p, v_p, conv_out, s_p, k_s, v_s, s_s, gates_dram, acts_dram):
    with ExitStack() as ctx:
        def sem(name):
            return ctx.enter_context(nc.semaphore(name))

        base = 16512
        top = [0]

        def at(name, offset, shape, dt=F32):
            size = int(np.prod(shape[1:])) * 4
            top[0] = max(top[0], offset + size)
            assert offset + size <= 212800, name
            return nc.alloc_sbuf_tensor_at(name, shape, dt, offset=base + offset)

        def region(offset):
            pos = [offset]

            def put(name, shape, dt=F32):
                t = at(name, pos[0], shape, dt)
                pos[0] += -(-int(np.prod(shape[1:])) * 4 // 32) * 32
                return t
            put.pos = pos
            return put

        put = region(0)
        sq = put("sq", [P, NSQ, P])
        R_NMIX = put.pos[0]
        nmix_b = put("nmix_b", [P, D])
        lncp = put("lncp", [P, 4 * P])
        lncs = put("lncs", [NB * NL, CACHED + NB * NB * NL])
        pos = put("pos", [P, 2, NT, AD])
        cw = put("cw", [P, NT, 2, AD])
        sw = put("sw", [P, NT, 2, AD])
        qkw_b = put("qkw_b", [P, 2, 2, AD])
        convw_t = put("convw_t", [P, 3 * BH, CONV])
        dnw_b = put("dnw_b", [P, BD])
        gconst = put("gconst", [P, 2, BH])
        g8 = put("g8", [P, NT, 2 * BH])
        gz = put("gz", [P, NT, BH])
        gl = put("gl", [P, NT, BH])
        gate_g = put("gate_g", [P, NT, BH])
        beta = put("beta", [P, NT, BH])
        nega = put("nega", [P, BH])
        R_STAT = put.pos[0]
        stat = put("stat", [P, 8, NT])
        ropes = put("ropes", [P, NT, 16])
        wg8_raw = put("wg8_raw", [P, CH, 8])
        wg8_hi = put("wg8_hi", [P, CH, 8], F32R)
        wg8_lo = put("wg8_lo", [P, CH, 8], F32R)
        cst = put("cst", [P, 3 * BH, NB, 3])
        cso = put("cso", [P, 3 * BH, (NB + 1) * 3])
        l2r = put("l2r", [P, 2 * BH, NT])
        smax = put("smax", [P, 2, 4])
        sstat = put("sstat", [NB * NL, 2, 8])
        R_X = put.pos[0]
        R_XN = R_X + 20480
        R_W = R_XN + 2 * CH * TOK * 4
        R_AQ = R_W + 40960
        R_AV = R_AQ + 12 * TOK * 4
        R_BZ = R_AV + NT * 512 * 4
        R_QK = R_BZ + NT * 512 * 4
        R_E = R_QK + 8 * TOK * 4

        ident, ones, asc = sq[:, IDENT, :], sq[:, ONES, :], sq[:, ASC, :]
        X = at("X", R_X, [P, NT, D])
        xs = at("xs", R_BZ, [P, 2, D])
        xn_hi = at("xn_hi", R_XN, [P, CH, TOK], F32R)
        xn_lo = at("xn_lo", R_XN + CH * TOK * 4, [P, CH, TOK], F32R)
        w_raw = at("w_raw", R_W, [P, CH, WC])
        w_hi = at("w_hi", R_W + 8192, [P, 2, CH, WC], F32R)
        w_lo = at("w_lo", R_W + 24576, [P, 2, CH, WC], F32R)
        qk = at("qk", R_AQ, [P, NT, 2 * AH * AD])
        co = at("co", R_AQ, [P, 3 * BH, TOK])
        av = at("av", R_AV, [P, NT, AH * AD])
        bz = at("bz", R_BZ, [P, NT, BH * BD])
        qkt = at("qkt", R_QK, [P, 2 * PAIRS, TOK])
        tmp1 = at("tmp1", R_E, [P, 16 * AD])
        tmp2 = at("tmp2", R_E + 4096, [P, 16 * AD])
        ext = at("ext", R_E, [P, 2, 3 + SEQ + NB * (3 + NL) + 1])
        cy = at("cy", R_E + 2 * 572 * 4 + 32, [P, 2, TOK])
        put = region(R_XN)
        l2s = at("l2s", R_X, [P, 2 * BH, TOK])
        cat = at("cat", R_X, [P, CH, TOK])
        sm = at("sm", R_E, [P, 2, 4 * P])
        pt = at("pt", R_E + 4096, [P, 2, 4, P])
        put = region(R_XN)

        def slots(name):
            return [put(f"{name}{s}", [P, BH, P]) for s in range(2)]
        eg, qd, lt, it, kd, kbg, vb, xt, xi, yv, ml, uu, wt = (
            slots(n) for n in ("eg", "qd", "lt", "it", "kd", "kbg", "vb", "xt", "xi", "yv", "ml", "uu", "wt"))
        vm = at("vm", R_XN + 2048, [P, NB, BD])
        vnt = put("vnt", [P, 3, BH, NB * NL])
        s_cur = put("s_cur", [P, BH, BD])
        gcol = put("gcol", [P, 2, 4, BH])
        ost = put("ost", [P, 2, 2, BH])
        ss0 = at("ss0", R_W + 40960 - 16384, [P, NB, BH, BD])
        assert put.pos[0] <= R_W + 40960 - 16384
        put = region(R_XN)
        ks = [put(f"ks{s}", [P, KTILES, AH * AD]) for s in range(2)]
        vs = [put(f"vs{s}", [P, KTILES, AH * AD]) for s in range(2)]
        kt = put("kt", [P, PAIRS, CACHED])
        assert put.pos[0] <= R_W + 40960
        put = region(R_E)
        sss = [put(f"sss{s}", [NB * NL, CACHED + NB * NL]) for s in range(2)]
        pts = put("pts", [P, KTILES + 1, NB * NL])
        qbd = put("qbd", [P, NB, PAIRS, NB * NL])

        cat_hi = at("cat_hi", R_AQ, [P, CH, TOK], F32R)
        cat_lo = at("cat_lo", R_AQ + CH * TOK * 4, [P, CH, TOK], F32R)
        hn_hi = at("hn_hi", R_AQ, [P, CH, TOK], F32R)
        hn_lo = at("hn_lo", R_AQ + CH * TOK * 4, [P, CH, TOK], F32R)
        R_B = R_AQ + 2 * CH * TOK * 4
        put = region(R_B)
        qt = put("qt", [P, 2 * PH, TOK])
        put = region(R_XN)
        hs = put("hs", [P, 2, D])
        cand = put("cand", [P, PH, TOPK, TOPK])
        eq = put("eq", [P, PH, TOPK, TOPK])
        tv = put("tv", [P, 2 * PH, TOPK])
        ti = put("ti", [P, 2 * PH, TOPK], U32)
        tif = put("tif", [P, 2 * PH, TOPK])
        bv = put("bv", [P, PH, TOPK])
        bi = put("bi", [P, PH, TOPK], U32)
        bhl = put("bhl", [P, 2, PH, TOPK], U32)
        bhlf = put("bhlf", [P, 2, PH, TOPK])
        picks = put("picks", [P, 3, PH * TOPK])
        gsum = put("gsum", [P, 2, PH])
        assert put.pos[0] <= R_W
        put = region(R_W)
        picks_t = put("picks_t", [P, 3, TOK])
        cols_s = put("cols_s", [P, 2, 3, GT])
        skt_s = put("skt_s", [P, 2, PK])
        sub_s = [put(f"sub_s{s}", [P, 2 * PH, PK]) for s in range(2)]
        assert put.pos[0] <= R_AQ
        put = region(put.pos[0] - 2 * 8192)
        one1 = [put(f"one1_{s}", [P, 4, PK]) for s in range(HOT)]
        one2 = [put(f"one2_{s}", [P, 4, PK]) for s in range(HOT)]
        assert put.pos[0] <= R_AQ
        gst = [at("gst0", R_XN, [P, PK, GT]), at("gst1", R_B, [P, PK, GT])]
        put = region(R_XN)
        v_raw = [put(f"v_raw{s}", [P, D]) for s in range(2)]
        v_hi = [put(f"v_hi{s}", [P, D], F32R) for s in range(4)]
        v_lo = [put(f"v_lo{s}", [P, D], F32R) for s in range(4)]
        gin = [put(f"gin{s}", [P, GBLOCKS, 2, GT]) for s in range(2)]
        assert put.pos[0] <= R_AQ
        put = region(R_NMIX)
        u_raw = [put(f"u_raw{s}", [P, CH, P]) for s in range(2)]
        u_hi = [put(f"u_hi{s}", [P, CH, P], F32R) for s in range(2)]
        u_lo = [put("u_lo0", [P, CH, P], F32R)]
        assert put.pos[0] <= R_STAT
        put = region(R_B + 2 * PH * TOK * 4)
        u_lo.append(put("u_lo1", [P, CH, P], F32R))
        act_c = [put(f"act_c{s}", [P, TOK]) for s in range(2)]
        act_l = [put(f"act_l{s}", [P, TOK]) for s in range(2)]
        put = region(R_B)
        a_hi = [put(f"a_hi{s}", [P, TOK], F32R) for s in range(4)]
        a_lo = [put(f"a_lo{s}", [P, TOK], F32R) for s in range(4)]
        y_t = put("y_t", [P, CH, TOK])

        bank = [ctx.enter_context(nc.psum_tensor(f"bank{i}", [P, 512], F32)) for i in range(8)]

        def quad(b, w=P, n=P):
            return bank[b][0:n, 0:4 * w].rearrange("p (h c) -> p h c", h=4)

        block = ctx.enter_context(nc.Block())

        NW1 = 14
        order1 = [0, 1, 2, 3, 4, 5, 12, 13, 6, 7, 8, 9, 10, 11]

        x_in = [sem(f"x_in{t}") for t in range(NT)]
        consts_in, small_in = sem("consts_in"), sem("small_in")
        ssq_ready, rstd_ready, xs_ready, xs_turned = sem("ssq_ready"), sem("rstd_ready"), sem("xs_ready"), sem("xs_turned")
        var_ready = sem("var_ready")
        xn_hi_ready, xn_lo_ready = sem("xn_hi_ready"), sem("xn_lo_ready")
        w_in, w_hi_ready, w_lo_ready, w_used = sem("w_in"), sem("w_hi_ready"), sem("w_lo_ready"), sem("w_used")
        g8_split = sem("g8_split")
        proj_ready, proj_evac = sem("proj_ready"), sem("proj_evac")
        rope_var, rope_rs, rope_done = sem("rope_var"), sem("rope_rs"), sem("rope_done")
        qk_turned, qkt_ready = sem("qk_turned"), sem("qkt_ready")
        kv_out = sem("kv_out")
        ext_ready, ext_state, conv_done, cso_done, silu_done = (
            sem("ext_ready"), sem("ext_state"), sem("conv_done"), sem("cso_done"), sem("silu_done"))
        l2_sq, l2_sum, l2_inv, l2_rt, l2_rows, l2_done = (
            sem("l2_sq"), sem("l2_sum"), sem("l2_inv"), sem("l2_rt"), sem("l2_rows"), sem("l2_done"))
        gates_v, gates_e = sem("gates_v"), sem("gates_e")
        out_done = sem("out_done")
        dve_chain, act_chain, pool_chain = sem("dve_chain"), sem("act_chain"), sem("pool_chain")
        s_scores, s_masked, s_exp, s_norm, s_turned, s_pt, s_out, s_cat = (
            sem("s_scores"), sem("s_masked"), sem("s_exp"), sem("s_norm"), sem("s_turned"), sem("s_pt"),
            sem("s_out"), sem("s_cat"))
        extra = {}

        def S_(name):
            if name not in extra:
                extra[name] = sem(name)
            return extra[name]

        NCONST = 3
        L2_BANKS = (2, 3, 5, 6)
        COPIES = 32
        ROWS = -(-PAST // COPIES)

        def copy_cache(act, n):
            a, b = n * ROWS, min((n + 1) * ROWS, PAST - NL)
            for dst, src in ((k_s, kc), (v_s, vc)):
                act.dma_start(dst[:, a:b, :], src[:, a + NL:b + NL, :]).then_inc(out_done, 16)

        UNITS = [(i, h) for i in range(SEQ // P) for h in range(AH)]

        def pe_attend(pe):
            pe.wait_ge(l2_done, 2 * BH + 1)

            def scores(u):
                i, h = UNITS[u]
                if u >= 4:
                    pe.wait_ge(s_masked, u - 3)
                r = slice(AD * (h % 2), AD * (h % 2) + AD)
                nc.tensor.matmul(bank[2 + u % 4][:, 0:(i + 1) * P], qkt[r, h // 2, i * P:(i + 1) * P],
                                 qkt[r, PAIRS + h // 2, 0:(i + 1) * P], start=True, stop=True).then_inc(s_scores, 1)

            def turn(u):
                i, h = UNITS[u]
                pe.wait_ge(s_norm, u + 1)
                if u >= 2:
                    pe.wait_ge(s_pt, u - 1)
                for j in range(i + 1):
                    last = nc.tensor.transpose(quad(u % 2)[:, j, :], sm[:, u % 2, j * P:(j + 1) * P], ident)
                last.then_inc(s_turned, 1)

            def values(u):
                i, h = UNITS[u]
                pe.wait_ge(s_pt, u + 1)
                if u >= 4:
                    pe.wait_ge(s_cat, u // 2 - 1)
                r = slice(AD * (h % 2), AD * (h % 2) + AD)
                for j in range(i + 1):
                    last = nc.tensor.matmul(bank[6 + (u // 2) % 2][r, 0:P], av[:, j, h * AD:(h + 1) * AD], pt[:, u % 2, j, :],
                                            start=j == 0, stop=j == i)
                last.then_inc(s_out, 1)

            for u in range(3):
                scores(u)
            for u in range(len(UNITS)):
                turn(u)
                if u:
                    values(u - 1)
                if u + 3 < len(UNITS):
                    scores(u + 3)
            values(len(UNITS) - 1)

        def dve_attend(dve, chain):
            dve.wait_ge(silu_done, 3 * BH)
            dve.wait_ge(cso_done, 3 * BH)

            def mask(u):
                i, h = UNITS[u]
                n = (i + 1) * P
                dve.wait_ge(s_scores, u + 1)
                if u >= 2:
                    dve.wait_ge(s_turned, u - 1)
                chain.link(nc.vector.tensor_tensor_reduce(
                    out=sm[:, u % 2, 0:n], in0=bank[2 + u % 4][:, 0:n], in1=lncp[:, 4 * P - n:4 * P], scale=1.0,
                    scalar=NEG, op0=ALU.add, op1=ALU.max, accum_out=smax[:, u % 2, 0:1]))
                nc.vector.tensor_scalar(smax[:, u % 2, 1:2], smax[:, u % 2, 0:1], -1.0, None, ALU.mult).then_inc(s_masked, 1)

            mask(0)
            for u in range(len(UNITS)):
                if u + 1 < len(UNITS):
                    mask(u + 1)
                n = (UNITS[u][0] + 1) * P
                dve.wait_ge(s_exp, u + 1)
                chain.link(nc.vector.reciprocal(smax[:, u % 2, 3:4], smax[:, u % 2, 2:3]))
                nc.vector.tensor_scalar(sm[:, u % 2, 0:n], sm[:, u % 2, 0:n], smax[:, u % 2, 3:4], None, ALU.mult).then_inc(s_norm, 1)

        def act_attend(act, chain):
            def turned(u):
                i, h = UNITS[u]
                act.wait_ge(s_turned, u + 1)
                if u >= 2:
                    act.wait_ge(s_out, u - 1)
                nc.scalar.activation(pt[:, u % 2, 0:i + 1, :], quad(u % 2)[:, 0:i + 1, :], ACT.Copy).then_inc(s_pt, 1)

            def pair(v):
                i = UNITS[2 * v][0]
                act.wait_ge(s_out, 2 * v + 2)
                nc.scalar.activation(cat[:, v % PAIRS, i * P:(i + 1) * P], bank[6 + v % 2][:, 0:P], ACT.Copy).then_inc(s_cat, 1)

            for u in range(len(UNITS)):
                n = (UNITS[u][0] + 1) * P
                act.wait_ge(s_masked, u + 1)
                nc.scalar.activation(sm[:, u % 2, 0:n], sm[:, u % 2, 0:n], ACT.Exp, bias=smax[:, u % 2, 1:2],
                                     accum_out=smax[:, u % 2, 2:3]).then_inc(s_exp, 1)
                if u:
                    turned(u - 1)
                if u % 2 == 0:
                    copy_cache(act, 8 + u // 2)
                if u >= 3 and u % 2:
                    pair(u // 2 - 1)
            turned(len(UNITS) - 1)
            pair(len(UNITS) // 2 - 1)

        GROUPS = [(0, 1), (2, 3), (4,)]
        names = ("gg rows kk tok eg gd dt dec sc front x0 x0t xi ml y yc xy xu uw uwc ws vn os s o ovar ort og ot cat "
                 "s_pe s_act s_dve vm st su")
        dl = {n: S_("delta_" + n) for n in names.split()}

        def cum(n):
            return sq[:, CUM_P if n < NT - 1 else CUM_S, :]

        def total(n):
            return sq[:, ONES if n < NT - 1 else BLK_S, :]

        def levels(n):
            return LEVELS if n < NT - 1 else 2

        def level_steps(group):
            return [(lv, n) for lv in range(1, levels(group[0])) for n in group]

        step_no = {}
        for g_ in GROUPS:
            for st_ in level_steps(g_):
                step_no[st_] = len(step_no)

        def sub(t, w, cols=None):
            return t[0:w, :, 0:(w if cols is None else cols)]

        def pe_delta(pe):
            pe.wait_ge(s_cat, len(UNITS) // 2)
            pe.wait_ge(gates_v, 3)
            pe.wait_ge(l2_done, 2 * BH + 1)
            for group in GROUPS:
                for n in group:
                    (t0, w), s = TILES[n], n % 2
                    cols = slice(t0, t0 + w)
                    if n == group[0] and n:
                        pe.wait_ge(dl["cat"], n)
                        pe.wait_ge(dl["s"], n)
                    elif n:
                        pe.wait_ge(dl["front"], n)
                        pe.wait_ge(dl["eg"], n)
                    pe.wait_ge(dl["gg"], n + 1)
                    nc.tensor.matmul(bank[6][0:w, 0:4], cum(n)[0:w, 0:w], gate_g[0:w, n, :], start=True, stop=True)
                    nc.tensor.matmul(bank[6][0:w, 4:8], total(n)[0:w, 0:w], gate_g[0:w, n, :], start=True, stop=True)
                    nc.tensor.matmul(quad(0, w), ones[0:w, :], sub(lt[s], w), start=True, stop=True)
                    nc.tensor.matmul(quad(1, w), ones[0:w, :], sub(it[s], w), start=True, stop=True).then_inc(dl["rows"], 1)
                    for h in range(BH):
                        nc.tensor.matmul(quad(2, w, w)[:, h, :], co[:, BH + h, cols], co[:, BH + h, cols], start=True, stop=True)
                        last = nc.tensor.matmul(quad(3, w, w)[:, h, :], co[:, BH + h, cols], co[:, h, cols], start=True, stop=True)
                    last.then_inc(dl["kk"], 1)
                    for h in range(BH):
                        for b, c in ((4, BH + h), (5, 2 * BH + h)):
                            if w == P:
                                last = nc.tensor.transpose(quad(b)[:, h, :], co[:, c, cols], ident)
                            else:
                                last = nc.tensor.matmul(quad(b)[0:w, h, :], co[:, c, cols], ident, start=True, stop=True)
                    last.then_inc(dl["tok"], 1)
                for n in group:
                    w, s = TILES[n][1], n % 2
                    pe.wait_ge(dl["x0"], n + 1)
                    if n:
                        pe.wait_ge(dl["xi"], n)
                    for h in range(BH):
                        if w == P:
                            last = nc.tensor.transpose(quad(7)[:, h, :], xt[s][:, h, :], ident)
                        else:
                            last = nc.tensor.matmul(quad(7, w, w)[:, h, :], xt[s][0:w, h, 0:w], ident[0:w, 0:w], start=True, stop=True)
                    last.then_inc(dl["x0t"], 1)
                pe.wait_ge(dl["front"], group[-1] + 1)
                for lv, n in level_steps(group):
                    w, s, q = TILES[n][1], n % 2, step_no[lv, n]
                    pe.wait_ge(dl["ml"], q + 1)
                    if lv == 1:
                        pe.wait_ge(dl["xi"], n + 1)
                    else:
                        pe.wait_ge(dl["xu"], step_no[lv - 1, n] + 1)
                    for h in range(BH):
                        last = nc.tensor.matmul(quad(s, w, w)[:, h, :], ml[s][0:w, h, 0:w], xi[s][0:w, h, 0:w], start=True, stop=True)
                    last.then_inc(dl["y"], 1)
                    if n != group[-1]:
                        continue
                    for m in group:
                        s, q = m % 2, step_no[lv, m]
                        pe.wait_ge(dl["yc"], q + 1)
                        for h in range(BH):
                            if lv < levels(m) - 1:
                                nc.tensor.matmul(quad(2 + s, w, w)[:, h, :], xt[s][0:w, h, 0:w], yv[s][0:w, h, 0:w], start=True, stop=True)
                            last = nc.tensor.matmul(quad(4 + s, w, w)[:, h, :], yv[s][0:w, h, 0:w], xt[s][0:w, h, 0:w], start=True, stop=True)
                        last.then_inc(dl["xy"], 1)
                for n in group:
                    w, s = TILES[n][1], n % 2
                    pe.wait_ge(dl["xu"], step_no[levels(n) - 1, n] + 1)
                    if n:
                        pe.wait_ge(dl["uwc"], n)
                    for h in range(BH):
                        if n < NT - 1:
                            nc.tensor.matmul(quad(6)[:, h, :], xt[s][:, h, :], vb[s][:, h, :], start=True, stop=True)
                        else:
                            nc.tensor.matmul(quad(6, w)[:, h, :], vb[s][0:w, h, :], xt[s][0:w, h, 0:w], start=True, stop=True)
                        last = nc.tensor.matmul(quad(7, w)[:, h, :], kbg[s][0:w, h, :], xt[s][0:w, h, 0:w], start=True, stop=True)
                    last.then_inc(dl["uw"], 1)
                if group[0] < NT - 1:
                    for n in group:
                        s = n % 2
                        pe.wait_ge(dl["uwc"], n + 1)
                        if n:
                            pe.wait_ge(dl["s"], n)
                            for h in range(BH):
                                last = nc.tensor.matmul(quad(0)[:, h, :], wt[s][:, h, :], s_cur[:, h, :], start=True, stop=True)
                            last.then_inc(dl["ws"], 1)
                            pe.wait_ge(dl["vn"], n)
                            pe.wait_ge(dl["o"], n)
                        vn = ml[s] if n else uu[s]
                        for h in range(BH):
                            if n:
                                nc.tensor.matmul(quad(1)[:, h, :], qd[s][:, h, :], s_cur[:, h, :], start=True, stop=False)
                            nc.tensor.matmul(quad(1)[:, h, :], it[s][:, h, :], vn[:, h, :], start=n == 0, stop=True)
                            last = nc.tensor.matmul(quad(2)[:, h, :], kd[s][:, h, :], vn[:, h, :], start=True, stop=True)
                        last.then_inc(dl["os"], 1)
                else:
                    pe_delta_sample(pe)
                for n in group:
                    w, s = TILES[n][1], n % 2
                    pe.wait_ge(dl["og"], n + 1)
                    if n:
                        pe.wait_ge(dl["cat"], n)
                    for h in range(BH):
                        last = nc.tensor.transpose(quad(3, w)[:, h, :], yv[s][0:w, h, :], ident[0:w, 0:w])
                    last.then_inc(dl["ot"], 1)

        def pe_delta_sample(pe):
            w, s = NB * NL, 0
            pe.wait_ge(dl["uwc"], NT)
            pe.wait_ge(S_("states_in"), 16)
            for h in range(BH):
                for b in range(NB):
                    c = slice(b * NL, (b + 1) * NL)
                    nc.tensor.matmul(quad(0, w)[:, h, c], ss0[:, b, h, :], wt[s][:, h, c], start=True, stop=True)
                    last = nc.tensor.matmul(quad(1, w)[:, h, c], ss0[:, b, h, :], qd[s][:, h, c], start=True, stop=True)
            last.then_inc(dl["s_pe"], 1)
            pe.wait_ge(dl["s_dve"], 1)
            for h in range(BH):
                last = nc.tensor.matmul(quad(2)[0:w, h, :], vnt[:, 0, h, :], ident, start=True, stop=True)
            last.then_inc(dl["s_pe"], 1)
            pe.wait_ge(dl["s_act"], 2)
            for h in range(BH):
                last = nc.tensor.matmul(quad(3, w)[:, h, :], ml[s][0:w, h, :], it[s][0:w, h, 0:w], start=True, stop=True)
            last.then_inc(dl["s_pe"], 1)
            pe.wait_ge(dl["s_dve"], 2)
            for h in range(BH):
                last = nc.tensor.matmul(quad(4)[0:w, h, :], vnt[:, 2, h, :], ident, start=True, stop=True)
            last.then_inc(dl["s_pe"], 1)
            for h in range(BH):
                pe.wait_ge(dl["vm"], h + 1)
                if h:
                    pe.wait_ge(dl["su"], h)
                for b2 in range(2):
                    last = nc.tensor.matmul(quad(6 + b2), kd[s][0:w, h, :], vm[0:w, 4 * b2:4 * b2 + 4, :], start=True, stop=True)
                last.then_inc(dl["st"], 1)

        def act_delta(act, chain):
            act.wait_ge(l2_done, 2 * BH + 1)
            for group in GROUPS:
                for n in group:
                    w, s = TILES[n][1], n % 2
                    act.wait_ge(dl["rows"], n + 1)
                    nc.scalar.activation(eg[s][:, :, 0:w], quad(0, w), ACT.Exp).then_inc(dl["eg"], 1)
                    act.wait_ge(dl["gd"], n + 1)
                    nc.scalar.activation(gcol[0:w, s, 1:3, :], gcol[0:w, s, 1:3, :], ACT.Exp).then_inc(dl["sc"], 1)
                    act.wait_ge(dl["dt"], n + 1)
                    nc.scalar.activation(sub(lt[s], w), sub(lt[s], w), ACT.Exp).then_inc(dl["dec"], 1)
                for n in group:
                    w, s = TILES[n][1], n % 2
                    act.wait_ge(dl["x0t"], n + 1)
                    nc.scalar.activation(sub(xi[s], w), quad(7, w, w), ACT.Copy).then_inc(dl["xi"], 1)
                for n in group:
                    copy_cache(act, 24 + n)
                for lv, n in level_steps(group):
                    w, s, q = TILES[n][1], n % 2, step_no[lv, n]
                    act.wait_ge(dl["y"], q + 1)
                    nc.scalar.activation(sub(yv[s], w), quad(s, w, w), ACT.Copy).then_inc(dl["yc"], 1)
                for n in group:
                    w, s = TILES[n][1], n % 2
                    act.wait_ge(dl["uw"], n + 1)
                    if n < NT - 1:
                        chain.mark(nc.scalar.activation(uu[s][:], quad(6), ACT.Copy))
                    else:
                        chain.mark(nc.scalar.activation(uu[s][:, :, 0:w], quad(6, w), ACT.Copy))
                    chain.link(nc.scalar.activation(wt[s][:, :, 0:w], quad(7, w), ACT.Copy))
                    act.sem_inc(dl["uwc"], 1)
                if group[0] < NT - 1:
                    for n in group:
                        act.wait_ge(dl["os"], n + 1)
                        nc.scalar.activation(yv[n % 2][:], quad(1), ACT.Copy).then_inc(dl["o"], 1)
                else:
                    w, s = NB * NL, 0
                    act.wait_ge(dl["s_pe"], 1)
                    nc.scalar.activation(vnt[:, 1], quad(1, w), ACT.Copy).then_inc(dl["s_act"], 1)
                    act.wait_ge(dl["s_pe"], 2)
                    nc.scalar.activation(ml[s][0:w], quad(2)[0:w], ACT.Copy).then_inc(dl["s_act"], 1)
                    act.wait_ge(dl["s_pe"], 4)
                    nc.scalar.activation(yv[s][0:w], quad(4)[0:w], ACT.Copy).then_inc(dl["o"], 1)
                for n in group:
                    act.wait_ge(dl["ovar"], n + 1)
                    nc.scalar.activation(ost[:, n % 2, 1, :], ost[:, n % 2, 1, :], ACT.Sqrt).then_inc(dl["ort"], 1)
                for n in group:
                    t0, w = TILES[n]
                    act.wait_ge(dl["ot"], n + 1)
                    nc.scalar.activation(cat[:, PAIRS:, t0:t0 + w], quad(3, w), ACT.Copy).then_inc(dl["cat"], 1)

        def dve_delta(dve, chain):
            tt = nc.vector.tensor_tensor
            chain.link(nc.vector.memset(ost[:], 1.0))
            for group in GROUPS:
                for n in group:
                    w, s = TILES[n][1], n % 2
                    chain.mark(tt(out=sub(lt[s], w), in0=bc(cum(n)[0:w, 0:w], 1, BH), in1=bc(gate_g[0:w, n, :], 2, w), op=ALU.mult))
                    chain.link(tt(out=sub(it[s], w), in0=bc(ident[0:w, 0:w], 1, BH), in1=bc(beta[0:w, n, :], 2, w), op=ALU.mult))
                    dve.sem_inc(dl["gg"], 1)
                for n in group:
                    (t0, w), s = TILES[n], n % 2
                    dve.wait_ge(dl["rows"], n + 1)
                    chain.link(nc.vector.tensor_copy(gcol[0:w, s, 0, :], bank[6][0:w, 0:4]))
                    chain.mark(nc.vector.tensor_copy(gcol[0:w, s, 2, :], bank[6][0:w, 0:4]))
                    chain.link(tt(out=gcol[0:w, s, 1, :], in0=bank[6][0:w, 4:8], in1=gcol[0:w, s, 0, :], op=ALU.subtract))
                    dve.sem_inc(dl["gd"], 1)
                    dve.wait_ge(dl["eg"], n + 1)
                    for h in range(BH):
                        chain.mark(nc.vector.tensor_scalar(lt[s][0:w, h, 0:w], quad(0, w, w)[:, h, :], gcol[0:w, s, 0, h:h + 1],
                                                           0.0, ALU.subtract, ALU.min))
                    chain.join()
                    dve.sem_inc(dl["dt"], 1)
                    chain.mark(tt(out=qd[s][:, :, 0:w], in0=co[:, 0:BH, t0:t0 + w], in1=eg[s][:, :, 0:w], op=ALU.mult))
                    dve.wait_ge(dl["sc"], n + 1)
                    chain.link(tt(out=gcol[0:w, s, 3, :], in0=beta[0:w, n, :], in1=gcol[0:w, s, 2, :], op=ALU.mult))
                    dve.wait_ge(dl["dec"], n + 1)
                    dve.wait_ge(dl["kk"], n + 1)
                    chain.link(tt(out=sub(it[s], w), in0=quad(3, w, w), in1=sub(lt[s], w), op=ALU.mult))
                    chain.mark(tt(out=sub(it[s], w), in0=sub(it[s], w), in1=bc(cum(n)[0:w, 0:w], 1, BH), op=ALU.mult))
                    chain.link(tt(out=sub(lt[s], w), in0=quad(2, w, w), in1=sub(lt[s], w), op=ALU.mult))
                    chain.link(tt(out=sub(lt[s], w), in0=sub(lt[s], w), in1=quad(1, w, w), op=ALU.mult))
                    chain.link(tt(out=sub(ml[s], w), in0=sub(lt[s], w), in1=bc(sq[0:w, LEVEL0, 0:w], 1, BH), op=ALU.mult))
                    chain.link(tt(out=sub(xt[s], w), in0=bc(ident[0:w, 0:w], 1, BH), in1=sub(ml[s], w), op=ALU.subtract))
                    dve.sem_inc(dl["x0"], 1)
                    dve.wait_ge(dl["tok"], n + 1)
                    chain.mark(tt(out=kd[s][0:w], in0=quad(4)[0:w], in1=bc(gcol[0:w, s, 1, :], 2, BD), op=ALU.mult))
                    chain.mark(tt(out=kbg[s][0:w], in0=quad(4)[0:w], in1=bc(gcol[0:w, s, 3, :], 2, BD), op=ALU.mult))
                    chain.link(tt(out=vb[s][0:w], in0=quad(5)[0:w], in1=bc(beta[0:w, n, :], 2, BD), op=ALU.mult))
                    dve.sem_inc(dl["front"], 1)
                for lv, n in level_steps(group):
                    w, s, q = TILES[n][1], n % 2, step_no[lv, n]
                    dve.wait_ge(dl["xy"], q + 1)
                    if lv < levels(n) - 1:
                        chain.mark(tt(out=sub(xi[s], w), in0=sub(xi[s], w), in1=quad(2 + s, w, w), op=ALU.subtract))
                    chain.link(tt(out=sub(xt[s], w), in0=sub(xt[s], w), in1=quad(4 + s, w, w), op=ALU.subtract))
                    dve.sem_inc(dl["xu"], 1)
                if group[0] < NT - 1:
                    for n in group:
                        s = n % 2
                        if n:
                            dve.wait_ge(dl["ws"], n)
                            tt(out=ml[s][:], in0=uu[s][:], in1=quad(0), op=ALU.subtract).then_inc(dl["vn"], 1)
                        dve.wait_ge(dl["os"], n + 1)
                        if n:
                            for h in range(BH):
                                chain.mark(nc.vector.scalar_tensor_tensor(out=s_cur[:, h, :], in0=s_cur[:, h, :], scalar=eg[s][:, h, P - 1:P],
                                                                          in1=quad(2)[:, h, :], op0=ALU.mult, op1=ALU.add))
                            chain.join()
                        else:
                            chain.link(nc.vector.tensor_copy(s_cur[:], quad(2)))
                        dve.sem_inc(dl["s"], 1)
                else:
                    w, s = NB * NL, 0
                    dve.wait_ge(dl["s_pe"], 1)
                    tt(out=vnt[:, 0], in0=uu[s][:, :, 0:w], in1=quad(0, w), op=ALU.subtract).then_inc(dl["s_dve"], 1)
                    dve.wait_ge(dl["s_act"], 1)
                    dve.wait_ge(dl["s_pe"], 3)
                    tt(out=vnt[:, 2], in0=vnt[:, 1], in1=quad(3, w), op=ALU.add).then_inc(dl["s_dve"], 1)
                    for h in range(BH):
                        if h:
                            dve.wait_ge(dl["st"], h)
                        tt(out=vm[0:w], in0=bc(ml[s][0:w, h, :], 1, NB), in1=bc(sq[0:w, BLK_S, 0:w:NL], 2, BD), op=ALU.mult).then_inc(dl["vm"], 1)
                        chain.link(tt(out=ss0[:, :, h, :], in0=ss0[:, :, h, :], in1=bc(eg[s][:, h, NL - 1:w:NL], 2, BD), op=ALU.mult))
                        dve.wait_ge(dl["st"], h + 1)
                        for b2 in range(2):
                            chain.mark(tt(out=ss0[:, 4 * b2:4 * b2 + 4, h, :], in0=ss0[:, 4 * b2:4 * b2 + 4, h, :], in1=quad(6 + b2), op=ALU.add))
                        chain.join()
                        dve.sem_inc(dl["su"], 1)
                for n in group:
                    w, s = TILES[n][1], n % 2
                    dve.wait_ge(dl["o"], n + 1)
                    chain.link(tt(out=xi[s][0:w], in0=yv[s][0:w], in1=yv[s][0:w], op=ALU.mult))
                    chain.link(nc.vector.tensor_reduce(ost[0:w, s, 0, :], xi[s][0:w], axis=AX.X, op=ALU.add))
                    chain.link(nc.vector.tensor_scalar(ost[0:w, s, 1, :], ost[0:w, s, 0, :], 1.0 / BD, EPS, ALU.mult, ALU.add))
                    nc.vector.reciprocal(ost[0:w, s, 1, :], ost[0:w, s, 1, :]).then_inc(dl["ovar"], 1)
                for n in group:
                    w, s = TILES[n][1], n % 2
                    dve.wait_ge(dl["ort"], n + 1)
                    chain.link(tt(out=yv[s][0:w], in0=yv[s][0:w], in1=bc(ost[0:w, s, 1, :], 2, BD), op=ALU.mult))
                    tt(out=yv[s][0:w], in0=yv[s][0:w], in1=bz[0:w, n, :].rearrange("p (h e) -> p h e", h=BH), op=ALU.mult).then_inc(dl["og"], 1)

        def pool_mix(pool, chain):
            for group in GROUPS:
                for lv, n in level_steps(group):
                    w, s = TILES[n][1], n % 2
                    if lv == 1:
                        pool.wait_ge(dl["x0"], n + 1)
                    else:
                        pool.wait_ge(dl["y"], step_no[lv - 1, n] + 1)
                    nc.gpsimd.tensor_tensor(out=sub(ml[s], w), in0=sub(lt[s], w), in1=bc(sq[0:w, LEVEL0 + lv, 0:w], 1, BH),
                                            op=ALU.mult).then_inc(dl["ml"], 1)
            pool_sample(pool, chain)

        def sp_delta(sp):
            sp.wait_ge(l2_done, 2 * BH + 1)
            sp.dma_start(ss0[:], s0.rearrange("b h k v -> k (b h) v")).then_inc(S_("states_in"), 16)
            sp.wait_ge(dl["s"], NT - 1)
            sp.dma_start(s_p.rearrange("h k v -> k h v"), s_cur[:]).then_inc(S_("states_out"), 16)
            sp.wait_ge(dl["su"], BH)
            sp.dma_start(s_s.rearrange("b h k v -> k (b h) v"), ss0[:]).then_inc(S_("states_out"), 16)

        QROWS = NB * NL
        keys_in = [S_(f"cached_keys_in{s}") for s in range(2)]
        values_in = [S_(f"cached_values_in{s}") for s in range(2)]
        sa = {n: S_("sample_" + n) for n in "q kt0 kt1 kta ktv scores masked exp norm turned pt out os used".split()}

        def score_banks(b):
            return bank[2 + 4 * (b % 2)][0:QROWS, :], bank[3 + 4 * (b % 2)][0:QROWS, :]

        def sp_sample(sp):
            sp.wait_ge(S_("states_out"), 32)
            sp.wait_ge(dl["cat"], NT)
            for b in range(NB):
                s = b % 2
                for dst, cache, done in ((ks[s], kc, keys_in[s]), (vs[s], vc, values_in[s])):
                    if b >= 2 and cache is kc:
                        sp.wait_ge(sa["kt0"], PAIRS * (b - 1))
                        sp.wait_ge(sa["kt1"], PAIRS * (b - 1))
                    elif b >= 2:
                        sp.wait_ge(sa["used"], b - 1)
                    groups = cache[b].rearrange("(j g s) c -> j g s c", g=32, s=16)
                    for j in range(OLD_TILES):
                        sp.dma_start(dst[:, j, :], groups[j, :, 0:4, :]).then_inc(done, 16)
                    sp.dma_start(dst[:, OLD_TILES:, :],
                                 cache[b, PAST - NEW_TILES * P:PAST, :].rearrange("(j p) c -> p j c", p=P)).then_inc(done, 16)

        def pe_sample(pe):
            pe.wait_ge(dl["cat"], NT)
            pe.wait_ge(dl["su"], BH)

            def turn_keys(b):
                s = b % 2
                pe.wait_ge(keys_in[s], 16 * 4 * (b // 2 + 1))
                for p in range(PAIRS):
                    q = b * PAIRS + p
                    if q:
                        pe.wait_ge(sa["kta"], q)
                    for j in range(4):
                        last = nc.tensor.transpose(quad(0)[:, j, :], ks[s][:, j, p * P:(p + 1) * P], ident)
                    last.then_inc(sa["kt0"], 1)
                    if q:
                        pe.wait_ge(sa["ktv"], q)
                    for j in range(4, KTILES):
                        last = nc.tensor.transpose(quad(1)[:, j - 4, :], ks[s][:, j, p * P:(p + 1) * P], ident)
                    last.then_inc(sa["kt1"], 1)

            def scores(b):
                pe.wait_ge(sa["kta"], PAIRS * (b + 1))
                pe.wait_ge(sa["ktv"], PAIRS * (b + 1))
                if b >= 2:
                    pe.wait_ge(sa["masked"], b - 1)
                lo, hi = score_banks(b)
                for p in range(PAIRS):
                    nc.tensor.matmul(lo, qbd[:, b, p, :], kt[:, p, 0:512], start=p == 0, stop=p == PAIRS - 1)
                for p in range(PAIRS):
                    nc.tensor.matmul(hi[:, 0:CACHED - 512], qbd[:, b, p, :], kt[:, p, 512:CACHED], start=p == 0, stop=p == PAIRS - 1)
                for p in range(PAIRS):
                    last = nc.tensor.matmul(hi[:, CACHED - 512:CACHED - 512 + QROWS], qbd[:, b, p, :], qkt[:, PAIRS + p, SEQ:TOK],
                                            start=p == 0, stop=p == PAIRS - 1)
                last.then_inc(sa["scores"], 1)

            turn_keys(0)
            pe.wait_ge(sa["q"], 1)
            scores(0)
            for b in range(NB):
                s = b % 2
                if b + 1 < NB:
                    turn_keys(b + 1)
                    scores(b + 1)
                pe.wait_ge(sa["norm"], b + 1)
                if b:
                    pe.wait_ge(sa["pt"], b)
                pts_bank = bank[4][:, 0:(KTILES + 1) * QROWS].rearrange("p (j q) -> p j q", q=QROWS)
                for j in range(KTILES):
                    nc.tensor.transpose(pts_bank[:, j, :], sss[s][:, j * P:(j + 1) * P], ident[0:QROWS, 0:QROWS])
                nc.tensor.matmul(pts_bank[0:QROWS, KTILES, :], sss[s][:, CACHED:CACHED + QROWS], ident[0:QROWS, 0:QROWS],
                                 start=True, stop=True).then_inc(sa["turned"], 1)
                pe.wait_ge(sa["pt"], b + 1)
                pe.wait_ge(values_in[s], 16 * 4 * (b // 2 + 1))
                if b:
                    pe.wait_ge(sa["os"], b)
                for p in range(PAIRS):
                    out = bank[5][:, 8 * p:8 * p + 8]
                    for j in range(KTILES):
                        nc.tensor.matmul(out, vs[s][:, j, p * P:(p + 1) * P], pts[:, j, 8 * p:8 * p + 8], start=j == 0, stop=False)
                    last = nc.tensor.matmul(out, av[0:QROWS, NT - 1, p * P:(p + 1) * P], pts[0:QROWS, KTILES, 8 * p:8 * p + 8],
                                            start=False, stop=True)
                last.then_inc(sa["out"], 1)
                pe.wait_ge(sa["out"], b + 1)
                pe.sem_inc(sa["used"], 1)

        def dve_sample(dve, chain):
            chain.link(nc.vector.memset(qbd[:], 0.0))
            for h in range(AH):
                r = slice(AD * (h % 2), AD * (h % 2) + AD)
                chain.mark(nc.vector.tensor_copy(qbd[r, :, h // 2, h * NL:(h + 1) * NL],
                                                 qkt[r, h // 2, SEQ:TOK].rearrange("p (b l) -> p b l", b=NB)))
            chain.join()
            dve.sem_inc(sa["q"], 1)

            def keys(b):
                if b:
                    dve.wait_ge(sa["scores"], b)
                for p in range(PAIRS):
                    dve.wait_ge(sa["kt1"], b * PAIRS + p + 1)
                    nc.vector.tensor_copy(kt[:, p, 512:CACHED], bank[1][:, 0:CACHED - 512]).then_inc(sa["ktv"], 1)

            keys(0)
            for b in range(NB):
                s = b % 2
                if b + 1 < NB:
                    keys(b + 1)
                dve.wait_ge(sa["scores"], b + 1)
                if b >= 2:
                    dve.wait_ge(sa["turned"], b - 1)
                m = 512
                lo, hi = score_banks(b)
                parts = ((0, lo, lncs[:, 0:m]),
                         (m, hi[:, 0:CACHED - m], lncs[:, m:CACHED]),
                         (CACHED, hi[:, CACHED - m:CACHED - m + QROWS], lncs[:, CACHED + b * QROWS:CACHED + (b + 1) * QROWS]))
                for x, (c0, src, lnc) in enumerate(parts):
                    chain.mark(nc.vector.tensor_tensor_reduce(
                        out=sss[s][:, c0:c0 + src.shape[1]], in0=src, in1=lnc, scale=1.0, scalar=NEG, op0=ALU.add, op1=ALU.max,
                        accum_out=sstat[:, s, x:x + 1]))
                chain.join()
                nc.vector.tensor_reduce(sstat[:, s, 3:4], sstat[:, s, 0:3], axis=AX.X, op=ALU.max, negate=True).then_inc(sa["masked"], 1)
                dve.wait_ge(sa["exp"], b + 1)
                chain.link(nc.vector.reciprocal(sstat[:, s, 5:6], sstat[:, s, 4:5]))
                nc.vector.tensor_scalar(sss[s][:], sss[s][:], sstat[:, s, 5:6], None, ALU.mult).then_inc(sa["norm"], 1)

        def act_sample(act, chain):
            def keys(b):
                if b:
                    act.wait_ge(sa["scores"], b)
                for p in range(PAIRS):
                    act.wait_ge(sa["kt0"], b * PAIRS + p + 1)
                    nc.scalar.activation(kt[:, p, 0:512], bank[0][:], ACT.Copy).then_inc(sa["kta"], 1)

            keys(0)
            for b in range(NB):
                s = b % 2
                if b + 1 < NB:
                    keys(b + 1)
                act.wait_ge(sa["masked"], b + 1)
                nc.scalar.activation(sss[s][:], sss[s][:], ACT.Exp, bias=sstat[:, s, 3:4], accum_out=sstat[:, s, 4:5]).then_inc(sa["exp"], 1)
                if b < COPIES - 24 - NT:
                    copy_cache(act, 24 + NT + b)
                act.wait_ge(sa["turned"], b + 1)
                if b:
                    act.wait_ge(sa["out"], b)
                pts_bank = bank[4][:, 0:(KTILES + 1) * QROWS].rearrange("p (j q) -> p j q", q=QROWS)
                chain.mark(nc.scalar.activation(pts[:, 0:KTILES, :], pts_bank[:, 0:KTILES, :], ACT.Copy))
                chain.link(nc.scalar.activation(pts[0:QROWS, KTILES, :], pts_bank[0:QROWS, KTILES, :], ACT.Copy))
                act.sem_inc(sa["pt"], 1)
                act.wait_ge(sa["out"], b + 1)
                c = slice(SEQ + b * NL, SEQ + (b + 1) * NL)
                o4 = bank[5][:, 0:8 * PAIRS].rearrange("p (i q) -> p i q", q=8)
                chain.mark(nc.scalar.activation(cat[0:AD, 0:PAIRS, c], o4[0:AD, :, 0:NL], ACT.Copy))
                chain.link(nc.scalar.activation(cat[AD:P, 0:PAIRS, c], o4[AD:P, :, NL:2 * NL], ACT.Copy))
                act.sem_inc(sa["os"], 1)

        def pool_sample(pool, chain):
            pool_ffn(pool, chain)

        NW_OUT, NW_PQ = 4, 8
        NW2 = NW1 + NW_OUT
        NW3 = NW2 + NW_PQ
        ff = {n: S_("ffn_" + n) for n in (
            "cat_hi cat_lo x_in norm_in h_used pq pq_evac sub sub_evac sub_free "
            "top_exp top_expd picks picks_turned picks_t cols ones gate_mm gate_bank staged").split()}
        gate_out = [S_("gate_out0"), S_("gate_out1")]
        QUADS = GT // 4
        assert GB * QUADS % HOT == 0

        def sp_ffn(sp):
            sp.wait_ge(sa["used"], NB)
            for k in range(NW1, NW3):
                sp.wait_ge(w_hi_ready, k)
                sp.wait_ge(w_lo_ready, k)
                src = wout[k - NW1] if k < NW2 else wpq[k - NW2]
                sp.dma_start(w_raw[:], src).then_inc(w_in, 16)
                if k == NW1:
                    sp.wait_ge(ff["cat_hi"], 2)
                    sp.wait_ge(ff["cat_lo"], 2)
                    for t in range(NT):
                        x = x_p[t * P:(t + 1) * P, :] if t < NT - 1 else x_s
                        sp.dma_start(X[0:TILES[t][1], t, :], x).then_inc(ff["x_in"], 16)
                    sp.dma_start(nmix_b[:], nffn.partition_broadcast(P)).then_inc(ff["norm_in"], 16)
            sp.wait_ge(w_used, NW3)
            sp.dma_start(skt_s[:], skt).then_inc(ff["norm_in"], 16)
            sp.wait_ge(xs_ready, 2 * NT)
            for s in range(2):
                load_u(sp, 0, s)
            for t in range(NT):
                with sp.Fori(0, WINDOW[t]) as i:
                    for s in range(2):
                        feed_pre(sp, i + WINDOW0[t], s)
            with sp.Fori(0, GBLOCKS // GB) as i:
                for b in range(GB):
                    for s in range(2):
                        feed_pre(sp, i * GB + (GATE_X0 + b), s)
                    sp.wait_ge(ff["staged"], i * GB + (b + 1))
                    sp.dma_start(gates_dram[bass.ds(i * GB + b, 1)].rearrange("o p a t -> p (o a t)"), gst[b % 2][:]).then_inc(gate_out[b % 2], 16)
            for s in range(2):
                sp.wait_ge(gate_out[s], 16 * (GBLOCKS // 2) + 16)
                sp.wait_ge(act_out[s], 16 * (AHEAD // 2) + 16)
            sp_dense(sp)

        def pe_ffn(pe, product):
            pe.wait_ge(ff["cat_lo"], 2)
            pe.wait_ge(sa["os"], NB)
            uses = 0
            for k in range(NW1, NW2):
                pe.wait_ge(w_lo_ready, k + 1)
                for t in range(NT):
                    if uses >= 4:
                        pe.wait_ge(ff["h_used"], uses - 3)
                    tok = token_columns(t)
                    product(bank[2 + uses % 4][:, 0:WC],
                            [(cat_hi[:, c, tok], cat_lo[:, c, tok], w_hi[:, k % 2, c, :], w_lo[:, k % 2, c, :])
                             for c in range(CH)]).then_inc(proj_ready, 1)
                    uses += 1
                pe.wait_ge(proj_ready, READY1 + uses)
                pe.sem_inc(w_used, 1)
            for m in range(2 * NT):
                t0, w = TILES[m // 2]
                pe.wait_ge(xs_ready, NT + m // 2 + 1)
                if m >= 2:
                    pe.wait_ge(xn_lo_ready, 2 * NT + m - 1)
                for j in range(4):
                    c = 4 * (m % 2) + j
                    last = nc.tensor.transpose(quad(m % 2, w)[:, j, :], hs[0:w, (m // 2) % 2, c * P:(c + 1) * P], ident[0:w, 0:w])
                last.then_inc(xs_turned, 1)
            pe.wait_ge(xn_lo_ready, 4 * NT)
            pe.wait_ge(ff["h_used"], NW_OUT * NT)
            uses = 0
            for c in range(2 * PH):
                k = NW2 + c // 2
                pe.wait_ge(w_lo_ready, k + 1)
                wcols = slice((c % 2) * P, (c % 2) * P + P)
                for h in range(2):
                    if uses >= 4:
                        pe.wait_ge(ff["pq_evac"], uses - 3)
                    cols = slice(h * HALF, (h + 1) * HALF)
                    product(bank[2 + uses % 4][:, 0:HALF],
                            [(w_hi[:, k % 2, i, wcols], w_lo[:, k % 2, i, wcols], hn_hi[:, i, cols], hn_lo[:, i, cols])
                             for i in range(CH)]).then_inc(ff["pq"], 1)
                    uses += 1
                if c % 2:
                    pe.wait_ge(ff["pq"], uses)
                    pe.sem_inc(w_used, 1)
            pe.wait_ge(ff["pq_evac"], uses)
            pe.wait_ge(ff["norm_in"], 32)

            def half_scores(t):
                t0, w = TILES[t]
                for g in range(4):
                    q = 4 * t + g
                    if q >= 2:
                        pe.wait_ge(ff["sub_evac"], q - 1)
                    for j in range(4):
                        c = 4 * g + j
                        last = nc.tensor.matmul(quad(4 + g % 2)[0:w, j, :], qt[:, c, t0:t0 + w], skt_s[:, c % 2, :], start=True, stop=True)
                    last.then_inc(ff["sub"], 1)

            def turn_picks(t):
                w = TILES[t][1]
                pe.wait_ge(ff["picks"], t + 1)
                if t:
                    pe.wait_ge(ff["picks_t"], t)
                for j in range(3):
                    last = nc.tensor.transpose(bank[6][:, j * P:j * P + w], picks[0:w, j, :], ident[0:w, 0:w])
                last.then_inc(ff["picks_turned"], 1)

            half_scores(0)
            for t in range(NT):
                if t + 1 < NT:
                    half_scores(t + 1)
                for s in range(2):
                    pre(pe, product, WINDOW0[t], s)
                if t:
                    turn_picks(t - 1)
                with pe.Fori(1, WINDOW[t]) as i:
                    for s in range(2):
                        pre(pe, product, i + WINDOW0[t], s)
            turn_picks(NT - 1)
            with pe.Fori(0, GBLOCKS // GB) as i:
                for n in range(GB * QUADS):
                    b, k = n // QUADS, n % QUADS
                    pe.wait_ge(ff["ones"], i * (GB * QUADS) + n + 1)
                    pe.wait_ge(ff["gate_bank"], i * (GB * QUADS) + n + 1)
                    for j in range(4):
                        last = nc.tensor.matmul(quad(4 + n % 2)[:, j, :], one2[n % HOT][:, j, :], one1[n % HOT][:, j, :], start=True, stop=True)
                    last.then_inc(ff["gate_mm"], 1)
                    if k in PRE_AFTER:
                        half = PRE_AFTER.index(k)
                        pre(pe, product, i * GB + (GATE_X0 + b), half // 2, (half % 2,))
            pe_dense(pe, product)

        def act_ffn(act, chain):
            act.wait_ge(sa["used"], NB)
            for h in range(2):
                nc.scalar.activation(cat_hi[:, 4 * h:4 * h + 4, :], cat[:, 4 * h:4 * h + 4, :], ACT.Copy).then_inc(ff["cat_hi"], 1)

            def split_hi(k):
                act.wait_ge(w_in, 16 * (k + 1))
                act.wait_ge(w_used, k - 1)
                nc.scalar.activation(w_hi[:, k % 2], w_raw[:], ACT.Copy).then_inc(w_hi_ready, 1)

            for k in range(NW1, NW2 + 2):
                split_hi(k)
            for t, (t0, w) in enumerate(TILES):
                act.wait_ge(ff["h_used"], (NW_OUT - 1) * NT + t + 1)
                if t:
                    act.wait_ge(ssq_ready, NT + t)
                nc.scalar.activation(tmp1[0:w, :], X[0:w, t, :], ACT.Square, accum_out=stat[0:w, 2, t:t + 1]).then_inc(ssq_ready, 1)
            act.wait_ge(var_ready, 2)
            nc.scalar.activation(stat[:, 3, :], stat[:, 3, :], ACT.Sqrt).then_inc(rstd_ready, 1)
            for m in range(2 * NT):
                t0, w = TILES[m // 2]
                act.wait_ge(xs_turned, 2 * NT + m + 1)
                nc.scalar.activation(hn_hi[:, 4 * (m % 2):4 * (m % 2) + 4, t0:t0 + w], quad(m % 2, w), ACT.Copy).then_inc(xn_hi_ready, 1)
            uses = 0
            for c in range(2 * PH):
                for h in range(2):
                    act.wait_ge(ff["pq"], uses + 1)
                    nc.scalar.activation(qt[:, c, h * HALF:(h + 1) * HALF], bank[2 + uses % 4][:, 0:HALF], ACT.Copy).then_inc(ff["pq_evac"], 1)
                    uses += 1
                if c % 2 and NW2 + c // 2 + 2 < NW3:
                    split_hi(NW2 + c // 2 + 2)

            def scores_out(t):
                w = TILES[t][1]
                if t >= 2:
                    act.wait_ge(ff["sub_free"], t - 1)
                for g in range(4):
                    act.wait_ge(ff["sub"], 4 * t + g + 1)
                    nc.scalar.activation(sub_s[t % 2][0:w, 4 * g:4 * g + 4, :], quad(4 + g % 2)[0:w], ACT.Copy).then_inc(ff["sub_evac"], 1)
            act.sem_inc(dn["gelu"], 4)
            scores_out(0)
            split_u(act, 0, 0)
            for t, (t0, w) in enumerate(TILES):
                if t + 1 < NT:
                    scores_out(t + 1)
                with act.Fori(0, WINDOW[t]) as i:
                    for s in range(2):
                        gelu_ahead(act, i + WINDOW0[t], s)
                act.wait_ge(ff["top_exp"], t + 1)
                nc.scalar.activation(bv[0:w], bv[0:w], ACT.Exp).then_inc(ff["top_expd"], 1)
            act.sem_inc(ff["gate_bank"], 2)
            with act.Fori(0, GBLOCKS // GB) as i:
                for b in range(GB):
                    act.wait_ge(gate_out[b % 2], i * (8 * GB) + (16 * (b // 2) + 16))
                    for k in range(QUADS):
                        n = b * QUADS + k
                        act.wait_ge(ff["gate_mm"], i * (GB * QUADS) + (n + 1 + HOT))
                        nc.scalar.activation(gst[b % 2][:, :, 4 * k:4 * k + 4], quad(4 + n % 2).rearrange("p t a -> p a t"), ACT.Copy)\
                            .then_inc(ff["gate_bank"], 1)
                        if k in PRE_AFTER:
                            half = PRE_AFTER.index(k)
                            gelu_ahead(act, i * GB + (GATE_X0 + b), half // 2, (half % 2,))
                    act.wait_ge(ff["gate_bank"], i * (GB * QUADS) + (2 + (b + 1) * QUADS))
                    act.sem_inc(ff["staged"], 1)
            act_dense(act, chain)

        def dve_ffn(dve, chain):
            tt, ts = nc.vector.tensor_tensor, nc.vector.tensor_scalar
            for h in range(2):
                dve.wait_ge(ff["cat_hi"], h + 1)
                tt(out=cat_lo[:, 4 * h:4 * h + 4, :], in0=cat[:, 4 * h:4 * h + 4, :], in1=cat_hi[:, 4 * h:4 * h + 4, :].bitcast(F32),
                   op=ALU.subtract).then_inc(ff["cat_lo"], 1)
            dve.wait_ge(ff["x_in"], 16 * NT)
            uses = 0
            for k in range(NW_OUT):
                for t, (t0, w) in enumerate(TILES):
                    dve.wait_ge(proj_ready, READY1 + uses + 1)
                    x = X[0:w, t, k * WC:(k + 1) * WC]
                    tt(out=x, in0=x, in1=bank[2 + uses % 4][rows(t), 0:WC], op=ALU.add).then_inc(ff["h_used"], 1)
                    uses += 1
            dve.wait_ge(ssq_ready, 2 * NT)
            chain.link(ts(stat[:, 3, :], stat[:, 2, :], 1.0 / D, EPS, ALU.mult, ALU.add))
            nc.vector.reciprocal(stat[:, 3, :], stat[:, 3, :]).then_inc(var_ready, 1)
            dve.wait_ge(rstd_ready, 2)
            dve.wait_ge(ff["norm_in"], 16)

            def scale_tokens(t):
                w = TILES[t][1]
                if t >= 2:
                    dve.wait_ge(xs_turned, 2 * NT + 2 * (t - 1))
                nc.vector.scalar_tensor_tensor(out=hs[0:w, t % 2, :], in0=X[0:w, t, :], scalar=stat[0:w, 3, t:t + 1],
                                               in1=nmix_b[0:w, :], op0=ALU.mult, op1=ALU.mult).then_inc(xs_ready, 1)
            scale_tokens(0)
            for m in range(2 * NT):
                t0, w = TILES[m // 2]
                if m % 2 == 0 and m // 2 + 1 < NT:
                    scale_tokens(m // 2 + 1)
                hi = hn_hi[:, 4 * (m % 2):4 * (m % 2) + 4, t0:t0 + w].bitcast(F32)
                dve.wait_ge(xn_hi_ready, 2 * NT + m + 1)
                tt(out=hn_lo[:, 4 * (m % 2):4 * (m % 2) + 4, t0:t0 + w], in0=quad(m % 2, w), in1=hi, op=ALU.subtract).then_inc(xn_lo_ready, 1)

            def top16(w, vals, idx, src, n):
                for j in range(n):
                    chain.mark(nc.vector.max(vals(j)[:, 0:8], src(j)))
                chain.join()
                for j in range(n):
                    chain.mark(nc.vector.max_index(idx(j)[:, 0:8], vals(j)[:, 0:8], src(j)))
                chain.join()
                for j in range(n):
                    chain.mark(nc.vector.match_replace(src(j), vals(j)[:, 0:8], src(j), NEG))
                chain.join()
                for j in range(n):
                    chain.mark(nc.vector.max(vals(j)[:, 8:16], src(j)))
                chain.join()
                for j in range(n):
                    chain.mark(nc.vector.max_index(idx(j)[:, 8:16], vals(j)[:, 8:16], src(j)))
                chain.join()

            def keep_picks(t):
                t0, w = TILES[t]
                dve.wait_ge(ff["picks_turned"], t + 1)
                for j in range(3):
                    chain.mark(nc.vector.tensor_copy(picks_t[:, j, t0:t0 + w], bank[6][:, j * P:j * P + w]))
                chain.join()
                dve.sem_inc(ff["picks_t"], 1)

            for t, (t0, w) in enumerate(TILES):
                sub_t = sub_s[t % 2]
                dve.wait_ge(ff["sub_evac"], 4 * (t + 1))
                top16(w, lambda j: tv[0:w, j, :], lambda j: ti[0:w, j, :], lambda j: sub_t[0:w, j, :], 2 * PH)
                dve.sem_inc(ff["sub_free"], 1)
                if t:
                    keep_picks(t - 1)
                chain.mark(nc.vector.tensor_copy(tif[0:w], ti[0:w]))
                tv4 = tv[0:w].rearrange("p (h c) k -> p h c k", c=2)
                chain.link(tt(out=cand[0:w], in0=bc(tv4[:, :, 0, :], 3, TOPK), in1=bc(tv4[:, :, 1, :], 2, TOPK), op=ALU.add))
                top16(w, lambda j: bv[0:w, j, :], lambda j: bi[0:w, j, :],
                      lambda j: cand[0:w, j].rearrange("p a b -> p (a b)"), PH)
                chain.mark(nc.vector.tensor_copy(gsum[0:w, 0, :], bv[0:w, :, 0]))
                chain.mark(ts(bhl[0:w, 0], bi[0:w], 4, None, ALU.logical_shift_right))
                chain.link(ts(bhl[0:w, 1], bi[0:w], TOPK - 1, None, ALU.bitwise_and))
                tt(out=bv[0:w], in0=bv[0:w], in1=bc(gsum[0:w, 0, :], 2, TOPK), op=ALU.subtract).then_inc(ff["top_exp"], 1)
                chain.link(nc.vector.tensor_copy(bhlf[0:w], bhl[0:w]))
                tif4 = tif[0:w].rearrange("p (h c) k -> p h c k", c=2)
                eq3 = eq[0:w].rearrange("p h k a -> p (h k) a")
                for c in range(2):
                    chain.link(tt(out=eq3, in0=bc(bhlf[0:w, c].rearrange("p h k -> p (h k)"), 2, TOPK),
                                  in1=bc(asc[0:w, 0:TOPK], 1, PH * TOPK), op=ALU.is_equal))
                    chain.link(tt(out=eq[0:w], in0=eq[0:w], in1=bc(tif4[:, :, c, :], 2, TOPK), op=ALU.mult))
                    chain.link(nc.vector.tensor_reduce(picks[0:w, c, :], eq3, axis=AX.X, op=ALU.add))
                dve.wait_ge(ff["top_expd"], t + 1)
                chain.link(nc.vector.tensor_reduce(gsum[0:w, 0, :], bv[0:w], axis=AX.X, op=ALU.add))
                chain.link(nc.vector.reciprocal(gsum[0:w, 1, :], gsum[0:w, 0, :]))
                tt(out=picks[0:w, 2, :].rearrange("p (h k) -> p h k", k=TOPK), in0=bv[0:w], in1=bc(gsum[0:w, 1, :], 2, TOPK),
                   op=ALU.mult).then_inc(ff["picks"], 1)
            keep_picks(NT - 1)
            with dve.Fori(0, GBLOCKS // GB) as i:
                for b in range(GB):
                    nc.vector.tensor_copy(cols_s[:, b % 2], picks_t[:, :, bass.ds(i * (GB * GT) + b * GT, GT)]).then_inc(ff["cols"], 1)
                    dve.wait_ge(ff["cols"], i * GB + (b + 1))
                    for k in range(QUADS):
                        n = b * QUADS + k
                        dve.wait_ge(ff["gate_mm"], i * (GB * QUADS) + (n + 1))
                        tt(out=one2[n % HOT][:], in0=bc(asc, 1, 4), in1=bc(cols_s[:, b % 2, 1, 4 * k:4 * k + 4], 2, PK), op=ALU.is_equal)
                        for j in range(4):
                            c = 4 * k + j
                            last = ts(one1[n % HOT][:, j, :], asc, cols_s[:, b % 2, 0, c:c + 1], cols_s[:, b % 2, 2, c:c + 1], ALU.is_equal, ALU.mult)
                        last.then_inc(ff["ones"], 1)
            dve_dense(dve, chain)

        def pool_ffn(pool, chain):
            for k in range(NW1, NW3):
                pool.wait_ge(w_hi_ready, k + 1)
                pool.wait_ge(w_used, k - 1)
                nc.gpsimd.tensor_tensor(out=w_lo[:, k % 2], in0=w_raw[:], in1=w_hi[:, k % 2].bitcast(F32),
                                        op=ALU.subtract).then_inc(w_lo_ready, 1)
            pool.sem_inc(ff["gate_mm"], HOT)
            for s in range(2):
                pool.sem_inc(gate_out[s], 16)
                pool.sem_inc(act_out[s], 16)
            lo_u(pool, 0, 0)
            for t in range(NT):
                with pool.Fori(0, WINDOW[t]) as i:
                    for s in range(2):
                        lo_u(pool, i + (WINDOW0[t] + s), 1 - s)
            with pool.Fori(0, GBLOCKS // GB) as i:
                for b in range(GB):
                    for s in range(2):
                        lo_u(pool, i * GB + (GATE_X0 + b + s), 1 - s)
            pool_dense(pool, chain)

        READY1 = 9 * NT + 2 * 3 * BH

        dn = {n: S_("dense_" + n) for n in "uhi ulo vhi vlo pre gelu mul ahi alo acc outs yturn yadd".split()}
        u_in = [S_(f"u_in{s}") for s in range(2)]
        v_in = [S_(f"v_in{s}") for s in range(2)]
        g_in = [S_(f"g_in{s}") for s in range(2)]
        act_out = [S_(f"act_out{s}") for s in range(2)]
        act_in = [S_(f"act_in{s}") for s in range(2)]
        PAIRS_E = PK // 2
        ITERS = PAIRS_E // 2 - 1
        WINDOW = [5, 5, 5, 5, 4]
        WINDOW0 = [sum(WINDOW[:t]) for t in range(NT)]
        GATE_X0 = sum(WINDOW)
        PRE_AFTER = [QUADS // 4 * (n + 1) for n in range(4)]
        assert GATE_X0 + GBLOCKS == AHEAD // 2
        OUT_TILES = 2 * CH
        def one(e):
            return bass.ds(e, 1)

        def load_u(sp, x, s):
            sp.dma_start(u_raw[s][:], eu[one(2 * x + s)].rearrange("o p c n -> p (o c) n")).then_inc(u_in[s], 16)

        def feed_pre(sp, x, s):
            sp.wait_ge(dn["ulo"], 2 * x + (s + 1))
            load_u(sp, x + 1, s)
            sp.wait_ge(dn["gelu"], 4 * x + (2 * s + 6))
            sp.dma_start(acts_dram[one(2 * x + s)].rearrange("o p t -> p (o t)"), act_c[s][:]).then_inc(act_out[s], 16)

        def pre(pe, product, x, s, halves=(0, 1)):
            pe.wait_ge(dn["ulo"], 2 * x + (s + 1))
            pe.wait_ge(dn["gelu"], 4 * x + (2 * s + 2))
            for h in halves:
                cols = slice(h * HALF, (h + 1) * HALF)
                product(bank[2 * s + h][:, 0:HALF],
                        [(u_hi[s][:, c, :], u_lo[s][:, c, :], hn_hi[:, c, cols], hn_lo[:, c, cols]) for c in range(CH)])\
                    .then_inc(dn["pre"], 1)

        def split_u(act, x, s):
            act.wait_ge(u_in[s], 16 * x + 16)
            if not isinstance(x, int) or x:
                act.wait_ge(dn["pre"], 4 * x + (2 * s - 2))
            nc.scalar.activation(u_hi[s][:], u_raw[s][:], ACT.Copy).then_inc(dn["uhi"], 1)

        def split_next_u(act, x, s):
            split_u(act, x if s == 0 else x + 1, 1 - s)

        def gelu(act, x, s, halves=(0, 1)):
            for h in halves:
                act.wait_ge(dn["pre"], 4 * x + (2 * s + h + 1))
                nc.scalar.activation(act_c[s][:, h * HALF:(h + 1) * HALF], bank[2 * s + h][:, 0:HALF], ACT.Gelu).then_inc(dn["gelu"], 1)

        def gelu_ahead(act, x, s, halves=(0, 1)):
            if 0 in halves:
                split_next_u(act, x, s)
                act.wait_ge(act_out[s], 16 * x + 16)
            gelu(act, x, s, halves)

        def lo_u(pool, x, s):
            pool.wait_ge(dn["uhi"], 2 * x + (s + 1))
            nc.gpsimd.tensor_tensor(out=u_lo[s][:], in0=u_raw[s][:], in1=u_hi[s][:].bitcast(F32), op=ALU.subtract).then_inc(dn["ulo"], 1)

        def sp_dense(sp):
            def load_v(g, j):
                sp.dma_start(v_raw[j][:], ev[one(2 * g + j)].rearrange("o p n -> p (o n)")).then_inc(v_in[j], 16)

            def load_weights(g, s):
                sp.dma_start(gin[s][:], gates_dram[:, :, bass.ds(2 * g, 2), :].rearrange("b p a t -> p b (a t)")).then_inc(g_in[s], 16)
                sp.dma_start(act_l[s][:], acts_dram[one(g)].rearrange("o p t -> p (o t)")).then_inc(act_in[s], 16)

            load_weights(0, 0)
            for j in range(2):
                load_v(0, j)
            load_weights(1, 1)
            with sp.Fori(0, ITERS) as i:
                for s in range(2):
                    for j in range(2):
                        sp.wait_ge(dn["vlo"], i * 4 + (2 * s + j + 1))
                        load_v(i * 2 + (s + 1), j)
                    sp.wait_ge(dn["ulo"], i * 2 + (AHEAD + s + 1))
                    load_u(sp, i + (AHEAD // 2 + 1), s)
                    sp.wait_ge(dn["alo"], i * 4 + (2 * s + 2 + 4))
                    load_weights(i * 2 + (s + 2), s)
            for j in range(2):
                sp.wait_ge(dn["vlo"], PK - 3 + j)
                load_v(PAIRS_E - 1, j)
            for t, (t0, w) in enumerate(TILES):
                sp.wait_ge(dn["yadd"], 2 * (t + 1))
                dst = y_p[t0:t0 + w, :] if t < NT - 1 else y_s
                sp.dma_start(dst, X[0:w, t, :]).then_inc(out_done, 16)
            sp.wait_ge(out_done, 16 * (1 + 2 * COPIES + NT))
            sp.wait_ge(kv_out, 16 * (2 * (NT - 1) + 2 * NB))
            sp.wait_ge(S_("states_out"), 32)

        def pe_dense(pe, product):
            def outs(g, s):
                pe.wait_ge(dn["alo"], 2 * g + (2 + 4))
                pe.wait_ge(dn["vlo"], 2 * g + 2)
                for d in range(CH):
                    for h in range(2):
                        x = 2 * d + h
                        cols, dc = slice(h * HALF, (h + 1) * HALF), slice(d * P, (d + 1) * P)
                        pe.wait_ge(dn["acc"], OUT_TILES * g + (x + 1))
                        product(bank[4 + x % 4][:, 0:HALF],
                                [(v_hi[2 * s + j][:, dc], v_lo[2 * s + j][:, dc], a_hi[2 * s + j][:, cols], a_lo[2 * s + j][:, cols])
                                 for j in range(2)]).then_inc(dn["outs"], 1)

            pe.sem_inc(dn["outs"], OUT_TILES)
            pre(pe, product, AHEAD // 2, 0)
            pe.wait_ge(ff["gate_bank"], GBLOCKS * QUADS + 2)
            with pe.Fori(0, ITERS) as i:
                pre(pe, product, i + AHEAD // 2, 1)
                outs(i * 2, 0)
                pre(pe, product, i + (AHEAD // 2 + 1), 0)
                outs(i * 2 + 1, 1)
            pre(pe, product, PAIRS_E - 1, 1)
            outs(PAIRS_E - 2, 0)
            outs(PAIRS_E - 1, 1)
            pe.wait_ge(dn["acc"], 4 + OUT_TILES * PAIRS_E)
            for m in range(2 * NT):
                t0, w = TILES[m // 2]
                if m >= 2:
                    pe.wait_ge(dn["yadd"], m - 1)
                for j in range(4):
                    c = 4 * (m % 2) + j
                    if w == P:
                        last = nc.tensor.transpose(quad(m % 2)[:, j, :], y_t[:, c, t0:t0 + w], ident)
                    else:
                        last = nc.tensor.matmul(quad(m % 2)[0:w, j, :], y_t[:, c, t0:t0 + w], ident, start=True, stop=True)
                last.then_inc(dn["yturn"], 1)

        def act_dense(act, chain):
            def pair(g, s, x, more=True):
                if more:
                    split_next_u(act, x, s)
                if not isinstance(g, int) or g:
                    act.wait_ge(dn["outs"], OUT_TILES * (g + 0))
                for j in range(2):
                    act.wait_ge(v_in[j], 16 * g + 16)
                    nc.scalar.activation(v_hi[2 * s + j][:], v_raw[j][:], ACT.Copy).then_inc(dn["vhi"], 1)
                act.wait_ge(dn["mul"], 2 * g + 1)
                nc.scalar.activation(a_hi[2 * s][:], act_l[s][:], ACT.Copy).then_inc(dn["ahi"], 1)
                act.wait_ge(dn["alo"], 2 * g + 2)
                gelu(act, x, s)
                act.wait_ge(dn["mul"], 2 * g + 2)
                nc.scalar.activation(a_hi[2 * s + 1][:], act_c[s][:], ACT.Copy).then_inc(dn["ahi"], 1)

            for s in range(2):
                act.wait_ge(gate_out[s], 16 * (GBLOCKS // 2) + 16)
                act.wait_ge(act_out[s], 16 * (AHEAD // 2) + 16)
            with act.Fori(0, ITERS) as i:
                for s in range(2):
                    pair(i * 2 + s, s, i + AHEAD // 2)
            pair(PAIRS_E - 2, 0, PAIRS_E - 1)
            pair(PAIRS_E - 1, 1, PAIRS_E - 1, more=False)

        def dve_dense(dve, chain):
            tt = nc.vector.tensor_tensor

            def pair(g, s, x, i):
                dve.wait_ge(g_in[s], 16 * i + 16)
                dve.wait_ge(act_in[s], 16 * i + 16)
                for j, a in enumerate((act_l[s], act_c[s])):
                    if j:
                        dve.wait_ge(dn["gelu"], 4 * x + (2 * s + 6))
                    t3 = a[:].rearrange("p (b t) -> p b t", b=GBLOCKS)
                    tt(out=t3, in0=t3, in1=gin[s][:, :, j, :], op=ALU.mult).then_inc(dn["mul"], 1)
                    dve.wait_ge(dn["ahi"], 2 * g + (j + 1))
                    tt(out=a_lo[2 * s + j][:], in0=a[:], in1=a_hi[2 * s + j][:].bitcast(F32), op=ALU.subtract).then_inc(dn["alo"], 1)

            def accumulate(g):
                for x in range(OUT_TILES):
                    y = y_t[:, x // 2, (x % 2) * HALF:(x % 2 + 1) * HALF]
                    dve.wait_ge(dn["outs"], OUT_TILES * g + (OUT_TILES + x + 1))
                    tt(out=y, in0=y, in1=bank[4 + x % 4][:, 0:HALF], op=ALU.add).then_inc(dn["acc"], 1)

            dve.wait_ge(gate_out[1], 16 * (GBLOCKS // 2) + 16)
            chain.link(nc.vector.memset(y_t[:], 0.0))
            dve.sem_inc(dn["acc"], 4)
            dve.sem_inc(dn["alo"], 4)
            with dve.Fori(0, ITERS) as i:
                for s in range(2):
                    pair(i * 2 + s, s, i + AHEAD // 2, i)
                    accumulate(i * 2 + s)
            for s in range(2):
                pair(PAIRS_E - 2 + s, s, PAIRS_E - 1, ITERS)
                accumulate(PAIRS_E - 2 + s)
            dve.wait_ge(dn["acc"], 4 + OUT_TILES * PAIRS_E)
            for m in range(2 * NT):
                t0, w = TILES[m // 2]
                dve.wait_ge(dn["yturn"], m + 1)
                x = X[0:w, m // 2, 512 * (m % 2):512 * (m % 2 + 1)].rearrange("p (j d) -> p j d", j=4)
                tt(out=x, in0=x, in1=quad(m % 2)[0:w], op=ALU.add).then_inc(dn["yadd"], 1)

        def pool_dense(pool, chain):
            def pair(g, s):
                for j in range(2):
                    pool.wait_ge(dn["vhi"], 2 * g + (j + 1))
                    nc.gpsimd.tensor_tensor(out=v_lo[2 * s + j][:], in0=v_raw[j][:], in1=v_hi[2 * s + j][:].bitcast(F32),
                                            op=ALU.subtract).then_inc(dn["vlo"], 1)

            with pool.Fori(0, ITERS) as i:
                for s in range(2):
                    lo_u(pool, i + (AHEAD // 2 + s), 1 - s)
                    pair(i * 2 + s, s)
            lo_u(pool, PAIRS_E - 1, 1)
            for s in range(2):
                pair(PAIRS_E - 2 + s, s)
        def sp_windows(sp):
            for t, (t0, w) in enumerate(TILES):
                sp.wait_ge(rope_done, t + 1)
                sp.wait_ge(proj_evac, 5 * NT + t + 1)
                if t < NT - 1:
                    sp.dma_start(k_p[t0:t0 + w, :], qk[0:w, t, 512:1024]).then_inc(kv_out, 16)
                    sp.dma_start(v_p[t0:t0 + w, :], av[0:w, t, :]).then_inc(kv_out, 16)
                else:
                    for dst, src in ((k_s, qk[0:w, t, 512:1024]), (v_s, av[0:w, t, :])):
                        for b in range(NB):
                            sp.dma_start(dst[b, PAST - NL:PAST, :], src[b * NL:(b + 1) * NL]).then_inc(kv_out, 16)

        def sp_mix(sp):
            sp.wait_ge(cso_done, 3 * BH)
            sp.dma_start(conv_out, cso[:]).then_inc(out_done, 16)
            sp_delta(sp)
            sp_sample(sp)
            sp_ffn(sp)

        @block.sync
        def _(sp):
            for t in range(NT):
                src = x_p[t * P:(t + 1) * P, :] if t < NT - 1 else x_s
                sp.dma_start(X[0:TILES[t][1], t, :], src).then_inc(x_in[t], 16)
                if t == 0:
                    sp.dma_start(nmix_b[:], nmix.partition_broadcast(P)).then_inc(consts_in, 16)
                    sp.dma_start(sq[:], squares).then_inc(consts_in, 16)
                    sp.dma_start(wg8_raw[:], wg8).then_inc(consts_in, 16)
            for k in range(NW1):
                if k:
                    sp.wait_ge(w_hi_ready, k)
                    sp.wait_ge(w_lo_ready, k)
                sp.dma_start(w_raw[:], win[order1[k]]).then_inc(w_in, 16)
                if k == 9:
                    sp_windows(sp)
                if k == 0:
                    for dst, src in ((pos[:], pos_t), (qkw_b[:], qkw.partition_broadcast(P)), (convw_t[:], convw),
                                     (dnw_b[:], dnw.partition_broadcast(P)), (gconst[:, 0, :], alog.partition_broadcast(P)),
                                     (gconst[:, 1, :], dtb.partition_broadcast(P)), (cst[:], conv_state),
                                     (lncp[:], lnc_p), (lncs[:], lnc_s)):
                        sp.dma_start(dst, src).then_inc(small_in, 16)
            sp_mix(sp)

        @block.scalar
        def _(act):
            chain = Chain(act, act_chain)
            act.wait_ge(dve_chain, 1)
            for t, (t0, w) in enumerate(TILES):
                act.wait_ge(x_in[t], 16)
                chain.link(nc.scalar.activation(tmp1[0:w, :], X[0:w, t, :], ACT.Square, accum_out=stat[0:w, 0, t:t + 1]))
                act.sem_inc(ssq_ready, 1)
            act.wait_ge(var_ready, 1)
            nc.scalar.activation(stat[:, 1, :], stat[:, 1, :], ACT.Sqrt).then_inc(rstd_ready, 1)

            def split_hi(k):
                act.wait_ge(w_in, 16 * (k + 1))
                if k >= 2:
                    act.wait_ge(w_used, k - 1)
                if k >= 6:
                    copy_cache(act, k - 6)
                nc.scalar.activation(w_hi[:, k % 2], w_raw[:], ACT.Copy).then_inc(w_hi_ready, 1)

            split_hi(0)
            for m in range(2 * NT):
                t0, w = TILES[m // 2]
                act.wait_ge(xs_turned, m + 1)
                nc.scalar.activation(xn_hi[:, 4 * (m % 2):4 * (m % 2) + 4, t0:t0 + w], quad(m % 2, w), ACT.Copy)\
                    .then_inc(xn_hi_ready, 1)
            split_hi(1)
            uses = 0
            for k in range(8):
                for t, (t0, w) in enumerate(TILES):
                    act.wait_ge(proj_ready, uses + 1)
                    src = bank[2 + uses % 4][rows(t), 0:WC]
                    if k < 4:
                        dst = qk[0:w, t, k * WC:(k + 1) * WC]
                    elif k < 6:
                        dst = av[0:w, t, (k - 4) * WC:(k - 3) * WC]
                    else:
                        dst = bz[0:w, t, (k - 6) * WC:(k - 5) * WC]
                    nc.scalar.activation(dst, src, ACT.Silu if k >= 6 else ACT.Copy).then_inc(proj_evac, 1)
                    uses += 1
                split_hi(k + 2)
                if k == 4:
                    act.wait_ge(rope_var, NT)
                    nc.scalar.activation(ropes[:], ropes[:], ACT.Sqrt).then_inc(rope_rs, 1)
            for t, (t0, w) in enumerate(TILES):
                act.wait_ge(proj_ready, uses + 1)
                nc.scalar.activation(g8[0:w, t, :], bank[2 + uses % 4][rows(t), 0:8], ACT.Copy).then_inc(proj_evac, 1)
                uses += 1
            E0 = 3 + SEQ

            def silu(c):
                act.wait_ge(conv_done, c + 1)
                if c == 0:
                    act.wait_ge(qk_turned, 2 * NT)
                    act.wait_ge(kv_out, 16 * (2 * (NT - 1) + 2 * NB))
                nc.scalar.activation(co[:, c, :], cy[:, c % 2, :], ACT.Silu).then_inc(silu_done, 1)

            for c in range(3 * BH):
                if c == 0:
                    act.wait_ge(rope_done, NT)
                    act.wait_ge(qkt_ready, 2 * NT)
                if c >= 2:
                    act.wait_ge(conv_done, c - 1)
                    act.wait_ge(cso_done, c - 1)
                slot = ext[:, c % 2, :]
                act.wait_ge(proj_ready, uses + 1)
                nc.scalar.activation(slot[:, 3:3 + HALF], bank[2 + uses % 4][:, 0:HALF], ACT.Copy).then_inc(proj_evac, 1)
                uses += 1
                act.wait_ge(proj_ready, uses + 1)
                b = bank[2 + uses % 4]
                chain.mark(nc.scalar.activation(slot[:, 3 + HALF:3 + SEQ], b[:, 0:SEQ - HALF], ACT.Copy))
                nc.scalar.activation(slot[:, E0:E0 + NB * 7].rearrange("p (b j) -> p b j", b=NB)[:, :, 3:7],
                                     b[:, SEQ - HALF:HALF].rearrange("p (b j) -> p b j", b=NB), ACT.Copy)\
                    .then_inc(proj_evac, 1)
                chain.join()
                act.wait_ge(proj_evac, uses + 1)
                act.sem_inc(ext_ready, 1)
                uses += 1
                if c % 2 and 8 + c // 2 + 2 < NW1:
                    split_hi(8 + c // 2 + 2)
                if c:
                    silu(c - 1)
            silu(3 * BH - 1)
            act.wait_ge(gates_v, 1)
            chain.mark(nc.scalar.activation(beta[:], g8[:, :, 0:BH], ACT.Sigmoid))
            chain.mark(nc.scalar.activation(nega[:], gconst[:, 0, :], ACT.Exp))
            chain.link(nc.scalar.activation(gl[:], gl[:], ACT.Exp, scale=-1.0))
            act.sem_inc(gates_e, 1)
            act.wait_ge(gates_v, 2)
            chain.link(nc.scalar.activation(gl[:], gl[:], ACT.Ln))
            act.sem_inc(gates_e, 1)
            act.wait_ge(l2_inv, 1)
            chain.mark(nc.scalar.activation(l2r[:, 0:BH, :], l2r[:, 0:BH, :], ACT.Sqrt, scale=1.0 / BD))
            chain.link(nc.scalar.activation(l2r[:, BH:, :], l2r[:, BH:, :], ACT.Sqrt))
            act.sem_inc(l2_rt, 1)
            act_attend(act, chain)
            act_delta(act, chain)
            act_sample(act, chain)
            act_ffn(act, chain)

        @block.vector
        def _(dve):
            chain = Chain(dve, dve_chain)
            chain.mark(nc.vector.memset(stat[:], 1.0))
            chain.mark(nc.vector.memset(ropes[:], 1.0))
            chain.mark(nc.vector.memset(g8[:], 0.0))
            chain.mark(nc.vector.memset(l2r[:], 1.0))
            dve.wait_ge(ssq_ready, NT)
            chain.link(nc.vector.tensor_scalar(stat[:, 1, :], stat[:, 0, :], 1.0 / D, EPS, ALU.mult, ALU.add))
            nc.vector.reciprocal(stat[:, 1, :], stat[:, 1, :]).then_inc(var_ready, 1)
            dve.wait_ge(rstd_ready, 1)
            dve.wait_ge(consts_in, 16 * NCONST)

            def scale_tokens(t):
                t0, w = TILES[t]
                if t >= 2:
                    dve.wait_ge(xs_turned, 2 * (t - 1))
                nc.vector.scalar_tensor_tensor(out=xs[0:w, t % 2, :], in0=X[0:w, t, :], scalar=stat[0:w, 1, t:t + 1],
                                               in1=nmix_b[0:w, :], op0=ALU.mult, op1=ALU.mult).then_inc(xs_ready, 1)
            scale_tokens(0)
            for m in range(2 * NT):
                t0, w = TILES[m // 2]
                if m % 2 == 0 and m // 2 + 1 < NT:
                    scale_tokens(m // 2 + 1)
                hi = xn_hi[:, 4 * (m % 2):4 * (m % 2) + 4, t0:t0 + w].bitcast(F32)
                dve.wait_ge(xn_hi_ready, m + 1)
                nc.vector.tensor_tensor(out=xn_lo[:, 4 * (m % 2):4 * (m % 2) + 4, t0:t0 + w], in0=quad(m % 2, w),
                                        in1=hi, op=ALU.subtract).then_inc(xn_lo_ready, 1)
            dve.wait_ge(small_in, 16 * 9)
            for j in range(2):
                chain.mark(nc.vector.tensor_tensor(out=cw[:, :, j, :], in0=pos[:, 0], in1=bc(qkw_b[:, j, 0, :], 1, NT), op=ALU.mult))
                chain.mark(nc.vector.tensor_tensor(out=sw[:, :, j, :], in0=pos[:, 1], in1=bc(qkw_b[:, j, 1, :], 1, NT), op=ALU.mult))
            chain.join()
            for t, (t0, w) in enumerate(TILES):
                dve.wait_ge(proj_evac, 3 * NT + t + 1)
                chain.link(nc.vector.tensor_tensor(out=tmp1[0:w, :], in0=qk[0:w, t, :], in1=qk[0:w, t, :], op=ALU.mult))
                chain.link(nc.vector.tensor_reduce(ropes[0:w, t, :], tmp1[0:w, :].rearrange("p (h e) -> p h e", e=AD),
                                                   axis=AX.X, op=ALU.add))
                chain.link(nc.vector.tensor_scalar(ropes[0:w, t, :], ropes[0:w, t, :], 1.0 / AD, EPS, ALU.mult, ALU.add))
                nc.vector.reciprocal(ropes[0:w, t, :], ropes[0:w, t, :]).then_inc(rope_var, 1)
            dve.wait_ge(rope_rs, 1)
            chain.link(nc.vector.tensor_scalar(ropes[:, :, 0:8], ropes[:, :, 0:8], AD ** -0.5, None, ALU.mult))
            for t, (t0, w) in enumerate(TILES):
                q4 = qk[0:w, t, :].rearrange("p (j h e) -> p j h e", j=2, e=AD)
                q3 = qk[0:w, t, :].rearrange("p (h e) -> p h e", e=AD)
                t4 = tmp1[0:w, :].rearrange("p (j h e) -> p j h e", j=2, e=AD)
                u4 = tmp2[0:w, :].rearrange("p (j h e) -> p j h e", j=2, e=AD)
                chain.link(nc.vector.tensor_tensor(out=q3, in0=q3, in1=bc(ropes[0:w, t, :], 2, AD), op=ALU.mult))
                H = AD // 2
                chain.mark(nc.vector.tensor_tensor(out=t4, in0=q4, in1=bc(cw[0:w, t], 2, AH), op=ALU.mult))
                chain.mark(nc.vector.tensor_tensor(out=u4[:, :, :, 0:H], in0=q4[:, :, :, H:AD], in1=bc(sw[0:w, t, :, 0:H], 2, AH), op=ALU.mult))
                chain.link(nc.vector.tensor_tensor(out=u4[:, :, :, H:AD], in0=q4[:, :, :, 0:H], in1=bc(sw[0:w, t, :, H:AD], 2, AH), op=ALU.mult))
                nc.vector.tensor_tensor(out=qk[0:w, t, :], in0=tmp1[0:w, :], in1=tmp2[0:w, :], op=ALU.add).then_inc(rope_done, 1)
                if t < NT - 1:
                    dve.wait_ge(rope_done, t + 1)
            for m in range(2 * NT):
                t0, w = TILES[m // 2]
                dve.wait_ge(qk_turned, m + 1)
                nc.vector.tensor_copy(qkt[:, 4 * (m % 2):4 * (m % 2) + 4, t0:t0 + w], quad(m % 2, w)).then_inc(qkt_ready, 1)
            dve.wait_ge(proj_evac, 8 * NT)
            bz4 = bz[:, 0:NT - 1, :].rearrange("p t (h e) -> p (t h) e", e=BD)
            chain.mark(nc.vector.tensor_tensor(out=bz4, in0=bz4, in1=bc(dnw_b[:], 1, (NT - 1) * BH), op=ALU.mult))
            bz1 = bz[0:NB * NL, NT - 1, :].rearrange("p (h e) -> p h e", e=BD)
            chain.mark(nc.vector.tensor_tensor(out=bz1, in0=bz1, in1=bc(dnw_b[0:NB * NL], 1, BH), op=ALU.mult))
            dve.wait_ge(qkt_ready, 2 * NT)
            E0 = 3 + SEQ
            for s in range(2):
                chain.link(nc.vector.memset(ext[:, s, 0:3], 0.0))
            for c in range(3 * BH):
                dve.wait_ge(ext_ready, c + 1)
                dve.wait_ge(ext_state, c + 1)
                if c >= 2:
                    dve.wait_ge(silu_done, c - 1)
                slot = ext[:, c % 2, :]
                es = slot[:, E0:E0 + NB * 7].rearrange("p (b j) -> p b j", b=NB)
                yp_, ys_ = cy[:, c % 2, 0:SEQ], cy[:, c % 2, SEQ:TOK].rearrange("p (b j) -> p b j", b=NB)
                chain.mark(nc.vector.tensor_scalar(yp_, slot[:, 0:SEQ], convw_t[:, c, 0:1], None, ALU.mult))
                chain.link(nc.vector.tensor_scalar(ys_, es[:, :, 0:NL], convw_t[:, c, 0:1], None, ALU.mult))
                for j in range(1, CONV):
                    chain.mark(nc.vector.scalar_tensor_tensor(out=yp_, in0=slot[:, j:j + SEQ], scalar=convw_t[:, c, j:j + 1],
                                                              in1=yp_, op0=ALU.mult, op1=ALU.add))
                    chain.link(nc.vector.scalar_tensor_tensor(out=ys_, in0=es[:, :, j:j + NL], scalar=convw_t[:, c, j:j + 1],
                                                              in1=ys_, op0=ALU.mult, op1=ALU.add))
                dve.sem_inc(conv_done, 1)
            dve.wait_ge(proj_evac, 9 * NT)
            chain.link(nc.vector.tensor_tensor(out=gz[:], in0=g8[:, :, BH:2 * BH], in1=bc(gconst[:, 1, :], 1, NT), op=ALU.add))
            chain.link(nc.vector.scalar_tensor_tensor(out=gl[:], in0=gz[:], scalar=-1.0, in1=gz[:], op0=ALU.mult, op1=ALU.max))
            dve.sem_inc(gates_v, 1)
            chain.mark(nc.vector.tensor_scalar(gz[:], gz[:], 0.0, None, ALU.max))
            dve.wait_ge(gates_e, 1)
            chain.link(nc.vector.tensor_scalar(gl[:], gl[:], 1.0, None, ALU.add))
            dve.sem_inc(gates_v, 1)
            dve.wait_ge(gates_e, 2)
            chain.link(nc.vector.tensor_tensor(out=gl[:], in0=gl[:], in1=gz[:], op=ALU.add))
            chain.link(nc.vector.scalar_tensor_tensor(out=gate_g[:], in0=gl[:], scalar=-1.0, in1=bc(nega[:], 1, NT), op0=ALU.mult, op1=ALU.mult))
            dve.sem_inc(gates_v, 1)
            dve.wait_ge(l2_sum, 1)
            sums = bank[0][:, 0:2 * BH * NT].rearrange("p (c t) -> p c t", t=NT)
            chain.mark(nc.vector.tensor_scalar(l2r[:, :, 0:NT - 1], sums[:, :, 0:NT - 1], EPS, None, ALU.add))
            chain.link(nc.vector.tensor_scalar(l2r[0:NB * NL, :, NT - 1], sums[0:NB * NL, :, NT - 1], EPS, None, ALU.add))
            nc.vector.reciprocal(l2r[:], l2r[:]).then_inc(l2_inv, 1)
            for c in range(2 * BH):
                dve.wait_ge(l2_rows, c + 1)
                nc.vector.tensor_tensor(out=co[:, c, 0:SEQ], in0=co[:, c, 0:SEQ], in1=bank[L2_BANKS[c % 4]][:], op=ALU.mult).then_inc(l2_done, 1)
            rows_s = bank[4][:, 0:2 * BH * NB * NL].rearrange("p (c t) -> p c t", t=NB * NL)
            nc.vector.tensor_tensor(out=co[:, 0:2 * BH, SEQ:TOK], in0=co[:, 0:2 * BH, SEQ:TOK], in1=rows_s, op=ALU.mult).then_inc(l2_done, 1)
            dve_attend(dve, chain)
            dve_delta(dve, chain)
            dve_sample(dve, chain)
            dve_ffn(dve, chain)

        @block.gpsimd
        def _(pool):
            chain = Chain(pool, pool_chain)

            def split_lo(k):
                pool.wait_ge(w_hi_ready, k + 1)
                if k >= 2:
                    pool.wait_ge(w_used, k - 1)
                nc.gpsimd.tensor_tensor(out=w_lo[:, k % 2], in0=w_raw[:], in1=w_hi[:, k % 2].bitcast(F32),
                                        op=ALU.subtract).then_inc(w_lo_ready, 1)
            pool.wait_ge(consts_in, 16 * NCONST)
            chain.link(nc.gpsimd.tensor_copy(wg8_hi[:], wg8_raw[:]))
            nc.gpsimd.tensor_tensor(out=wg8_lo[:], in0=wg8_raw[:], in1=wg8_hi[:].bitcast(F32), op=ALU.subtract).then_inc(g8_split, 1)
            split_lo(0)
            split_lo(1)
            for k in range(8):
                split_lo(k + 2)
            pool.wait_ge(small_in, 16 * 9)
            pool.wait_ge(rope_done, NT)
            E0 = 3 + SEQ
            for c in range(3 * BH):
                slot = ext[:, c % 2, :]
                es = slot[:, E0:E0 + NB * 7].rearrange("p (b j) -> p b j", b=NB)
                if c >= 2:
                    pool.wait_ge(conv_done, c - 1)
                nc.gpsimd.tensor_copy(es[:, :, 0:3], cst[:, c]).then_inc(ext_state, 1)
                pool.wait_ge(ext_ready, c + 1)
                chain.mark(nc.gpsimd.tensor_copy(cso[:, c, 0:3], slot[:, SEQ:SEQ + 3]))
                chain.link(nc.gpsimd.tensor_copy(cso[:, c, 3:27].rearrange("p (b j) -> p b j", b=NB), es[:, :, 4:7]))
                pool.sem_inc(cso_done, 1)
                if 2 <= c < 2 + 2 * BH:
                    pool.wait_ge(silu_done, c - 1)
                    nc.gpsimd.tensor_tensor(out=l2s[:, c - 2, :], in0=co[:, c - 2, :], in1=co[:, c - 2, :], op=ALU.mult).then_inc(l2_sq, 1)
                if c % 2 and 8 + c // 2 + 2 < NW1:
                    split_lo(8 + c // 2 + 2)
            pool_mix(pool, chain)

        @block.tensor
        def _(pe):
            def product(out, pairs):
                n = len(pairs)
                for i, (ah, al, bh, bl) in enumerate(pairs):
                    nc.tensor.matmul(out, ah, bh, start=i == 0, stop=False)
                    nc.tensor.matmul(out, ah, bl, start=False, stop=False)
                    last = nc.tensor.matmul(out, al, bh, start=False, stop=i == n - 1)
                return last

            pe.wait_ge(consts_in, 16 * NCONST)
            for m in range(2 * NT):
                t0, w = TILES[m // 2]
                pe.wait_ge(xs_ready, m // 2 + 1)
                if m >= 2:
                    pe.wait_ge(xn_lo_ready, m - 1)
                for j in range(4):
                    c = 4 * (m % 2) + j
                    last = nc.tensor.transpose(quad(m % 2, w)[:, j, :], xs[0:w, (m // 2) % 2, c * P:(c + 1) * P], ident[0:w, 0:w])
                last.then_inc(xs_turned, 1)
            pe.wait_ge(xn_lo_ready, 2 * NT)
            uses = 0
            for k in range(8):
                pe.wait_ge(w_lo_ready, k + 1)
                for t in range(NT):
                    if uses >= 4:
                        pe.wait_ge(proj_evac, uses - 3)
                    tok = token_columns(t)
                    last = product(bank[2 + uses % 4][:, 0:WC],
                                   [(xn_hi[:, c, tok], xn_lo[:, c, tok], w_hi[:, k % 2, c, :], w_lo[:, k % 2, c, :])
                                    for c in range(CH)])
                    last.then_inc(proj_ready, 1)
                    uses += 1
                pe.wait_ge(proj_ready, uses)
                pe.sem_inc(w_used, 1)
            pe.wait_ge(g8_split, 1)
            for t in range(NT):
                pe.wait_ge(proj_evac, uses - 3)
                tok = token_columns(t)
                product(bank[2 + uses % 4][:, 0:8],
                        [(xn_hi[:, c, tok], xn_lo[:, c, tok], wg8_hi[:, c, :], wg8_lo[:, c, :])
                         for c in range(CH)]).then_inc(proj_ready, 1)
                uses += 1
            for m in range(2 * NT):
                t0, w = TILES[m // 2]
                pe.wait_ge(rope_done, m // 2 + 1)
                if m >= 2:
                    pe.wait_ge(qkt_ready, m - 1)
                for j in range(4):
                    c = 4 * (m % 2) + j
                    last = nc.tensor.transpose(quad(m % 2, w)[:, j, :], qk[0:w, m // 2, c * P:(c + 1) * P], ident[0:w, 0:w])
                last.then_inc(qk_turned, 1)
            for c in range(3 * BH):
                k = 8 + c // 2
                pe.wait_ge(w_lo_ready, k + 1)
                wcols = slice((c % 2) * P, (c % 2) * P + P)
                for h in range(2):
                    pe.wait_ge(proj_evac, uses - 3)
                    cols = slice(h * HALF, (h + 1) * HALF)
                    product(bank[2 + uses % 4][:, 0:HALF],
                            [(w_hi[:, k % 2, i, wcols], w_lo[:, k % 2, i, wcols], xn_hi[:, i, cols], xn_lo[:, i, cols])
                             for i in range(CH)]).then_inc(proj_ready, 1)
                    uses += 1
                if c % 2:
                    pe.wait_ge(proj_ready, uses)
                    pe.sem_inc(w_used, 1)
            pe.wait_ge(proj_evac, uses)
            pe.wait_ge(qkt_ready, 2 * NT)
            for c in range(2 * BH):
                pe.wait_ge(l2_sq, c + 1)
                for t, (t0, w) in enumerate(TILES):
                    last = nc.tensor.matmul(bank[0][0:w, c * NT + t:c * NT + t + 1], l2s[:, c, t0:t0 + w], ones[:, 0:1], start=True, stop=True)
            last.then_inc(l2_sum, 1)
            pe.wait_ge(l2_rt, 1)
            for c in range(2 * BH):
                if c >= 4:
                    pe.wait_ge(l2_done, c - 3)
                for t, (t0, w) in enumerate(TILES):
                    out = bank[L2_BANKS[c % 4]][:, t0:t0 + w] if t < NT - 1 else bank[4][:, c * w:(c + 1) * w]
                    last = nc.tensor.matmul(out, l2r[0:w, c, t:t + 1].broadcast_to([w, P]), ident[0:w, 0:w], start=True, stop=True)
                last.then_inc(l2_rows, 1)
            pe_attend(pe)
            pe_delta(pe)
            pe_sample(pe)
            pe_ffn(pe, product)


def kernel(**inputs):
    import concourse.bacc as bacc
    from concourse.bass_utils import run_bass_kernel_spmd as run

    a = {k: np.asarray(v) for k, v in inputs.items()}

    def tiles(w, cols):
        d, n = w.shape
        return np.ascontiguousarray(w.reshape(CH, P, n // cols, cols).transpose(2, 1, 0, 3))

    w_in = a["w_in"][0]
    eu = tiles(a["expert_u"][0].T, P)
    main = 14 * WC
    qkw = np.stack([a["q_norm_w"][0], a["k_norm_w"][0]])
    qkw = np.stack([qkw, np.roll(qkw, AD // 2, axis=1)], 1)
    arrays = {
        "x_p": a["x_prompt"].reshape(SEQ, D),
        "x_s": a["x_sample"].reshape(NB * NL, D),
        "kc": a["cache_k_win"].reshape(NB, PAST, AH * AD),
        "vc": a["cache_v_win"].reshape(NB, PAST, AH * AD),
        "conv_state": a["state_conv"][0].transpose(2, 0, 1).reshape(3 * BH, P, NB, 3).transpose(1, 0, 2, 3),
        "s0": a["state_delta"].reshape(NB, BH, BD, BD),
        "nmix": a["norm_mix_w"].reshape(D),
        "win": tiles(w_in[:, :main], WC),
        "wg8": tiles(w_in[:, main:], 8)[0],
        "qkw": qkw,
        "convw": a["conv_w"][0].reshape(CONV, 3 * BH, P).transpose(2, 1, 0),
        "alog": a["a_log"].reshape(BH),
        "dtb": a["dt_bias"].reshape(BH),
        "dnw": a["delta_norm_w"].reshape(BD),
        "wout": tiles(a["w_out"][0], WC),
        "nffn": a["norm_ffn_w"].reshape(D),
        "wpq": tiles(a["w_pq"][0], WC),
        "skt": a["sub_keys"][0].transpose(2, 0, 1),
        "eu": np.concatenate([eu[0::2], eu[1::2]]),
        "ev": a["expert_v"][0].reshape(PK, PK, D),
        "pos_t": position_tables(),
        "lnc_p": prompt_log_counts(),
        "lnc_s": sample_log_counts(),
        "squares": square_tables(),
    }
    outs = {
        "y_p": (SEQ, D), "y_s": (NB * NL, D), "k_p": (SEQ, AH * AD), "v_p": (SEQ, AH * AD),
        "conv_out": (P, 3 * BH, (NB + 1) * 3), "s_p": (BH, BD, BD),
        "k_s": (NB, PAST, AH * AD), "v_s": (NB, PAST, AH * AD), "s_s": (NB, BH, BD, BD),
    }
    nc = bacc.Bacc("TRN2", target_bir_lowering=False, num_devices=1)
    args = []
    for name, v in arrays.items():
        arrays[name] = np.ascontiguousarray(v)
        args.append(nc.dram_tensor(name, v.shape, F32, kind="ExternalInput").ap())
    for name, shape in outs.items():
        args.append(nc.dram_tensor(name, shape, F32, kind="ExternalOutput").ap())
    args.append(nc.dram_tensor("gates_dram", (GBLOCKS, P, PK, GT), F32, kind="Internal").ap())
    args.append(nc.dram_tensor("acts_dram", (AHEAD, P, TOK), F32, kind="Internal").ap())
    hybrid_step(nc, *args)
    r = run(nc, [arrays], core_ids=[0]).results[0]
    conv = r["conv_out"].transpose(1, 0, 2).reshape(3 * BH * P, NB + 1, 3).transpose(1, 2, 0)
    return (
        r["y_p"].reshape(1, SEQ, D), r["y_s"].reshape(NB, NL, D),
        r["k_p"].reshape(1, 1, SEQ, AH, AD), r["v_p"].reshape(1, 1, SEQ, AH, AD),
        np.ascontiguousarray(conv[0:1])[None], r["s_p"][None, None],
        r["k_s"].reshape(1, NB, PAST, AH, AD), r["v_s"].reshape(1, NB, PAST, AH, AD),
        np.ascontiguousarray(conv[1:])[None], r["s_s"][None],
    )
```

```python
from contextlib import ExitStack

import numpy as np

import concourse.bass as bass
from concourse import mybir

F32 = mybir.dt.float32
F32R = mybir.dt.float32r
U32 = mybir.dt.uint32
ALU = mybir.AluOpType
ACT = mybir.ActivationFunctionType
AX = mybir.AxisListType

P = 128
D = 1024
CH = D // P
SEQ, NB, NL = 512, 8, 4
TOK = SEQ + NB * NL
TILES = [(t * P, P) for t in range(SEQ // P)] + [(SEQ, NB * NL)]
NT = len(TILES)
HALF = TOK // 2
AH, AD = 8, 64
PAIRS = AH // 2
BH, BD = 4, 128
PAST = 2048
CONV = 4
EPS = 1e-6
NEG = -1e30
WC = 256
OLD_TILES, NEW_TILES = 3, 4
KTILES = OLD_TILES + NEW_TILES
CACHED = KTILES * P
KT_SPLIT = 4 * P
PH, PK, TOPK = 8, 128, 16
EXPERTS = PK * PK
LEVELS = 7
GT = 68
GBLOCKS = TOK // GT
GB = 4
HOT = 4
AHEAD = PK // 2


def position_tables():
    half = AD // 2
    inv = np.float32(10000.0) ** (-np.arange(half, dtype=np.float32) / np.float32(half))
    pos = np.concatenate([np.arange(SEQ), np.tile(PAST + np.arange(NL), NB)]).astype(np.float32)
    ang = (pos[:, None] * inv[None, :].astype(np.float32)).astype(np.float32).astype(np.float64)
    cos, sin = np.cos(ang), np.sin(ang)
    out = np.zeros((2, NT * P, AD), np.float32)
    out[0, :TOK] = np.concatenate([cos, cos], 1)
    out[1, :TOK] = np.concatenate([-sin, sin], 1)
    return out.reshape(2, NT, P, AD).transpose(2, 0, 1, 3).copy()


def log_count(dist):
    count = np.zeros(dist.shape)
    for window, dil in ((128, 1), (512, 4), (2048, 16)):
        count += (dist >= 0) & (dist <= window) & (dist % dil == 0)
    return np.where(count > 0, np.log(np.maximum(count, 1)), NEG).astype(np.float32)


def prompt_log_counts():
    q, k = np.arange(P)[:, None], np.arange(P)[None, :]
    return np.concatenate([log_count(d * P + q - k) for d in (3, 2, 1, 0)], 1)


def sample_log_counts():
    p = np.arange(P)
    pos = [(j * 32 + p // 4) * 16 + p % 4 for j in range(OLD_TILES)]
    pos += [PAST - NEW_TILES * P + j * P + p for j in range(NEW_TILES)]
    pos = np.concatenate(pos)
    rows = PAST + np.tile(np.arange(NL), AH)
    cached = log_count(rows[:, None] - pos[None, :])
    own = log_count(np.arange(NL)[:, None] - np.arange(NL)[None, :])
    new = np.full((AH * NL, NB, NB * NL), NEG, np.float32)
    for b in range(NB):
        new[:, b, b * NL:(b + 1) * NL] = np.tile(own, (AH, 1))
    return np.concatenate([cached, new.reshape(AH * NL, -1)], 1)


def square_tables():
    i = np.arange(P)
    j, c = i[:, None], i[None, :]
    out = [j == c, np.ones((P, P)), j <= c, (j <= c) & (j // NL == c // NL), j // NL == c // NL,
           np.broadcast_to(c, (P, P))]
    for lv in range(LEVELS):
        s = 1 << lv
        out.append((j // (2 * s) == c // (2 * s)) & ((c // s) % 2 == 1) & ((j // s) % 2 == 0))
    return np.stack(out, 1).astype(np.float32)


IDENT, ONES, CUM_P, CUM_S, BLK_S, ASC, LEVEL0 = range(7)
NSQ = LEVEL0 + LEVELS


class Chain:

    def __init__(self, eng, sem):
        self.eng, self.sem, self.n = eng, sem, 0

    def mark(self, ins):
        ins.then_inc(self.sem, 1)
        self.n += 1

    def join(self):
        self.eng.wait_ge(self.sem, self.n)

    def link(self, ins):
        self.mark(ins)
        self.join()


def rows(n):
    w = TILES[n][1]
    return slice(P - w, P)


def token_columns(n):
    t0, w = TILES[n]
    return slice(t0 + w - P, t0 + w)


def bc(ap, axis, count):
    ap = ap.unsqueeze(axis)
    shape = list(ap.shape)
    shape[axis] = count
    return ap.broadcast_to(shape)


def hybrid_step(nc, x_p, x_s, kc, vc, conv_state, s0, nmix, win, wg8, qkw, convw, alog, dtb, dnw, wout, nffn,
                wpq, skt, eu, ev, pos_t, lnc_p, lnc_s, squares,
                y_p, y_s, k_p, v_p, conv_out, s_p, k_s, v_s, s_s, gates_dram, acts_dram):
    with ExitStack() as ctx:
        def sem(name):
            return ctx.enter_context(nc.semaphore(name))

        base = 16512
        top = [0]

        def at(name, offset, shape, dt=F32):
            size = int(np.prod(shape[1:])) * 4
            top[0] = max(top[0], offset + size)
            assert offset + size <= 212800, name
            return nc.alloc_sbuf_tensor_at(name, shape, dt, offset=base + offset)

        def region(offset):
            pos = [offset]

            def put(name, shape, dt=F32):
                t = at(name, pos[0], shape, dt)
                pos[0] += -(-int(np.prod(shape[1:])) * 4 // 32) * 32
                return t
            put.pos = pos
            return put

        put = region(0)
        sq = put("sq", [P, NSQ, P])
        R_NMIX = put.pos[0]
        nmix_b = put("nmix_b", [P, D])
        lncp = put("lncp", [P, 4 * P])
        lncs = put("lncs", [NB * NL, CACHED + NB * NB * NL])
        pos = put("pos", [P, 2, NT, AD])
        cw = put("cw", [P, NT, 2, AD])
        sw = put("sw", [P, NT, 2, AD])
        qkw_b = put("qkw_b", [P, 2, 2, AD])
        convw_t = put("convw_t", [P, 3 * BH, CONV])
        dnw_b = put("dnw_b", [P, BD])
        gconst = put("gconst", [P, 2, BH])
        g8 = put("g8", [P, NT, 2 * BH])
        gz = put("gz", [P, NT, BH])
        gl = put("gl", [P, NT, BH])
        gate_g = put("gate_g", [P, NT, BH])
        beta = put("beta", [P, NT, BH])
        nega = put("nega", [P, BH])
        R_STAT = put.pos[0]
        stat = put("stat", [P, 8, NT])
        ropes = put("ropes", [P, NT, 16])
        wg8_raw = put("wg8_raw", [P, CH, 8])
        wg8_hi = put("wg8_hi", [P, CH, 8], F32R)
        wg8_lo = put("wg8_lo", [P, CH, 8], F32R)
        cst = put("cst", [P, 3 * BH, NB, 3])
        cso = put("cso", [P, 3 * BH, (NB + 1) * 3])
        l2r = put("l2r", [P, 2 * BH, NT])
        smax = put("smax", [P, 4, 4])
        sstat = put("sstat", [NB * NL, 2, 8])
        R_X = put.pos[0]
        R_XN = R_X + 20480
        R_W = R_XN + 2 * CH * TOK * 4
        R_AQ = R_W + 40960
        R_AV = R_AQ + 12 * TOK * 4
        R_BZ = R_AV + NT * 512 * 4
        R_QK = R_BZ + NT * 512 * 4
        R_E = R_QK + 8 * TOK * 4

        ident, ones, asc = sq[:, IDENT, :], sq[:, ONES, :], sq[:, ASC, :]
        X = at("X", R_X, [P, NT, D])
        xs = at("xs", R_BZ, [P, 2, D])
        xn_hi = at("xn_hi", R_XN, [P, CH, TOK], F32R)
        xn_lo = at("xn_lo", R_XN + CH * TOK * 4, [P, CH, TOK], F32R)
        w_raw = [at("w_raw0", R_W, [P, CH, WC]), at("w_raw1", R_E + 9216, [P, CH, WC])]
        w_hi = at("w_hi", R_W + 8192, [P, 2, CH, WC], F32R)
        w_lo = at("w_lo", R_W + 24576, [P, 2, CH, WC], F32R)
        qk = at("qk", R_AQ, [P, NT, 2 * AH * AD])
        co = at("co", R_AQ, [P, 3 * BH, TOK])
        av = at("av", R_AV, [P, NT, AH * AD])
        bz = at("bz", R_BZ, [P, NT, BH * BD])
        qkt = at("qkt", R_QK, [P, 2 * PAIRS, TOK])
        tmp1 = at("tmp1", R_E, [P, 16 * AD])
        tmp2 = at("tmp2", R_E + 4096, [P, 16 * AD])
        g8t = at("g8t", R_E + 18432, [2 * BH, TOK])
        ext = at("ext", R_E, [P, 2, 3 + SEQ + NB * (3 + NL) + 1])
        cy = at("cy", R_E + 2 * 572 * 4 + 32, [P, 2, TOK])
        put = region(R_XN)
        l2s = at("l2s", R_X, [P, 2 * BH, TOK])
        cat = at("cat", R_X, [P, CH, TOK])
        sm = at("sm", R_E, [P, 4, 4 * P])
        pt = at("pt", R_E + 8192, [P, 2, 4, P])
        put = region(R_XN)

        def slots(name):
            return [put(f"{name}{s}", [P, BH, P]) for s in range(2)]
        eg, qd, lt, it, kd, kbg, vb, xt, xi, yv, ml, uu, wt = (
            slots(n) for n in ("eg", "qd", "lt", "it", "kd", "kbg", "vb", "xt", "xi", "yv", "ml", "uu", "wt"))
        vm = [at("vm0", R_XN + 2048, [P, NB, BD]), at("vm1", R_XN + 49152, [P, NB, BD])]
        wq = at("wq", R_XN + 51200, [P, BH, NB, 2, NL])
        vnt = put("vnt", [P, 3, BH, NB * NL])
        s_cur = put("s_cur", [P, BH, BD])
        gcol = put("gcol", [P, 2, 4, BH])
        ost = put("ost", [P, 2, 2, BH])
        ss0 = at("ss0", R_W + 40960 - 16384, [P, NB, BH, BD])
        assert put.pos[0] <= R_W + 40960 - 16384
        put = region(R_XN)
        ks = [put(f"ks{s}", [P, KTILES, AH * AD]) for s in range(2)]
        vs_old = [None, put("vs_old1", [P, OLD_TILES, AH * AD])]
        assert put.pos[0] <= R_W
        put = region(R_AQ)
        vs_old[0] = put("vs_old0", [P, OLD_TILES, AH * AD])
        vs_new = [put(f"vs_new{s}", [P, NEW_TILES, AH * AD]) for s in range(2)]
        assert put.pos[0] <= R_AV
        kt_lo = at("kt_lo", R_BZ, [P, PAIRS, KT_SPLIT])
        put = region(R_E)
        sss = [put(f"sss{s}", [NB * NL, CACHED + NB * NL]) for s in range(2)]
        pts = put("pts", [P, KTILES + 1, NB * NL])
        qbd = put("qbd", [P, NB, PAIRS, NB * NL])
        kt_hi = put("kt_hi", [P, PAIRS, CACHED - KT_SPLIT])

        cat_hi = at("cat_hi", R_AQ, [P, CH, TOK], F32R)
        cat_lo = at("cat_lo", R_AQ + CH * TOK * 4, [P, CH, TOK], F32R)
        hn_hi = at("hn_hi", R_AQ, [P, CH, TOK], F32R)
        hn_lo = at("hn_lo", R_AQ + CH * TOK * 4, [P, CH, TOK], F32R)
        R_B = R_AQ + 2 * CH * TOK * 4
        put = region(R_B)
        qt = put("qt", [P, 2 * PH, TOK])
        put = region(R_XN)
        hs = put("hs", [P, 2, D])
        cand = put("cand", [P, PH, TOPK, TOPK])
        eq = put("eq", [P, PH, TOPK, TOPK])
        tv = put("tv", [P, 2 * PH, TOPK])
        ti = put("ti", [P, 2 * PH, TOPK], U32)
        tif = put("tif", [P, 2 * PH, TOPK])
        bv = put("bv", [P, PH, TOPK])
        bi = put("bi", [P, PH, TOPK], U32)
        bhl = put("bhl", [P, 2, PH, TOPK], U32)
        bhlf = put("bhlf", [P, 2, PH, TOPK])
        picks = put("picks", [P, 3, PH * TOPK])
        gsum = put("gsum", [P, 2, PH])
        assert put.pos[0] <= R_W
        put = region(R_W)
        picks_t = put("picks_t", [P, 3, TOK])
        cols_s = put("cols_s", [P, 2, 3, GT])
        skt_s = put("skt_s", [P, 2, PK])
        sub_s = [put(f"sub_s{s}", [P, 2 * PH, PK]) for s in range(2)]
        assert put.pos[0] <= R_AQ
        put = region(put.pos[0] - 2 * 8192)
        one1 = [put(f"one1_{s}", [P, 4, PK]) for s in range(HOT)]
        one2 = [put(f"one2_{s}", [P, 4, PK]) for s in range(HOT)]
        assert put.pos[0] <= R_AQ
        gst = [at("gst0", R_XN, [P, PK, GT]), at("gst1", R_B, [P, PK, GT])]
        put = region(R_XN)
        v_raw = [put(f"v_raw{s}", [P, D]) for s in range(2)]
        v_hi = [put(f"v_hi{s}", [P, D], F32R) for s in range(4)]
        v_lo = [put(f"v_lo{s}", [P, D], F32R) for s in range(4)]
        gin = [put(f"gin{s}", [P, GBLOCKS, 2, GT]) for s in range(2)]
        assert put.pos[0] <= R_AQ
        put = region(R_NMIX)
        u_raw = [put(f"u_raw{s}", [P, CH, P]) for s in range(2)]
        u_hi = [put(f"u_hi{s}", [P, CH, P], F32R) for s in range(2)]
        u_lo = [put("u_lo0", [P, CH, P], F32R)]
        assert put.pos[0] <= R_STAT
        put = region(R_B + 2 * PH * TOK * 4)
        u_lo.append(put("u_lo1", [P, CH, P], F32R))
        act_c = [put(f"act_c{s}", [P, TOK]) for s in range(2)]
        act_l = [put(f"act_l{s}", [P, TOK]) for s in range(2)]
        put = region(R_B)
        a_hi = [put(f"a_hi{s}", [P, TOK], F32R) for s in range(4)]
        a_lo = [put(f"a_lo{s}", [P, TOK], F32R) for s in range(4)]
        y_t = put("y_t", [P, CH, TOK])

        bank = [ctx.enter_context(nc.psum_tensor(f"bank{i}", [P, 512], F32)) for i in range(8)]

        def quad(b, w=P, n=P):
            return bank[b][0:n, 0:4 * w].rearrange("p (h c) -> p h c", h=4)

        block = ctx.enter_context(nc.Block())

        NW1 = 14
        order1 = [0, 1, 2, 3, 4, 5, 12, 13, 6, 7, 8, 9, 10, 11]

        x_in = [sem(f"x_in{t}") for t in range(NT)]
        consts_in, small_in = sem("consts_in"), sem("small_in")
        ssq_ready, rstd_ready, xs_ready, xs_turned = sem("ssq_ready"), sem("rstd_ready"), sem("xs_ready"), sem("xs_turned")
        var_ready = sem("var_ready")
        xn_hi_ready, xn_lo_ready = sem("xn_hi_ready"), sem("xn_lo_ready")
        w_in, w_hi_ready, w_lo_ready, w_used = [sem("w_in0"), sem("w_in1")], sem("w_hi_ready"), sem("w_lo_ready"), sem("w_used")
        logits_done = sem("logits_done")
        proj_ready, proj_evac = sem("proj_ready"), sem("proj_evac")
        rope_var, rope_rs, rope_done = sem("rope_var"), sem("rope_rs"), sem("rope_done")
        qk_turned, qkt_ready = sem("qk_turned"), sem("qkt_ready")
        kv_out = sem("kv_out")
        ext_ready, ext_state, conv_done, cso_done, silu_done = (
            sem("ext_ready"), sem("ext_state"), sem("conv_done"), sem("cso_done"), sem("silu_done"))
        l2_sq, l2_sum, l2_inv, l2_rt, l2_rows, l2_done = (
            sem("l2_sq"), sem("l2_sum"), sem("l2_inv"), sem("l2_rt"), sem("l2_rows"), sem("l2_done"))
        gates_dve, gates_act = sem("gates_dve"), sem("gates_act")
        out_done = sem("out_done")
        dve_chain, act_chain, pool_chain = sem("dve_chain"), sem("act_chain"), sem("pool_chain")
        s_scores, s_masked, s_exp, s_norm, s_turned, s_pt, s_out, s_cat = (
            sem("s_scores"), sem("s_masked"), sem("s_exp"), sem("s_norm"), sem("s_turned"), sem("s_pt"),
            sem("s_out"), sem("s_cat"))
        extra = {}

        def S_(name):
            if name not in extra:
                extra[name] = sem(name)
            return extra[name]

        NCONST = 3
        NKV = 2 * (NT - 1) + 2 * NB
        L2_BANKS = (2, 3, 5, 6)
        COPIES_W, COPIES_A, COPIES_D = NW1 // 2, -(-SEQ // P * AH // 3), 2 * (LEVELS - 1)
        COPIES = COPIES_W + COPIES_A + COPIES_D
        ROWS = -(-PAST // COPIES)

        def copy_cache(act, n):
            a, b = n * ROWS, min((n + 1) * ROWS, PAST - NL)
            for dst, src in ((k_s, kc), (v_s, vc)):
                act.dma_start(dst[:, a:b, :], src[:, a + NL:b + NL, :]).then_inc(out_done, 16)

        UNITS = [(i, h) for i in range(SEQ // P) for h in range(AH)]

        def pe_attend(pe):
            pe.wait_ge(l2_done, 2 * BH + 1)

            def scores(u):
                i, h = UNITS[u]
                if u >= 4:
                    pe.wait_ge(s_masked, u - 3)
                r = slice(AD * (h % 2), AD * (h % 2) + AD)
                nc.tensor.matmul(bank[2 + u % 4][:, 0:(i + 1) * P], qkt[r, h // 2, i * P:(i + 1) * P],
                                 qkt[r, PAIRS + h // 2, 0:(i + 1) * P], start=True, stop=True).then_inc(s_scores, 1)

            def turn(u):
                i, h = UNITS[u]
                pe.wait_ge(s_norm, u + 1)
                if u >= 2:
                    pe.wait_ge(s_pt, u - 1)
                for j in range(i + 1):
                    last = nc.tensor.transpose(quad(u % 2)[:, j, :], sm[:, u % 4, j * P:(j + 1) * P], ident)
                last.then_inc(s_turned, 1)

            def values(u):
                i, h = UNITS[u]
                pe.wait_ge(s_pt, u + 1)
                if u >= 4:
                    pe.wait_ge(s_cat, u // 2 - 1)
                r = slice(AD * (h % 2), AD * (h % 2) + AD)
                for j in range(i + 1):
                    last = nc.tensor.matmul(bank[6 + (u // 2) % 2][r, 0:P], av[:, j, h * AD:(h + 1) * AD], pt[:, u % 2, j, :],
                                            start=j == 0, stop=j == i)
                last.then_inc(s_out, 1)

            for u in range(4):
                scores(u)
            for u in range(len(UNITS)):
                turn(u)
                if u:
                    values(u - 1)
                if u + 4 < len(UNITS):
                    scores(u + 4)
            values(len(UNITS) - 1)

        def dve_attend(dve, chain):
            dve.wait_ge(silu_done, 3 * BH)
            dve.wait_ge(cso_done, 3 * BH)

            def mask(u):
                i, h = UNITS[u]
                n = (i + 1) * P
                dve.wait_ge(s_scores, u + 1)
                if u >= 4:
                    dve.wait_ge(s_turned, u - 3)
                chain.link(nc.vector.tensor_tensor_reduce(
                    out=sm[:, u % 4, 0:n], in0=bank[2 + u % 4][:, 0:n], in1=lncp[:, 4 * P - n:4 * P], scale=1.0,
                    scalar=NEG, op0=ALU.add, op1=ALU.max, accum_out=smax[:, u % 4, 0:1]))
                nc.vector.tensor_scalar(smax[:, u % 4, 1:2], smax[:, u % 4, 0:1], -1.0, None, ALU.mult).then_inc(s_masked, 1)

            mask(0)
            mask(1)
            for u in range(len(UNITS)):
                if u + 2 < len(UNITS):
                    mask(u + 2)
                n = (UNITS[u][0] + 1) * P
                dve.wait_ge(s_exp, u + 1)
                chain.link(nc.vector.reciprocal(smax[:, u % 4, 3:4], smax[:, u % 4, 2:3]))
                nc.vector.tensor_scalar(sm[:, u % 4, 0:n], sm[:, u % 4, 0:n], smax[:, u % 4, 3:4], None, ALU.mult).then_inc(s_norm, 1)

        def act_attend(act, chain):
            def turned(u):
                i, h = UNITS[u]
                act.wait_ge(s_turned, u + 1)
                if u >= 2:
                    act.wait_ge(s_out, u - 1)
                nc.scalar.activation(pt[:, u % 2, 0:i + 1, :], quad(u % 2)[:, 0:i + 1, :], ACT.Copy).then_inc(s_pt, 1)

            def pair(v):
                i = UNITS[2 * v][0]
                act.wait_ge(s_out, 2 * v + 2)
                nc.scalar.activation(cat[:, v % PAIRS, i * P:(i + 1) * P], bank[6 + v % 2][:, 0:P], ACT.Copy).then_inc(s_cat, 1)

            def exponentials(u):
                n = (UNITS[u][0] + 1) * P
                act.wait_ge(s_masked, u + 1)
                nc.scalar.activation(sm[:, u % 4, 0:n], sm[:, u % 4, 0:n], ACT.Exp, bias=smax[:, u % 4, 1:2],
                                     accum_out=smax[:, u % 4, 2:3]).then_inc(s_exp, 1)

            exponentials(0)
            exponentials(1)
            for u in range(len(UNITS)):
                if u + 2 < len(UNITS):
                    exponentials(u + 2)
                if u % 3 == 0:
                    copy_cache(act, COPIES_W + u // 3)
                if u:
                    turned(u - 1)
                if u >= 3 and u % 2:
                    pair(u // 2 - 1)
            turned(len(UNITS) - 1)
            pair(len(UNITS) // 2 - 1)

        GROUPS = [(0, 1), (2, 3), (4,)]
        names = ("gg rows kk tok eg gd dt dec sc front x0 x0t xi ml y yc xy xu uw uwc ws vn os s o ovar ort og ot cat "
                 "s_pe s_act s_dve vm st su pf tk kq sd")
        dl = {n: S_("delta_" + n) for n in names.split()}

        sample_bank = bank[0][:, 0:2 * BH * NB * NL].rearrange("p (h b k l) -> p h b k l", h=BH, b=NB, k=2)
        STATE_BANKS = (6, 2)

        def cum(n):
            return sq[:, CUM_P if n < NT - 1 else CUM_S, :]

        def total(n):
            return sq[:, ONES if n < NT - 1 else BLK_S, :]

        def levels(n):
            return LEVELS if n < NT - 1 else 2

        def level_steps(group):
            return [(lv, n) for lv in range(1, levels(group[0])) for n in group]

        step_no = {}
        for g_ in GROUPS:
            for st_ in level_steps(g_):
                step_no[st_] = len(step_no)

        def sub(t, w, cols=None):
            return t[0:w, :, 0:(w if cols is None else cols)]

        def pe_delta(pe):
            pe.wait_ge(s_cat, len(UNITS) // 2)
            pe.wait_ge(gates_dve, 3)
            pe.wait_ge(l2_done, 2 * BH + 1)

            def front(n):
                (t0, w), s = TILES[n], n % 2
                cols = slice(t0, t0 + w)
                if n in (2, 4):
                    pe.wait_ge(dl["o"], n)
                    pe.wait_ge(dl["s"], n)
                elif n:
                    pe.wait_ge(dl["front"], n)
                    pe.wait_ge(dl["tk"], n)
                    pe.wait_ge(dl["eg"], n)
                pe.wait_ge(dl["gg"], n + 1)
                nc.tensor.matmul(bank[6][0:w, 0:4], cum(n)[0:w, 0:w], gate_g[0:w, n, :], start=True, stop=True)
                nc.tensor.matmul(bank[6][0:w, 4:8], total(n)[0:w, 0:w], gate_g[0:w, n, :], start=True, stop=True)
                nc.tensor.matmul(quad(0, w), ones[0:w, :], sub(lt[s], w), start=True, stop=True)
                nc.tensor.matmul(quad(1, w), ones[0:w, :], sub(it[s], w), start=True, stop=True).then_inc(dl["rows"], 1)
                for h in range(BH):
                    nc.tensor.matmul(quad(2, w, w)[:, h, :], co[:, BH + h, cols], co[:, BH + h, cols], start=True, stop=True)
                    last = nc.tensor.matmul(quad(3, w, w)[:, h, :], co[:, BH + h, cols], co[:, h, cols], start=True, stop=True)
                last.then_inc(dl["kk"], 1)
                for h in range(BH):
                    for b, c in ((4, BH + h), (5, 2 * BH + h)):
                        if w == P:
                            last = nc.tensor.transpose(quad(b)[:, h, :], co[:, c, cols], ident)
                        else:
                            last = nc.tensor.matmul(quad(b)[0:w, h, :], co[:, c, cols], ident, start=True, stop=True)
                last.then_inc(dl["tok"], 1)

            front(0)
            for group in GROUPS:
                for n in group[1:]:
                    front(n)
                for n in group:
                    w, s = TILES[n][1], n % 2
                    pe.wait_ge(dl["x0"], n + 1)
                    if n:
                        pe.wait_ge(dl["xi"], n)
                    if n == group[0] and n:
                        pe.wait_ge(dl["cat"], n)
                    for h in range(BH):
                        if w == P:
                            last = nc.tensor.transpose(quad(7)[:, h, :], xt[s][:, h, :], ident)
                        else:
                            last = nc.tensor.matmul(quad(7, w, w)[:, h, :], xt[s][0:w, h, 0:w], ident[0:w, 0:w], start=True, stop=True)
                    last.then_inc(dl["x0t"], 1)
                pe.wait_ge(dl["front"], group[-1] + 1)
                pe.wait_ge(dl["tk"], group[-1] + 1)
                pe.wait_ge(dl["pf"], 3 * (group[-1] + 1))
                for lv, n in level_steps(group):
                    w, s, q = TILES[n][1], n % 2, step_no[lv, n]
                    pe.wait_ge(dl["ml"], q + 1)
                    if lv == 1:
                        pe.wait_ge(dl["xi"], n + 1)
                    else:
                        pe.wait_ge(dl["xu"], step_no[lv - 1, n] + 1)
                    for h in range(BH):
                        last = nc.tensor.matmul(quad(s, w, w)[:, h, :], ml[s][0:w, h, 0:w], xi[s][0:w, h, 0:w], start=True, stop=True)
                    last.then_inc(dl["y"], 1)
                    if n != group[-1]:
                        continue
                    for m in group:
                        s, q = m % 2, step_no[lv, m]
                        pe.wait_ge(dl["yc"], q + 1)
                        for h in range(BH):
                            if lv < levels(m) - 1:
                                nc.tensor.matmul(quad(2 + s, w, w)[:, h, :], xt[s][0:w, h, 0:w], yv[s][0:w, h, 0:w], start=True, stop=True)
                            last = nc.tensor.matmul(quad(4 + s, w, w)[:, h, :], yv[s][0:w, h, 0:w], xt[s][0:w, h, 0:w], start=True, stop=True)
                        last.then_inc(dl["xy"], 1)
                for n in group:
                    w, s = TILES[n][1], n % 2
                    pe.wait_ge(dl["xu"], step_no[levels(n) - 1, n] + 1)
                    if n:
                        pe.wait_ge(dl["uwc"], n)
                    for h in range(BH):
                        if n < NT - 1:
                            nc.tensor.matmul(quad(6)[:, h, :], xt[s][:, h, :], vb[s][:, h, :], start=True, stop=True)
                        else:
                            nc.tensor.matmul(quad(6, w)[:, h, :], vb[s][0:w, h, :], xt[s][0:w, h, 0:w], start=True, stop=True)
                        last = nc.tensor.matmul(quad(7, w)[:, h, :], kbg[s][0:w, h, :], xt[s][0:w, h, 0:w], start=True, stop=True)
                    last.then_inc(dl["uw"], 1)
                if group[0] < NT - 1:
                    for n in group:
                        s = n % 2
                        pe.wait_ge(dl["uwc"], n + 1)
                        if n:
                            pe.wait_ge(dl["s"], n)
                            for h in range(BH):
                                last = nc.tensor.matmul(quad(0)[:, h, :], wt[s][:, h, :], s_cur[:, h, :], start=True, stop=True)
                            last.then_inc(dl["ws"], 1)
                            pe.wait_ge(dl["vn"], n)
                            pe.wait_ge(dl["o"], n)
                        vn = ml[s] if n else uu[s]
                        for h in range(BH):
                            if n:
                                nc.tensor.matmul(quad(1)[:, h, :], qd[s][:, h, :], s_cur[:, h, :], start=True, stop=False)
                            nc.tensor.matmul(quad(1)[:, h, :], it[s][:, h, :], vn[:, h, :], start=n == 0, stop=True)
                            last = nc.tensor.matmul(quad(2)[:, h, :], kd[s][:, h, :], vn[:, h, :], start=True, stop=True)
                        last.then_inc(dl["os"], 1)
                else:
                    pe_delta_sample(pe)
                if group[-1] + 1 < NT:
                    front(group[-1] + 1)
                for n in group:
                    w, s = TILES[n][1], n % 2
                    pe.wait_ge(dl["og"], n + 1)
                    if n:
                        pe.wait_ge(dl["cat"], n)
                    for h in range(BH):
                        last = nc.tensor.transpose(quad(7, w)[:, h, :], yv[s][0:w, h, :], ident[0:w, 0:w])
                    last.then_inc(dl["ot"], 1)

        def pe_delta_sample(pe):
            w, s = NB * NL, 0
            pe.wait_ge(dl["uwc"], NT)
            pe.wait_ge(S_("states_in"), 16)
            for h in range(BH):
                for b in range(NB):
                    last = nc.tensor.matmul(sample_bank[:, h, b], ss0[:, b, h, :], wq[:, h, b], start=True, stop=True)
            last.then_inc(dl["s_pe"], 1)
            pe.wait_ge(dl["s_dve"], 1)
            for h in range(BH):
                last = nc.tensor.matmul(quad(2)[0:w, h, :], vnt[:, 0, h, :], ident, start=True, stop=True)
            last.then_inc(dl["s_pe"], 1)
            pe.wait_ge(dl["s_act"], 2)
            for h in range(BH):
                last = nc.tensor.matmul(quad(3, w)[:, h, :], ml[s][0:w, h, :], it[s][0:w, h, 0:w], start=True, stop=True)
            last.then_inc(dl["s_pe"], 1)
            pe.wait_ge(dl["s_dve"], 2)
            for h in range(BH):
                last = nc.tensor.matmul(quad(4)[0:w, h, :], vnt[:, 2, h, :], ident, start=True, stop=True)
            last.then_inc(dl["s_pe"], 1)
            for h in range(BH):
                pe.wait_ge(dl["vm"], h + 1)
                if h >= 2:
                    pe.wait_ge(dl["su"], h - 1)
                for b2 in range(2):
                    last = nc.tensor.matmul(quad(STATE_BANKS[h % 2] + b2), kd[s][0:w, h, :], vm[h % 2][0:w, 4 * b2:4 * b2 + 4, :],
                                            start=True, stop=True)
                last.then_inc(dl["st"], 1)

        def act_delta(act, chain):
            act.wait_ge(l2_done, 2 * BH + 1)
            for group in GROUPS:
                for n in group:
                    w, s = TILES[n][1], n % 2
                    act.wait_ge(dl["rows"], n + 1)
                    nc.scalar.activation(eg[s][:, :, 0:w], quad(0, w), ACT.Exp).then_inc(dl["eg"], 1)
                    act.wait_ge(dl["gd"], n + 1)
                    nc.scalar.activation(gcol[0:w, s, 1:3, :], gcol[0:w, s, 1:3, :], ACT.Exp).then_inc(dl["sc"], 1)
                    act.wait_ge(dl["dt"], n + 1)
                    nc.scalar.activation(sub(lt[s], w), sub(lt[s], w), ACT.Exp).then_inc(dl["dec"], 1)
                    act.wait_ge(dl["tok"], n + 1)
                    act.wait_ge(dl["pf"], 3 * n + 2)
                    for h in range(BH):
                        for out, b, scale in ((kd[s], 4, gcol[0:w, s, 1, h:h + 1]), (kbg[s], 4, gcol[0:w, s, 3, h:h + 1]),
                                              (vb[s], 5, beta[0:w, n, h:h + 1])):
                            last = nc.scalar.activation(out[0:w, h, :], quad(b)[0:w, h, :], ACT.Copy, scale=scale)
                    last.then_inc(dl["tk"], 1)
                for n in group:
                    w, s = TILES[n][1], n % 2
                    act.wait_ge(dl["x0t"], n + 1)
                    nc.scalar.activation(sub(xi[s], w), quad(7, w, w), ACT.Copy).then_inc(dl["xi"], 1)
                for lv, n in level_steps(group):
                    w, s, q = TILES[n][1], n % 2, step_no[lv, n]
                    if n == group[0] and n < NT - 1:
                        copy_cache(act, COPIES_W + COPIES_A + group[0] // 2 * (LEVELS - 1) + lv - 1)
                    act.wait_ge(dl["y"], q + 1)
                    nc.scalar.activation(sub(yv[s], w), quad(s, w, w), ACT.Copy).then_inc(dl["yc"], 1)
                for n in group:
                    w, s = TILES[n][1], n % 2
                    act.wait_ge(dl["uw"], n + 1)
                    if n < NT - 1:
                        chain.mark(nc.scalar.activation(uu[s][:], quad(6), ACT.Copy))
                    else:
                        chain.mark(nc.scalar.activation(uu[s][:, :, 0:w], quad(6, w), ACT.Copy))
                    if n < NT - 1:
                        chain.link(nc.scalar.activation(wt[s][:], quad(7), ACT.Copy))
                    else:
                        chain.link(nc.scalar.activation(wq[:, :, :, 0, :], quad(7, w).rearrange("p h (b l) -> p h b l", l=NL), ACT.Copy))
                    act.sem_inc(dl["uwc"], 1)
                if group[0] < NT - 1:
                    for n in group:
                        act.wait_ge(dl["os"], n + 1)
                        nc.scalar.activation(yv[n % 2][:], quad(1), ACT.Copy).then_inc(dl["o"], 1)
                else:
                    w, s = NB * NL, 0
                    act.wait_ge(dl["s_dve"], 1)
                    nc.scalar.activation(vnt[:, 1].rearrange("p h (b l) -> p h b l", l=NL), sample_bank[:, :, :, 1, :], ACT.Copy)\
                        .then_inc(dl["s_act"], 1)
                    act.wait_ge(dl["s_pe"], 2)
                    nc.scalar.activation(ml[s][0:w], quad(2)[0:w], ACT.Copy).then_inc(dl["s_act"], 1)
                    act.wait_ge(dl["s_pe"], 4)
                    nc.scalar.activation(yv[s][0:w], quad(4)[0:w], ACT.Copy).then_inc(dl["o"], 1)
                for n in group:
                    act.wait_ge(dl["ovar"], n + 1)
                    nc.scalar.activation(ost[:, n % 2, 1, :], ost[:, n % 2, 1, :], ACT.Sqrt).then_inc(dl["ort"], 1)
                for n in group:
                    t0, w = TILES[n]
                    act.wait_ge(dl["ot"], n + 1)
                    nc.scalar.activation(cat[:, PAIRS:, t0:t0 + w], quad(7, w), ACT.Copy).then_inc(dl["cat"], 1)

        def dve_delta(dve, chain):
            tt = nc.vector.tensor_tensor
            chain.link(nc.vector.memset(ost[:], 1.0))

            def seeds(group):
                for n in group:
                    w, s = TILES[n][1], n % 2
                    chain.mark(tt(out=sub(lt[s], w), in0=bc(cum(n)[0:w, 0:w], 1, BH), in1=bc(gate_g[0:w, n, :], 2, w), op=ALU.mult))
                    chain.link(tt(out=sub(it[s], w), in0=bc(ident[0:w, 0:w], 1, BH), in1=bc(beta[0:w, n, :], 2, w), op=ALU.mult))
                    dve.sem_inc(dl["gg"], 1)

            seeds(GROUPS[0])
            for g, group in enumerate(GROUPS):
                for n in group:
                    (t0, w), s = TILES[n], n % 2
                    dve.wait_ge(dl["rows"], n + 1)
                    chain.link(nc.vector.tensor_copy(gcol[0:w, s, 0, :], bank[6][0:w, 0:4]))
                    chain.mark(nc.vector.tensor_copy(gcol[0:w, s, 2, :], bank[6][0:w, 0:4]))
                    chain.link(tt(out=gcol[0:w, s, 1, :], in0=bank[6][0:w, 4:8], in1=gcol[0:w, s, 0, :], op=ALU.subtract))
                    dve.sem_inc(dl["gd"], 1)
                    dve.wait_ge(dl["eg"], n + 1)
                    for h in range(BH):
                        chain.mark(nc.vector.tensor_scalar(lt[s][0:w, h, 0:w], quad(0, w, w)[:, h, :], gcol[0:w, s, 0, h:h + 1],
                                                           0.0, ALU.subtract, ALU.min))
                    chain.join()
                    dve.sem_inc(dl["dt"], 1)
                    dve.wait_ge(dl["dec"], n + 1)
                    dve.wait_ge(dl["kk"], n + 1)
                    tt(out=sub(it[s], w), in0=quad(3, w, w), in1=sub(lt[s], w), op=ALU.mult).then_inc(dl["kq"], 1)
                    dve.wait_ge(dl["kq"], n + 1)
                    chain.link(tt(out=sub(lt[s], w), in0=quad(2, w, w), in1=sub(lt[s], w), op=ALU.mult))
                    chain.link(tt(out=sub(lt[s], w), in0=sub(lt[s], w), in1=quad(1, w, w), op=ALU.mult))
                    chain.link(tt(out=sub(ml[s], w), in0=sub(lt[s], w), in1=bc(sq[0:w, LEVEL0, 0:w], 1, BH), op=ALU.mult))
                    chain.link(tt(out=sub(xt[s], w), in0=bc(ident[0:w, 0:w], 1, BH), in1=sub(ml[s], w), op=ALU.subtract))
                    dve.sem_inc(dl["x0"], 1)
                    dve.sem_inc(dl["front"], 1)
                for lv, n in level_steps(group):
                    w, s, q = TILES[n][1], n % 2, step_no[lv, n]
                    dve.wait_ge(dl["xy"], q + 1)
                    if lv < levels(n) - 1:
                        chain.mark(tt(out=sub(xi[s], w), in0=sub(xi[s], w), in1=quad(2 + s, w, w), op=ALU.subtract))
                    chain.link(tt(out=sub(xt[s], w), in0=sub(xt[s], w), in1=quad(4 + s, w, w), op=ALU.subtract))
                    dve.sem_inc(dl["xu"], 1)
                if group[0] < NT - 1:
                    for n in group:
                        s = n % 2
                        if n:
                            dve.wait_ge(dl["ws"], n)
                            tt(out=ml[s][:], in0=uu[s][:], in1=quad(0), op=ALU.subtract).then_inc(dl["vn"], 1)
                        dve.wait_ge(dl["os"], n + 1)
                        if n:
                            for h in range(BH):
                                chain.mark(nc.vector.scalar_tensor_tensor(out=s_cur[:, h, :], in0=s_cur[:, h, :], scalar=eg[s][:, h, P - 1:P],
                                                                          in1=quad(2)[:, h, :], op0=ALU.mult, op1=ALU.add))
                            chain.join()
                        else:
                            chain.link(nc.vector.tensor_copy(s_cur[:], quad(2)))
                        dve.sem_inc(dl["s"], 1)
                else:
                    w, s = NB * NL, 0
                    dve.wait_ge(dl["s_pe"], 1)
                    tt(out=vnt[:, 0].rearrange("p h (b l) -> p h b l", l=NL), in0=uu[s][:, :, 0:w].rearrange("p h (b l) -> p h b l", l=NL),
                       in1=sample_bank[:, :, :, 0, :], op=ALU.subtract).then_inc(dl["s_dve"], 1)
                    dve.wait_ge(dl["s_act"], 1)
                    dve.wait_ge(dl["s_pe"], 3)
                    tt(out=vnt[:, 2], in0=vnt[:, 1], in1=quad(3, w), op=ALU.add).then_inc(dl["s_dve"], 1)

                    def spread(h):
                        if h >= 2:
                            dve.wait_ge(dl["st"], h - 1)
                        tt(out=vm[h % 2][0:w], in0=bc(ml[s][0:w, h, :], 1, NB), in1=bc(sq[0:w, BLK_S, 0:w:NL], 2, BD), op=ALU.mult).then_inc(dl["vm"], 1)
                    dve.wait_ge(dl["s_act"], 2)
                    spread(0)
                    spread(1)
                    for h in range(BH):
                        dve.wait_ge(dl["st"], h + 1)
                        dve.wait_ge(dl["sd"], h + 1)
                        for b2 in range(2):
                            chain.mark(tt(out=ss0[:, 4 * b2:4 * b2 + 4, h, :], in0=ss0[:, 4 * b2:4 * b2 + 4, h, :],
                                          in1=quad(STATE_BANKS[h % 2] + b2), op=ALU.add))
                        chain.join()
                        dve.sem_inc(dl["su"], 1)
                        if h + 2 < BH:
                            spread(h + 2)
                if g + 1 < len(GROUPS):
                    seeds(GROUPS[g + 1])
                for n in group:
                    w, s = TILES[n][1], n % 2
                    dve.wait_ge(dl["o"], n + 1)
                    chain.link(tt(out=xi[s][0:w], in0=yv[s][0:w], in1=yv[s][0:w], op=ALU.mult))
                    chain.link(nc.vector.tensor_reduce(ost[0:w, s, 0, :], xi[s][0:w], axis=AX.X, op=ALU.add))
                    chain.link(nc.vector.tensor_scalar(ost[0:w, s, 1, :], ost[0:w, s, 0, :], 1.0 / BD, EPS, ALU.mult, ALU.add))
                    nc.vector.reciprocal(ost[0:w, s, 1, :], ost[0:w, s, 1, :]).then_inc(dl["ovar"], 1)
                for n in group:
                    w, s = TILES[n][1], n % 2
                    dve.wait_ge(dl["ort"], n + 1)
                    chain.link(tt(out=yv[s][0:w], in0=yv[s][0:w], in1=bc(ost[0:w, s, 1, :], 2, BD), op=ALU.mult))
                    tt(out=yv[s][0:w], in0=yv[s][0:w], in1=bz[0:w, n, :].rearrange("p (h e) -> p h e", h=BH), op=ALU.mult).then_inc(dl["og"], 1)

        def pool_mix(pool, chain):
            tt = nc.gpsimd.tensor_tensor
            pool.wait_ge(l2_done, 2 * BH + 1)
            pool.wait_ge(gates_dve, 3)
            for group in GROUPS:
                for n in group:
                    (t0, w), s = TILES[n], n % 2
                    pool.wait_ge(dl["eg"], n + 1)
                    if n < NT - 1:
                        tt(out=qd[s][:], in0=co[:, 0:BH, t0:t0 + w], in1=eg[s][:], op=ALU.mult).then_inc(dl["pf"], 1)
                    else:
                        tt(out=wq[:, :, :, 1, :], in0=co[:, 0:BH, t0:t0 + w].rearrange("p h (b l) -> p h b l", l=NL),
                           in1=eg[s][:, :, 0:w].rearrange("p h (b l) -> p h b l", l=NL), op=ALU.mult).then_inc(dl["pf"], 1)
                    pool.wait_ge(dl["sc"], n + 1)
                    tt(out=gcol[0:w, s, 3, :], in0=beta[0:w, n, :], in1=gcol[0:w, s, 2, :], op=ALU.mult).then_inc(dl["pf"], 1)
                    pool.wait_ge(dl["kq"], n + 1)
                    tt(out=sub(it[s], w), in0=sub(it[s], w), in1=bc(cum(n)[0:w, 0:w], 1, BH), op=ALU.mult).then_inc(dl["pf"], 1)
                for lv, n in level_steps(group):
                    w, s = TILES[n][1], n % 2
                    if lv == 1:
                        pool.wait_ge(dl["x0"], n + 1)
                    else:
                        pool.wait_ge(dl["y"], step_no[lv - 1, n] + 1)
                    nc.gpsimd.tensor_tensor(out=sub(ml[s], w), in0=sub(lt[s], w), in1=bc(sq[0:w, LEVEL0 + lv, 0:w], 1, BH),
                                            op=ALU.mult).then_inc(dl["ml"], 1)
            pool.wait_ge(dl["s_pe"], 1)
            for h in range(BH):
                tt(out=ss0[:, :, h, :], in0=ss0[:, :, h, :], in1=bc(eg[0][:, h, NL - 1:NB * NL:NL], 2, BD), op=ALU.mult).then_inc(dl["sd"], 1)
            pool_sample(pool, chain)

        def sp_delta(sp):
            sp.wait_ge(l2_done, 2 * BH + 1)
            sp.dma_start(ss0[:], s0.rearrange("b h k v -> k (b h) v")).then_inc(S_("states_in"), 16)
            sp.wait_ge(dl["s"], NT - 1)
            sp.dma_start(s_p.rearrange("h k v -> k h v"), s_cur[:]).then_inc(kv_out, 16)
            sp.wait_ge(dl["st"], BH)
            sp.wait_ge(dl["sd"], BH)
            load_cached(sp, 0, kc)
            load_cached(sp, 1, kc)
            sp.wait_ge(dl["su"], BH)
            sp.dma_start(s_s.rearrange("b h k v -> k (b h) v"), ss0[:]).then_inc(kv_out, 16)
        QROWS = NB * NL
        keys_in = [S_(f"cached_keys_in{s}") for s in range(2)]
        values_in = [S_(f"cached_values_in{s}") for s in range(2)]
        sa = {n: S_("sample_" + n) for n in "q kt0 kt1 kta ktv scores masked exp norm turned pt out os used".split()}

        def score_banks(b):
            return bank[2 + 4 * (b % 2)][0:QROWS, :], bank[3 + 4 * (b % 2)][0:QROWS, :]

        def load_cached(sp, b, cache):
            s = b % 2
            old, new, done = (ks[s][:, 0:OLD_TILES, :], ks[s][:, OLD_TILES:, :], keys_in[s]) if cache is kc else \
                (vs_old[s][:], vs_new[s][:], values_in[s])
            groups = cache[b].rearrange("(j g s) c -> j g s c", g=32, s=16)
            for j in range(OLD_TILES):
                sp.dma_start(old[:, j, :], groups[j, :, 0:4, :]).then_inc(done, 16)
            sp.dma_start(new, cache[b, PAST - NEW_TILES * P:PAST, :].rearrange("(j p) c -> p j c", p=P)).then_inc(done, 16)

        def sp_sample(sp):
            sp.wait_ge(dl["cat"], NT)
            for b in range(2):
                load_cached(sp, b, vc)
            sp.wait_ge(kv_out, 16 * (NKV + 2))
            sp.dma_start(w_raw[0][:], wout[0]).then_inc(w_in[0], 16)
            for b in range(2, NB):
                sp.wait_ge(sa["kt0"], PAIRS * (b - 1))
                sp.wait_ge(sa["kt1"], PAIRS * (b - 1))
                load_cached(sp, b, kc)
                sp.wait_ge(sa["used"], b - 1)
                load_cached(sp, b, vc)
            sp.wait_ge(sa["scores"], NB)
            sp.dma_start(w_raw[1][:], wout[1]).then_inc(w_in[1], 16)

        def pe_sample(pe):
            pe.wait_ge(dl["cat"], NT)
            pe.wait_ge(dl["su"], BH)

            def turn_keys(b):
                s = b % 2
                pe.wait_ge(keys_in[s], 16 * 4 * (b // 2 + 1))
                for p in range(PAIRS):
                    q = b * PAIRS + p
                    if q:
                        pe.wait_ge(sa["kta"], q)
                    for j in range(4):
                        last = nc.tensor.transpose(quad(0)[:, j, :], ks[s][:, j, p * P:(p + 1) * P], ident)
                    last.then_inc(sa["kt0"], 1)
                    if q:
                        pe.wait_ge(sa["ktv"], q)
                    for j in range(4, KTILES):
                        last = nc.tensor.transpose(quad(1)[:, j - 4, :], ks[s][:, j, p * P:(p + 1) * P], ident)
                    last.then_inc(sa["kt1"], 1)

            def scores(b):
                pe.wait_ge(sa["kta"], PAIRS * (b + 1))
                pe.wait_ge(sa["ktv"], PAIRS * (b + 1))
                if b >= 2:
                    pe.wait_ge(sa["masked"], b - 1)
                lo, hi = score_banks(b)
                for p in range(PAIRS):
                    nc.tensor.matmul(lo, qbd[:, b, p, :], kt_lo[:, p, :], start=p == 0, stop=p == PAIRS - 1)
                for p in range(PAIRS):
                    nc.tensor.matmul(hi[:, 0:CACHED - 512], qbd[:, b, p, :], kt_hi[:, p, :], start=p == 0, stop=p == PAIRS - 1)
                for p in range(PAIRS):
                    last = nc.tensor.matmul(hi[:, CACHED - 512:CACHED - 512 + QROWS], qbd[:, b, p, :], qkt[:, PAIRS + p, SEQ:TOK],
                                            start=p == 0, stop=p == PAIRS - 1)
                last.then_inc(sa["scores"], 1)

            turn_keys(0)
            pe.wait_ge(sa["q"], 1)
            scores(0)
            for b in range(NB):
                s = b % 2
                if b + 1 < NB:
                    turn_keys(b + 1)
                    scores(b + 1)
                pe.wait_ge(sa["norm"], b + 1)
                if b:
                    pe.wait_ge(sa["pt"], b)
                pts_bank = bank[4][:, 0:(KTILES + 1) * QROWS].rearrange("p (j q) -> p j q", q=QROWS)
                for j in range(KTILES):
                    nc.tensor.transpose(pts_bank[:, j, :], sss[s][:, j * P:(j + 1) * P], ident[0:QROWS, 0:QROWS])
                nc.tensor.matmul(pts_bank[0:QROWS, KTILES, :], sss[s][:, CACHED:CACHED + QROWS], ident[0:QROWS, 0:QROWS],
                                 start=True, stop=True).then_inc(sa["turned"], 1)
                pe.wait_ge(sa["pt"], b + 1)
                pe.wait_ge(values_in[s], 16 * 4 * (b // 2 + 1))
                if b:
                    pe.wait_ge(sa["os"], b)
                for p in range(PAIRS):
                    out = bank[5][:, 8 * p:8 * p + 8]
                    for j in range(KTILES):
                        v = vs_old[s][:, j] if j < OLD_TILES else vs_new[s][:, j - OLD_TILES]
                        nc.tensor.matmul(out, v[:, p * P:(p + 1) * P], pts[:, j, 8 * p:8 * p + 8], start=j == 0, stop=False)
                    last = nc.tensor.matmul(out, av[0:QROWS, NT - 1, p * P:(p + 1) * P], pts[0:QROWS, KTILES, 8 * p:8 * p + 8],
                                            start=False, stop=True)
                last.then_inc(sa["out"], 1)
                pe.wait_ge(sa["out"], b + 1)
                pe.sem_inc(sa["used"], 1)

        def dve_sample(dve, chain):
            chain.link(nc.vector.memset(qbd[:], 0.0))
            for h in range(AH):
                r = slice(AD * (h % 2), AD * (h % 2) + AD)
                chain.mark(nc.vector.tensor_copy(qbd[r, :, h // 2, h * NL:(h + 1) * NL],
                                                 qkt[r, h // 2, SEQ:TOK].rearrange("p (b l) -> p b l", b=NB)))
            chain.join()
            dve.sem_inc(sa["q"], 1)

            def keys(b):
                if b:
                    dve.wait_ge(sa["scores"], b)
                for p in range(PAIRS):
                    dve.wait_ge(sa["kt1"], b * PAIRS + p + 1)
                    nc.vector.tensor_copy(kt_hi[:, p, :], bank[1][:, 0:CACHED - 512]).then_inc(sa["ktv"], 1)

            keys(0)
            for b in range(NB):
                s = b % 2
                if b + 1 < NB:
                    keys(b + 1)
                dve.wait_ge(sa["scores"], b + 1)
                if b >= 2:
                    dve.wait_ge(sa["turned"], b - 1)
                m = 512
                lo, hi = score_banks(b)
                parts = ((0, lo, lncs[:, 0:m]),
                         (m, hi[:, 0:CACHED - m], lncs[:, m:CACHED]),
                         (CACHED, hi[:, CACHED - m:CACHED - m + QROWS], lncs[:, CACHED + b * QROWS:CACHED + (b + 1) * QROWS]))
                for x, (c0, src, lnc) in enumerate(parts):
                    chain.mark(nc.vector.tensor_tensor_reduce(
                        out=sss[s][:, c0:c0 + src.shape[1]], in0=src, in1=lnc, scale=1.0, scalar=NEG, op0=ALU.add, op1=ALU.max,
                        accum_out=sstat[:, s, x:x + 1]))
                chain.join()
                nc.vector.tensor_reduce(sstat[:, s, 3:4], sstat[:, s, 0:3], axis=AX.X, op=ALU.max, negate=True).then_inc(sa["masked"], 1)
                dve.wait_ge(sa["exp"], b + 1)
                chain.link(nc.vector.reciprocal(sstat[:, s, 5:6], sstat[:, s, 4:5]))
                nc.vector.tensor_scalar(sss[s][:], sss[s][:], sstat[:, s, 5:6], None, ALU.mult).then_inc(sa["norm"], 1)

        def act_sample(act, chain):
            def keys(b):
                if b:
                    act.wait_ge(sa["scores"], b)
                for p in range(PAIRS):
                    act.wait_ge(sa["kt0"], b * PAIRS + p + 1)
                    nc.scalar.activation(kt_lo[:, p, :], bank[0][:], ACT.Copy).then_inc(sa["kta"], 1)

            keys(0)
            for b in range(NB):
                s = b % 2
                if b + 1 < NB:
                    keys(b + 1)
                act.wait_ge(sa["masked"], b + 1)
                nc.scalar.activation(sss[s][:], sss[s][:], ACT.Exp, bias=sstat[:, s, 3:4], accum_out=sstat[:, s, 4:5]).then_inc(sa["exp"], 1)
                if b == 3:
                    split_weights(act, NW1)
                act.wait_ge(sa["turned"], b + 1)
                if b:
                    act.wait_ge(sa["out"], b)
                pts_bank = bank[4][:, 0:(KTILES + 1) * QROWS].rearrange("p (j q) -> p j q", q=QROWS)
                chain.mark(nc.scalar.activation(pts[:, 0:KTILES, :], pts_bank[:, 0:KTILES, :], ACT.Copy))
                chain.link(nc.scalar.activation(pts[0:QROWS, KTILES, :], pts_bank[0:QROWS, KTILES, :], ACT.Copy))
                act.sem_inc(sa["pt"], 1)
                act.wait_ge(sa["out"], b + 1)
                c = slice(SEQ + b * NL, SEQ + (b + 1) * NL)
                o4 = bank[5][:, 0:8 * PAIRS].rearrange("p (i q) -> p i q", q=8)
                chain.mark(nc.scalar.activation(cat[0:AD, 0:PAIRS, c], o4[0:AD, :, 0:NL], ACT.Copy))
                chain.link(nc.scalar.activation(cat[AD:P, 0:PAIRS, c], o4[AD:P, :, NL:2 * NL], ACT.Copy))
                act.sem_inc(sa["os"], 1)

        def pool_sample(pool, chain):
            pool_ffn(pool, chain)

        NW_OUT, NW_PQ = 4, 8
        NW2 = NW1 + NW_OUT
        NW3 = NW2 + NW_PQ
        ff = {n: S_("ffn_" + n) for n in (
            "cat_hi cat_lo h_used pq pq_evac sub sub_evac sub_free "
            "top_exp top_expd picks picks_turned picks_t cols ones gate_mm gate_bank ones_raw").split()}
        gate_out = [S_("gate_out0"), S_("gate_out1")]
        CAT_PARTS = 4
        CAT_COLS = TOK // CAT_PARTS
        QUADS = GT // 4
        assert GB * QUADS % HOT == 0

        def split_weights(act, k):
            act.wait_ge(w_in[k % 2], 16 * (k // 2 + 1))
            act.wait_ge(w_used, k - 1)
            nc.scalar.activation(w_hi[:, k % 2], w_raw[k % 2][:], ACT.Copy).then_inc(w_hi_ready, 1)

        def sp_ffn(sp):
            sp.wait_ge(sa["used"], NB)
            for k in range(NW1 + 2, NW3):
                sp.wait_ge(w_hi_ready, k - 1)
                sp.wait_ge(w_lo_ready, k - 1)
                src = wout[k - NW1] if k < NW2 else wpq[k - NW2]
                sp.dma_start(w_raw[k % 2][:], src).then_inc(w_in[k % 2], 16)
                if k == NW1 + 2:
                    sp.wait_ge(ff["cat_lo"], CAT_PARTS)
                    for t in range(NT):
                        x = x_p[t * P:(t + 1) * P, :] if t < NT - 1 else x_s
                        sp.dma_start(X[0:TILES[t][1], t, :], x).then_inc(x_in[t], 16)
                    sp.dma_start(nmix_b[:], nffn.partition_broadcast(P)).then_inc(consts_in, 16)
            sp.wait_ge(w_used, NW3)
            sp.dma_start(skt_s[:], skt).then_inc(consts_in, 16)
            sp.wait_ge(xs_ready, 2 * NT)
            for s in range(2):
                load_u(sp, 0, s)
            for t in range(NT):
                with sp.Fori(0, WINDOW[t]) as i:
                    for s in range(2):
                        feed_pre(sp, i + WINDOW0[t], s)
            with sp.Fori(0, GBLOCKS // GB) as i:
                for b in range(GB):
                    for s in range(2):
                        feed_pre(sp, i * GB + (GATE_X0 + b), s)
            for x in range(AHEAD // 2 - LAST_AHEAD, AHEAD // 2):
                for s in range(2):
                    feed_pre(sp, x, s)
                if x == AHEAD // 2 - LAST_AHEAD:
                    for b in range(2):
                        sp.wait_ge(gate_out[b], 16 * (GBLOCKS // 2) + 16)
                    for j in range(2):
                        load_v(sp, 0, j)
            for s in range(2):
                sp.wait_ge(act_out[s], 16 * (AHEAD // 2) + 16)
            sp_dense(sp)

        def pe_ffn(pe, product):
            pe.wait_ge(sa["os"], NB)
            uses = 0
            for k in range(NW1, NW2):
                pe.wait_ge(w_lo_ready, k + 1)
                for t in range(NT):
                    if uses >= 4:
                        pe.wait_ge(ff["h_used"], uses - 3)
                    tok = token_columns(t)
                    pe.wait_ge(ff["cat_lo"], -(-tok.stop // CAT_COLS))
                    product(bank[2 + uses % 4][:, 0:WC],
                            [(cat_hi[:, c, tok], cat_lo[:, c, tok], w_hi[:, k % 2, c, :], w_lo[:, k % 2, c, :])
                             for c in range(CH)]).then_inc(proj_ready, 1)
                    uses += 1
                pe.wait_ge(proj_ready, READY1 + uses)
                pe.sem_inc(w_used, 1)
            for m in range(2 * NT):
                t0, w = TILES[m // 2]
                pe.wait_ge(xs_ready, NT + m // 2 + 1)
                if m >= 2:
                    pe.wait_ge(xn_lo_ready, 2 * NT + m - 1)
                for j in range(4):
                    c = 4 * (m % 2) + j
                    last = nc.tensor.transpose(quad(m % 2, w)[:, j, :], hs[0:w, (m // 2) % 2, c * P:(c + 1) * P], ident[0:w, 0:w])
                last.then_inc(xs_turned, 1)
            pe.wait_ge(xn_lo_ready, 4 * NT)
            pe.wait_ge(ff["h_used"], NW_OUT * NT)
            uses = 0
            for c in range(2 * PH):
                k = NW2 + c // 2
                pe.wait_ge(w_lo_ready, k + 1)
                wcols = slice((c % 2) * P, (c % 2) * P + P)
                for h in range(2):
                    if uses >= 4:
                        pe.wait_ge(ff["pq_evac"], uses - 3)
                    cols = slice(h * HALF, (h + 1) * HALF)
                    product(bank[2 + uses % 4][:, 0:HALF],
                            [(w_hi[:, k % 2, i, wcols], w_lo[:, k % 2, i, wcols], hn_hi[:, i, cols], hn_lo[:, i, cols])
                             for i in range(CH)]).then_inc(ff["pq"], 1)
                    uses += 1
                if c % 2:
                    pe.wait_ge(ff["pq"], uses)
                    pe.sem_inc(w_used, 1)
            pe.wait_ge(ff["pq_evac"], uses)
            pe.wait_ge(consts_in, 16 * (NCONST + 2))

            def half_scores(t):
                t0, w = TILES[t]
                for g in range(4):
                    q = 4 * t + g
                    if q >= 2:
                        pe.wait_ge(ff["sub_evac"], q - 1)
                    for j in range(4):
                        c = 4 * g + j
                        last = nc.tensor.matmul(quad(4 + g % 2)[0:w, j, :], qt[:, c, t0:t0 + w], skt_s[:, c % 2, :], start=True, stop=True)
                    last.then_inc(ff["sub"], 1)

            def turn_picks(t):
                w = TILES[t][1]
                pe.wait_ge(ff["picks"], t + 1)
                if t:
                    pe.wait_ge(ff["picks_t"], t)
                for j in range(3):
                    last = nc.tensor.transpose(bank[6][:, j * P:j * P + w], picks[0:w, j, :], ident[0:w, 0:w])
                last.then_inc(ff["picks_turned"], 1)

            pe.sem_inc(dn["pre"], 4)
            half_scores(0)
            for t in range(NT):
                if t + 1 < NT:
                    half_scores(t + 1)
                for s in range(2):
                    pre(pe, product, WINDOW0[t], s)
                if t:
                    turn_picks(t - 1)
                with pe.Fori(1, WINDOW[t]) as i:
                    for s in range(2):
                        pre(pe, product, i + WINDOW0[t], s)
            turn_picks(NT - 1)
            with pe.Fori(0, GBLOCKS // GB) as i:
                for n in range(GB * QUADS):
                    b, k = n // QUADS, n % QUADS
                    pe.wait_ge(ff["ones"], i * (GB * QUADS) + n + 1)
                    pe.wait_ge(ff["gate_bank"], i * (GB * QUADS) + n + 1)
                    for j in range(4):
                        last = nc.tensor.matmul(quad(4 + n % 2)[:, j, :], one2[n % HOT][:, j, :], one1[n % HOT][:, j, :], start=True, stop=True)
                    last.then_inc(ff["gate_mm"], 1)
                    if k in PRE_AFTER:
                        half = PRE_AFTER.index(k)
                        pre(pe, product, i * GB + (GATE_X0 + b), half // 2, (half % 2,))
            for x in range(AHEAD // 2 - LAST_AHEAD, AHEAD // 2):
                for s in range(2):
                    pre(pe, product, x, s)
            pe_dense(pe, product)

        def act_ffn(act, chain):
            act.wait_ge(sa["used"], NB)
            for i in range(CAT_PARTS):
                cols = slice(i * CAT_COLS, (i + 1) * CAT_COLS)
                nc.scalar.activation(cat_hi[:, :, cols], cat[:, :, cols], ACT.Copy).then_inc(ff["cat_hi"], 1)

            for k in range(NW1 + 1, NW2 + 1):
                split_weights(act, k)
            for t, (t0, w) in enumerate(TILES):
                act.wait_ge(ff["h_used"], (NW_OUT - 1) * NT + t + 1)
                if t:
                    act.wait_ge(ssq_ready, NT + t)
                nc.scalar.activation(tmp1[0:w, :], X[0:w, t, :], ACT.Square, accum_out=stat[0:w, 2, t:t + 1]).then_inc(ssq_ready, 1)
            act.wait_ge(var_ready, 2)
            nc.scalar.activation(stat[:, 3, :], stat[:, 3, :], ACT.Sqrt).then_inc(rstd_ready, 1)
            for m in range(2 * NT):
                t0, w = TILES[m // 2]
                act.wait_ge(xs_turned, 2 * NT + m + 1)
                nc.scalar.activation(hn_hi[:, 4 * (m % 2):4 * (m % 2) + 4, t0:t0 + w], quad(m % 2, w), ACT.Copy).then_inc(xn_hi_ready, 1)
            split_weights(act, NW2 + 1)
            uses = 0
            for c in range(2 * PH):
                for h in range(2):
                    act.wait_ge(ff["pq"], uses + 1)
                    nc.scalar.activation(qt[:, c, h * HALF:(h + 1) * HALF], bank[2 + uses % 4][:, 0:HALF], ACT.Copy).then_inc(ff["pq_evac"], 1)
                    uses += 1
                if c % 2 and NW2 + c // 2 + 2 < NW3:
                    split_weights(act, NW2 + c // 2 + 2)

            def scores_out(t):
                w = TILES[t][1]
                if t >= 2:
                    act.wait_ge(ff["sub_free"], t - 1)
                for g in range(4):
                    act.wait_ge(ff["sub"], 4 * t + g + 1)
                    nc.scalar.activation(sub_s[t % 2][0:w, 4 * g:4 * g + 4, :], quad(4 + g % 2)[0:w], ACT.Copy).then_inc(ff["sub_evac"], 1)
            act.sem_inc(dn["gelu"], 4)
            scores_out(0)
            split_u(act, 0, 0)
            for t, (t0, w) in enumerate(TILES):
                if t + 1 < NT:
                    scores_out(t + 1)
                with act.Fori(0, WINDOW[t]) as i:
                    for s in range(2):
                        gelu_ahead(act, i + WINDOW0[t], s)
                act.wait_ge(ff["top_exp"], t + 1)
                nc.scalar.activation(bv[0:w], bv[0:w], ACT.Exp).then_inc(ff["top_expd"], 1)
            act.sem_inc(ff["gate_bank"], 2)
            with act.Fori(0, GBLOCKS // GB) as i:
                for b in range(GB):
                    act.wait_ge(gate_out[b % 2], i * (8 * GB) + (16 * (b // 2) + 16))
                    for k in range(QUADS):
                        n = b * QUADS + k
                        act.wait_ge(ff["gate_mm"], i * (GB * QUADS) + (n + 1 + HOT))
                        nc.scalar.activation(gst[b % 2][:, :, 4 * k:4 * k + 4], quad(4 + n % 2).rearrange("p t a -> p a t"), ACT.Copy)\
                            .then_inc(ff["gate_bank"], 1)
                        if k in PRE_AFTER:
                            half = PRE_AFTER.index(k)
                            gelu_ahead(act, i * GB + (GATE_X0 + b), half // 2, (half % 2,))
                    act.wait_ge(ff["gate_bank"], i * (GB * QUADS) + (2 + (b + 1) * QUADS))
                    act.dma_start(gates_dram[bass.ds(i * GB + b, 1)].rearrange("o p a t -> p (o a t)"), gst[b % 2][:]).then_inc(gate_out[b % 2], 16)
            for x in range(AHEAD // 2 - LAST_AHEAD, AHEAD // 2):
                for s in range(2):
                    gelu_ahead(act, x, s)
            act_dense(act, chain)

        def dve_ffn(dve, chain):
            tt, ts = nc.vector.tensor_tensor, nc.vector.tensor_scalar
            for i in range(CAT_PARTS):
                cols = slice(i * CAT_COLS, (i + 1) * CAT_COLS)
                dve.wait_ge(ff["cat_hi"], i + 1)
                tt(out=cat_lo[:, :, cols], in0=cat[:, :, cols], in1=cat_hi[:, :, cols].bitcast(F32), op=ALU.subtract).then_inc(ff["cat_lo"], 1)
            for t in range(NT):
                dve.wait_ge(x_in[t], 32)
            uses = 0
            for k in range(NW_OUT):
                for t, (t0, w) in enumerate(TILES):
                    dve.wait_ge(proj_ready, READY1 + uses + 1)
                    x = X[0:w, t, k * WC:(k + 1) * WC]
                    tt(out=x, in0=x, in1=bank[2 + uses % 4][rows(t), 0:WC], op=ALU.add).then_inc(ff["h_used"], 1)
                    uses += 1
            dve.wait_ge(ssq_ready, 2 * NT)
            chain.link(ts(stat[:, 3, :], stat[:, 2, :], 1.0 / D, EPS, ALU.mult, ALU.add))
            nc.vector.reciprocal(stat[:, 3, :], stat[:, 3, :]).then_inc(var_ready, 1)
            dve.wait_ge(rstd_ready, 2)
            dve.wait_ge(consts_in, 16 * (NCONST + 1))

            def scale_tokens(t):
                w = TILES[t][1]
                if t >= 2:
                    dve.wait_ge(xs_turned, 2 * NT + 2 * (t - 1))
                nc.vector.scalar_tensor_tensor(out=hs[0:w, t % 2, :], in0=X[0:w, t, :], scalar=stat[0:w, 3, t:t + 1],
                                               in1=nmix_b[0:w, :], op0=ALU.mult, op1=ALU.mult).then_inc(xs_ready, 1)
            scale_tokens(0)
            for m in range(2 * NT):
                t0, w = TILES[m // 2]
                if m % 2 == 0 and m // 2 + 1 < NT:
                    scale_tokens(m // 2 + 1)
                hi = hn_hi[:, 4 * (m % 2):4 * (m % 2) + 4, t0:t0 + w].bitcast(F32)
                dve.wait_ge(xn_hi_ready, 2 * NT + m + 1)
                tt(out=hn_lo[:, 4 * (m % 2):4 * (m % 2) + 4, t0:t0 + w], in0=quad(m % 2, w), in1=hi, op=ALU.subtract).then_inc(xn_lo_ready, 1)

            def top16(w, vals, idx, src, n):
                for j in range(n):
                    chain.mark(nc.vector.max(vals(j)[:, 0:8], src(j)))
                chain.join()
                for j in range(n):
                    chain.mark(nc.vector.max_index(idx(j)[:, 0:8], vals(j)[:, 0:8], src(j)))
                chain.join()
                for j in range(n):
                    chain.mark(nc.vector.match_replace(src(j), vals(j)[:, 0:8], src(j), NEG))
                chain.join()
                for j in range(n):
                    chain.mark(nc.vector.max(vals(j)[:, 8:16], src(j)))
                chain.join()
                for j in range(n):
                    chain.mark(nc.vector.max_index(idx(j)[:, 8:16], vals(j)[:, 8:16], src(j)))
                chain.join()

            def keep_picks(t):
                t0, w = TILES[t]
                dve.wait_ge(ff["picks_turned"], t + 1)
                for j in range(3):
                    chain.mark(nc.vector.tensor_copy(picks_t[:, j, t0:t0 + w], bank[6][:, j * P:j * P + w]))
                chain.join()
                dve.sem_inc(ff["picks_t"], 1)

            for t, (t0, w) in enumerate(TILES):
                sub_t = sub_s[t % 2]
                dve.wait_ge(ff["sub_evac"], 4 * (t + 1))
                top16(w, lambda j: tv[0:w, j, :], lambda j: ti[0:w, j, :], lambda j: sub_t[0:w, j, :], 2 * PH)
                dve.sem_inc(ff["sub_free"], 1)
                if t:
                    keep_picks(t - 1)
                chain.mark(nc.vector.tensor_copy(tif[0:w], ti[0:w]))
                tv4 = tv[0:w].rearrange("p (h c) k -> p h c k", c=2)
                chain.link(tt(out=cand[0:w], in0=bc(tv4[:, :, 0, :], 3, TOPK), in1=bc(tv4[:, :, 1, :], 2, TOPK), op=ALU.add))
                top16(w, lambda j: bv[0:w, j, :], lambda j: bi[0:w, j, :],
                      lambda j: cand[0:w, j].rearrange("p a b -> p (a b)"), PH)
                chain.mark(nc.vector.tensor_copy(gsum[0:w, 0, :], bv[0:w, :, 0]))
                chain.mark(ts(bhl[0:w, 0], bi[0:w], 4, None, ALU.logical_shift_right))
                chain.link(ts(bhl[0:w, 1], bi[0:w], TOPK - 1, None, ALU.bitwise_and))
                tt(out=bv[0:w], in0=bv[0:w], in1=bc(gsum[0:w, 0, :], 2, TOPK), op=ALU.subtract).then_inc(ff["top_exp"], 1)
                chain.link(nc.vector.tensor_copy(bhlf[0:w], bhl[0:w]))
                tif4 = tif[0:w].rearrange("p (h c) k -> p h c k", c=2)
                eq3 = eq[0:w].rearrange("p h k a -> p (h k) a")
                for c in range(2):
                    chain.link(tt(out=eq3, in0=bc(bhlf[0:w, c].rearrange("p h k -> p (h k)"), 2, TOPK),
                                  in1=bc(asc[0:w, 0:TOPK], 1, PH * TOPK), op=ALU.is_equal))
                    chain.link(tt(out=eq[0:w], in0=eq[0:w], in1=bc(tif4[:, :, c, :], 2, TOPK), op=ALU.mult))
                    chain.link(nc.vector.tensor_reduce(picks[0:w, c, :], eq3, axis=AX.X, op=ALU.add))
                dve.wait_ge(ff["top_expd"], t + 1)
                chain.link(nc.vector.tensor_reduce(gsum[0:w, 0, :], bv[0:w], axis=AX.X, op=ALU.add))
                chain.link(nc.vector.reciprocal(gsum[0:w, 1, :], gsum[0:w, 0, :]))
                tt(out=picks[0:w, 2, :].rearrange("p (h k) -> p h k", k=TOPK), in0=bv[0:w], in1=bc(gsum[0:w, 1, :], 2, TOPK),
                   op=ALU.mult).then_inc(ff["picks"], 1)
            keep_picks(NT - 1)
            with dve.Fori(0, GBLOCKS // GB) as i:
                for b in range(GB):
                    nc.vector.tensor_copy(cols_s[:, b % 2], picks_t[:, :, bass.ds(i * (GB * GT) + b * GT, GT)]).then_inc(ff["cols"], 1)
                    dve.wait_ge(ff["cols"], i * GB + (b + 1))
                    for k in range(QUADS):
                        n = b * QUADS + k
                        dve.wait_ge(ff["gate_mm"], i * (GB * QUADS) + (n + 1))
                        tt(out=one2[n % HOT][:], in0=bc(asc, 1, 4), in1=bc(cols_s[:, b % 2, 1, 4 * k:4 * k + 4], 2, PK), op=ALU.is_equal)
                        tt(out=one1[n % HOT][:], in0=bc(asc, 1, 4), in1=bc(cols_s[:, b % 2, 0, 4 * k:4 * k + 4], 2, PK), op=ALU.is_equal)\
                            .then_inc(ff["ones_raw"], 1)
            dve_dense(dve, chain)

        def pool_ffn(pool, chain):
            for k in range(NW1, NW3):
                pool.wait_ge(w_hi_ready, k + 1)
                pool.wait_ge(w_used, k - 1)
                nc.gpsimd.tensor_tensor(out=w_lo[:, k % 2], in0=w_raw[k % 2][:], in1=w_hi[:, k % 2].bitcast(F32),
                                        op=ALU.subtract).then_inc(w_lo_ready, 1)
            pool.sem_inc(ff["gate_mm"], HOT)
            for s in range(2):
                pool.sem_inc(gate_out[s], 16)
                pool.sem_inc(act_out[s], 16)
            lo_u(pool, 0, 0)
            for t in range(NT):
                with pool.Fori(0, WINDOW[t]) as i:
                    for s in range(2):
                        lo_u(pool, i + (WINDOW0[t] + s), 1 - s)
            with pool.Fori(0, GBLOCKS // GB) as i:
                for b in range(GB):
                    for k in range(QUADS):
                        n = b * QUADS + k
                        pool.wait_ge(ff["ones_raw"], i * (GB * QUADS) + (n + 1))
                        nc.gpsimd.tensor_tensor(out=one1[n % HOT][:], in0=one1[n % HOT][:], in1=bc(cols_s[:, b % 2, 2, 4 * k:4 * k + 4], 2, PK),
                                                op=ALU.mult).then_inc(ff["ones"], 1)
                        if k in (PRE_AFTER[1], PRE_AFTER[3]):
                            s = PRE_AFTER.index(k) // 2
                            lo_u(pool, i * GB + (GATE_X0 + b + s), 1 - s)
            for x in range(AHEAD // 2 - LAST_AHEAD, AHEAD // 2):
                for s in range(2):
                    lo_u(pool, x + s, 1 - s)
            pool_dense(pool, chain)

        READY1 = 8 * NT + 2 + 2 * 3 * BH

        dn = {n: S_("dense_" + n) for n in "uhi ulo vhi vlo pre gelu mul ahi alo acc outs yturn yadd".split()}
        u_in = [S_(f"u_in{s}") for s in range(2)]
        v_in = [S_(f"v_in{s}") for s in range(2)]
        g_in = [S_(f"g_in{s}") for s in range(2)]
        act_out = [S_(f"act_out{s}") for s in range(2)]
        act_in = [S_(f"act_in{s}") for s in range(2)]
        PAIRS_E = PK // 2
        ITERS = PAIRS_E // 2 - 1
        LAST_AHEAD = 1
        WINDOW = [5, 4, 4, 5, 5]
        WINDOW0 = [sum(WINDOW[:t]) for t in range(NT)]
        GATE_X0 = sum(WINDOW)
        PRE_AFTER = [QUADS // 4 * (n + 1) for n in range(4)]
        assert GATE_X0 + GBLOCKS + LAST_AHEAD == AHEAD // 2
        OUT_TILES = 2 * CH
        def one(e):
            return bass.ds(e, 1)

        def load_u(sp, x, s):
            sp.dma_start(u_raw[s][:], eu[one(2 * x + s)].rearrange("o p c n -> p (o c) n")).then_inc(u_in[s], 16)

        def feed_pre(sp, x, s):
            sp.wait_ge(dn["ulo"], 2 * x + (s + 1))
            load_u(sp, x + 1, s)
            sp.wait_ge(dn["gelu"], 4 * x + (2 * s + 6))
            sp.dma_start(acts_dram[one(2 * x + s)].rearrange("o p t -> p (o t)"), act_c[s][:]).then_inc(act_out[s], 16)

        def pre(pe, product, x, s, halves=(0, 1)):
            pe.wait_ge(dn["ulo"], 2 * x + (s + 1))
            pe.wait_ge(dn["gelu"], 4 * x + (2 * s + 2))
            for h in halves:
                cols = slice(h * HALF, (h + 1) * HALF)
                product(bank[2 * s + h][:, 0:HALF],
                        [(u_hi[s][:, c, :], u_lo[s][:, c, :], hn_hi[:, c, cols], hn_lo[:, c, cols]) for c in range(CH)])\
                    .then_inc(dn["pre"], 1)

        def split_u(act, x, s):
            act.wait_ge(u_in[s], 16 * x + 16)
            act.wait_ge(dn["pre"], 4 * x + (2 * s + 2))
            nc.scalar.activation(u_hi[s][:], u_raw[s][:], ACT.Copy).then_inc(dn["uhi"], 1)

        def split_next_u(act, x, s):
            split_u(act, x if s == 0 else x + 1, 1 - s)

        def gelu(act, x, s, halves=(0, 1)):
            for h in halves:
                act.wait_ge(dn["pre"], 4 * x + (2 * s + h + 5))
                nc.scalar.activation(act_c[s][:, h * HALF:(h + 1) * HALF], bank[2 * s + h][:, 0:HALF], ACT.Gelu).then_inc(dn["gelu"], 1)

        def gelu_ahead(act, x, s, halves=(0, 1)):
            if 0 in halves:
                split_next_u(act, x, s)
                act.wait_ge(act_out[s], 16 * x + 16)
            gelu(act, x, s, halves)

        def lo_u(pool, x, s):
            pool.wait_ge(dn["uhi"], 2 * x + (s + 1))
            nc.gpsimd.tensor_tensor(out=u_lo[s][:], in0=u_raw[s][:], in1=u_hi[s][:].bitcast(F32), op=ALU.subtract).then_inc(dn["ulo"], 1)

        def load_v(sp, g, j):
            sp.dma_start(v_raw[j][:], ev[one(2 * g + j)].rearrange("o p n -> p (o n)")).then_inc(v_in[j], 16)

        def sp_dense(sp):
            def load_weights(g, s):
                sp.dma_start(gin[s][:], gates_dram[:, :, bass.ds(2 * g, 2), :].rearrange("b p a t -> p b (a t)")).then_inc(g_in[s], 16)
                sp.dma_start(act_l[s][:], acts_dram[one(g)].rearrange("o p t -> p (o t)")).then_inc(act_in[s], 16)

            load_weights(0, 0)
            load_weights(1, 1)
            with sp.Fori(0, ITERS) as i:
                for s in range(2):
                    for j in range(2):
                        sp.wait_ge(dn["vlo"], i * 4 + (2 * s + j + 1))
                        load_v(sp, i * 2 + (s + 1), j)
                    sp.wait_ge(dn["ulo"], i * 2 + (AHEAD + s + 1))
                    load_u(sp, i + (AHEAD // 2 + 1), s)
                    sp.wait_ge(dn["alo"], i * 4 + (2 * s + 2 + 4))
                    load_weights(i * 2 + (s + 2), s)
            for j in range(2):
                sp.wait_ge(dn["vlo"], PK - 3 + j)
                load_v(sp, PAIRS_E - 1, j)
            for t, (t0, w) in enumerate(TILES):
                sp.wait_ge(dn["yadd"], 2 * (t + 1))
                dst = y_p[t0:t0 + w, :] if t < NT - 1 else y_s
                sp.dma_start(dst, X[0:w, t, :]).then_inc(out_done, 16)
            sp.wait_ge(out_done, 16 * (1 + 2 * COPIES + NT))
            sp.wait_ge(kv_out, 16 * (NKV + 2))

        def pe_dense(pe, product):
            def outs(g, s):
                pe.wait_ge(dn["alo"], 2 * g + (2 + 4))
                pe.wait_ge(dn["vlo"], 2 * g + 2)
                for d in range(CH):
                    for h in range(2):
                        x = 2 * d + h
                        cols, dc = slice(h * HALF, (h + 1) * HALF), slice(d * P, (d + 1) * P)
                        pe.wait_ge(dn["acc"], OUT_TILES * g + (x + 1))
                        product(bank[4 + x % 4][:, 0:HALF],
                                [(v_hi[2 * s + j][:, dc], v_lo[2 * s + j][:, dc], a_hi[2 * s + j][:, cols], a_lo[2 * s + j][:, cols])
                                 for j in range(2)]).then_inc(dn["outs"], 1)

            pe.sem_inc(dn["outs"], 2 * OUT_TILES)
            pre(pe, product, AHEAD // 2, 0)
            pe.wait_ge(ff["gate_bank"], GBLOCKS * QUADS + 2)
            with pe.Fori(0, ITERS) as i:
                pre(pe, product, i + AHEAD // 2, 1)
                outs(i * 2, 0)
                pre(pe, product, i + (AHEAD // 2 + 1), 0)
                outs(i * 2 + 1, 1)
            pre(pe, product, PAIRS_E - 1, 1)
            outs(PAIRS_E - 2, 0)
            outs(PAIRS_E - 1, 1)
            pe.wait_ge(dn["acc"], 4 + OUT_TILES * PAIRS_E)
            for m in range(2 * NT):
                t0, w = TILES[m // 2]
                if m >= 2:
                    pe.wait_ge(dn["yadd"], m - 1)
                for j in range(4):
                    c = 4 * (m % 2) + j
                    if w == P:
                        last = nc.tensor.transpose(quad(m % 2)[:, j, :], y_t[:, c, t0:t0 + w], ident)
                    else:
                        last = nc.tensor.matmul(quad(m % 2)[0:w, j, :], y_t[:, c, t0:t0 + w], ident, start=True, stop=True)
                last.then_inc(dn["yturn"], 1)

        def act_dense(act, chain):
            def pair(g, s, x, more=True):
                if more:
                    split_next_u(act, x, s)
                act.wait_ge(dn["outs"], OUT_TILES * g + OUT_TILES)
                for j in range(2):
                    act.wait_ge(v_in[j], 16 * g + 16)
                    nc.scalar.activation(v_hi[2 * s + j][:], v_raw[j][:], ACT.Copy).then_inc(dn["vhi"], 1)
                act.wait_ge(dn["mul"], 2 * g + 1)
                nc.scalar.activation(a_hi[2 * s][:], act_l[s][:], ACT.Copy).then_inc(dn["ahi"], 1)
                act.wait_ge(dn["alo"], 2 * g + 2)
                gelu(act, x, s)
                act.wait_ge(dn["mul"], 2 * g + 2)
                nc.scalar.activation(a_hi[2 * s + 1][:], act_c[s][:], ACT.Copy).then_inc(dn["ahi"], 1)

            for s in range(2):
                act.wait_ge(gate_out[s], 16 * (GBLOCKS // 2) + 16)
                act.wait_ge(act_out[s], 16 * (AHEAD // 2) + 16)
            with act.Fori(0, ITERS) as i:
                for s in range(2):
                    pair(i * 2 + s, s, i + AHEAD // 2)
            pair(PAIRS_E - 2, 0, PAIRS_E - 1)
            pair(PAIRS_E - 1, 1, PAIRS_E - 1, more=False)

        def dve_dense(dve, chain):
            tt = nc.vector.tensor_tensor

            def pair(g, s, x, i):
                dve.wait_ge(g_in[s], 16 * i + 16)
                dve.wait_ge(act_in[s], 16 * i + 16)
                for j, a in enumerate((act_l[s], act_c[s])):
                    if j:
                        dve.wait_ge(dn["gelu"], 4 * x + (2 * s + 6))
                    t3 = a[:].rearrange("p (b t) -> p b t", b=GBLOCKS)
                    tt(out=t3, in0=t3, in1=gin[s][:, :, j, :], op=ALU.mult).then_inc(dn["mul"], 1)
                    dve.wait_ge(dn["ahi"], 2 * g + (j + 1))
                    tt(out=a_lo[2 * s + j][:], in0=a[:], in1=a_hi[2 * s + j][:].bitcast(F32), op=ALU.subtract).then_inc(dn["alo"], 1)

            def accumulate(g):
                for x in range(OUT_TILES):
                    y = y_t[:, x // 2, (x % 2) * HALF:(x % 2 + 1) * HALF]
                    dve.wait_ge(dn["outs"], OUT_TILES * g + (2 * OUT_TILES + x + 1))
                    tt(out=y, in0=y, in1=bank[4 + x % 4][:, 0:HALF], op=ALU.add).then_inc(dn["acc"], 1)

            dve.wait_ge(gate_out[1], 16 * (GBLOCKS // 2) + 16)
            chain.link(nc.vector.memset(y_t[:], 0.0))
            dve.sem_inc(dn["acc"], 4)
            dve.sem_inc(dn["alo"], 4)
            with dve.Fori(0, ITERS) as i:
                for s in range(2):
                    pair(i * 2 + s, s, i + AHEAD // 2, i)
                    accumulate(i * 2 + s)
            for s in range(2):
                pair(PAIRS_E - 2 + s, s, PAIRS_E - 1, ITERS)
                accumulate(PAIRS_E - 2 + s)
            dve.wait_ge(dn["acc"], 4 + OUT_TILES * PAIRS_E)
            for m in range(2 * NT):
                t0, w = TILES[m // 2]
                dve.wait_ge(dn["yturn"], m + 1)
                x = X[0:w, m // 2, 512 * (m % 2):512 * (m % 2 + 1)].rearrange("p (j d) -> p j d", j=4)
                tt(out=x, in0=x, in1=quad(m % 2)[0:w], op=ALU.add).then_inc(dn["yadd"], 1)

        def pool_dense(pool, chain):
            def pair(g, s):
                for j in range(2):
                    pool.wait_ge(dn["vhi"], 2 * g + (j + 1))
                    nc.gpsimd.tensor_tensor(out=v_lo[2 * s + j][:], in0=v_raw[j][:], in1=v_hi[2 * s + j][:].bitcast(F32),
                                            op=ALU.subtract).then_inc(dn["vlo"], 1)

            with pool.Fori(0, ITERS) as i:
                for s in range(2):
                    lo_u(pool, i + (AHEAD // 2 + s), 1 - s)
                    pair(i * 2 + s, s)
            lo_u(pool, PAIRS_E - 1, 1)
            for s in range(2):
                pair(PAIRS_E - 2 + s, s)
        def sp_windows(sp):
            for t, (t0, w) in enumerate(TILES):
                sp.wait_ge(rope_done, t + 1)
                sp.wait_ge(proj_evac, 5 * NT + t + 1)
                if t < NT - 1:
                    sp.dma_start(k_p[t0:t0 + w, :], qk[0:w, t, 512:1024]).then_inc(kv_out, 16)
                    sp.dma_start(v_p[t0:t0 + w, :], av[0:w, t, :]).then_inc(kv_out, 16)
                else:
                    for dst, src in ((k_s, qk[0:w, t, 512:1024]), (v_s, av[0:w, t, :])):
                        for b in range(NB):
                            sp.dma_start(dst[b, PAST - NL:PAST, :], src[b * NL:(b + 1) * NL]).then_inc(kv_out, 16)

        def sp_mix(sp):
            sp.wait_ge(cso_done, 3 * BH)
            sp.dma_start(conv_out, cso[:]).then_inc(out_done, 16)
            sp_delta(sp)
            sp_sample(sp)
            sp_ffn(sp)

        @block.sync
        def _(sp):
            for t in range(NT):
                src = x_p[t * P:(t + 1) * P, :] if t < NT - 1 else x_s
                sp.dma_start(X[0:TILES[t][1], t, :], src).then_inc(x_in[t], 16)
                if t == 0:
                    sp.dma_start(nmix_b[:], nmix.partition_broadcast(P)).then_inc(consts_in, 16)
                    sp.dma_start(sq[:], squares).then_inc(consts_in, 16)
                    sp.dma_start(wg8_raw[:], wg8).then_inc(consts_in, 16)
            for k in range(NW1):
                if k >= 2:
                    sp.wait_ge(w_hi_ready, k - 1)
                    sp.wait_ge(w_lo_ready, k - 1)
                sp.dma_start(w_raw[k % 2][:], win[order1[k]]).then_inc(w_in[k % 2], 16)
                if k == 9:
                    sp_windows(sp)
                if k == 0:
                    for dst, src in ((pos[:], pos_t), (qkw_b[:], qkw.partition_broadcast(P)), (convw_t[:], convw),
                                     (dnw_b[:], dnw.partition_broadcast(P)), (gconst[:, 0, :], alog.partition_broadcast(P)),
                                     (gconst[:, 1, :], dtb.partition_broadcast(P)), (cst[:], conv_state),
                                     (lncp[:], lnc_p), (lncs[:], lnc_s)):
                        sp.dma_start(dst, src).then_inc(small_in, 16)
            sp_mix(sp)

        @block.scalar
        def _(act):
            chain = Chain(act, act_chain)
            act.wait_ge(dve_chain, 1)
            for t, (t0, w) in enumerate(TILES):
                act.wait_ge(x_in[t], 16)
                chain.link(nc.scalar.activation(tmp1[0:w, :], X[0:w, t, :], ACT.Square, accum_out=stat[0:w, 0, t:t + 1]))
                act.sem_inc(ssq_ready, 1)
            act.wait_ge(var_ready, 1)
            nc.scalar.activation(stat[:, 1, :], stat[:, 1, :], ACT.Sqrt).then_inc(rstd_ready, 1)

            def split_hi(k):
                act.wait_ge(w_in[k % 2], 16 * (k // 2 + 1))
                if k >= 2:
                    act.wait_ge(w_used, k - 1)
                if k % 2 == 0:
                    copy_cache(act, k // 2)
                nc.scalar.activation(w_hi[:, k % 2], w_raw[k % 2][:], ACT.Copy).then_inc(w_hi_ready, 1)

            split_hi(0)
            for m in range(2 * NT):
                t0, w = TILES[m // 2]
                act.wait_ge(xs_turned, m + 1)
                nc.scalar.activation(xn_hi[:, 4 * (m % 2):4 * (m % 2) + 4, t0:t0 + w], quad(m % 2, w), ACT.Copy)\
                    .then_inc(xn_hi_ready, 1)
            split_hi(1)
            uses = 0
            for k in range(8):
                for t, (t0, w) in enumerate(TILES):
                    act.wait_ge(proj_ready, uses + 1)
                    src = bank[2 + uses % 4][rows(t), 0:WC]
                    if k < 4:
                        dst = qk[0:w, t, k * WC:(k + 1) * WC]
                    elif k < 6:
                        dst = av[0:w, t, (k - 4) * WC:(k - 3) * WC]
                    else:
                        dst = bz[0:w, t, (k - 6) * WC:(k - 5) * WC]
                    nc.scalar.activation(dst, src, ACT.Silu if k >= 6 else ACT.Copy).then_inc(proj_evac, 1)
                    uses += 1
                split_hi(k + 2)
                if k == 4:
                    act.wait_ge(rope_var, NT)
                    nc.scalar.activation(ropes[:], ropes[:], ACT.Sqrt).then_inc(rope_rs, 1)
            for h in range(2):
                act.wait_ge(proj_ready, uses + 1)
                nc.scalar.activation(g8t[:, h * HALF:(h + 1) * HALF], bank[2 + uses % 4][0:2 * BH, 0:HALF], ACT.Copy).then_inc(proj_evac, 1)
                uses += 1
            act.wait_ge(gates_dve, 1)
            chain.mark(nc.scalar.activation(beta[:], g8[:, :, 0:BH], ACT.Sigmoid))
            chain.mark(nc.scalar.activation(nega[:], gconst[:, 0, :], ACT.Exp))
            chain.link(nc.scalar.activation(gl[:], gl[:], ACT.Exp, scale=-1.0))
            act.sem_inc(gates_act, 1)
            act.wait_ge(gates_dve, 2)
            chain.link(nc.scalar.activation(gl[:], gl[:], ACT.Ln))
            act.sem_inc(gates_act, 1)
            E0 = 3 + SEQ

            def silu(c):
                act.wait_ge(conv_done, c + 1)
                if c == 0:
                    act.wait_ge(qk_turned, 2 * NT)
                    act.wait_ge(kv_out, 16 * NKV)
                nc.scalar.activation(co[:, c, :], cy[:, c % 2, :], ACT.Silu).then_inc(silu_done, 1)

            for c in range(3 * BH):
                if c == 0:
                    act.wait_ge(rope_done, NT)
                    act.wait_ge(qkt_ready, 2 * NT)
                if c >= 2:
                    act.wait_ge(conv_done, c - 1)
                    act.wait_ge(cso_done, c - 1)
                slot = ext[:, c % 2, :]
                act.wait_ge(proj_ready, uses + 1)
                nc.scalar.activation(slot[:, 3:3 + HALF], bank[2 + uses % 4][:, 0:HALF], ACT.Copy).then_inc(proj_evac, 1)
                uses += 1
                act.wait_ge(proj_ready, uses + 1)
                b = bank[2 + uses % 4]
                chain.mark(nc.scalar.activation(slot[:, 3 + HALF:3 + SEQ], b[:, 0:SEQ - HALF], ACT.Copy))
                nc.scalar.activation(slot[:, E0:E0 + NB * 7].rearrange("p (b j) -> p b j", b=NB)[:, :, 3:7],
                                     b[:, SEQ - HALF:HALF].rearrange("p (b j) -> p b j", b=NB), ACT.Copy)\
                    .then_inc(proj_evac, 1)
                chain.join()
                act.wait_ge(proj_evac, uses + 1)
                act.sem_inc(ext_ready, 1)
                uses += 1
                if c % 2 and 8 + c // 2 + 2 < NW1:
                    split_hi(8 + c // 2 + 2)
                if c:
                    silu(c - 1)
            silu(3 * BH - 1)
            act.wait_ge(l2_inv, 1)
            chain.mark(nc.scalar.activation(l2r[:, 0:BH, :], l2r[:, 0:BH, :], ACT.Sqrt, scale=1.0 / BD))
            chain.link(nc.scalar.activation(l2r[:, BH:, :], l2r[:, BH:, :], ACT.Sqrt))
            act.sem_inc(l2_rt, 1)
            act_attend(act, chain)
            act_delta(act, chain)
            act_sample(act, chain)
            act_ffn(act, chain)

        @block.vector
        def _(dve):
            chain = Chain(dve, dve_chain)
            chain.mark(nc.vector.memset(stat[:], 1.0))
            chain.mark(nc.vector.memset(ropes[:], 1.0))
            chain.mark(nc.vector.memset(g8[:], 0.0))
            chain.mark(nc.vector.memset(l2r[:], 1.0))
            dve.wait_ge(ssq_ready, NT)
            chain.link(nc.vector.tensor_scalar(stat[:, 1, :], stat[:, 0, :], 1.0 / D, EPS, ALU.mult, ALU.add))
            nc.vector.reciprocal(stat[:, 1, :], stat[:, 1, :]).then_inc(var_ready, 1)
            dve.wait_ge(rstd_ready, 1)
            dve.wait_ge(consts_in, 16 * NCONST)

            def scale_tokens(t):
                t0, w = TILES[t]
                if t >= 2:
                    dve.wait_ge(xs_turned, 2 * (t - 1))
                nc.vector.scalar_tensor_tensor(out=xs[0:w, t % 2, :], in0=X[0:w, t, :], scalar=stat[0:w, 1, t:t + 1],
                                               in1=nmix_b[0:w, :], op0=ALU.mult, op1=ALU.mult).then_inc(xs_ready, 1)
            scale_tokens(0)
            for m in range(2 * NT):
                t0, w = TILES[m // 2]
                if m % 2 == 0 and m // 2 + 1 < NT:
                    scale_tokens(m // 2 + 1)
                hi = xn_hi[:, 4 * (m % 2):4 * (m % 2) + 4, t0:t0 + w].bitcast(F32)
                dve.wait_ge(xn_hi_ready, m + 1)
                nc.vector.tensor_tensor(out=xn_lo[:, 4 * (m % 2):4 * (m % 2) + 4, t0:t0 + w], in0=quad(m % 2, w),
                                        in1=hi, op=ALU.subtract).then_inc(xn_lo_ready, 1)
            dve.wait_ge(small_in, 16 * 9)
            for j in range(2):
                chain.mark(nc.vector.tensor_tensor(out=cw[:, :, j, :], in0=pos[:, 0], in1=bc(qkw_b[:, j, 0, :], 1, NT), op=ALU.mult))
                chain.mark(nc.vector.tensor_tensor(out=sw[:, :, j, :], in0=pos[:, 1], in1=bc(qkw_b[:, j, 1, :], 1, NT), op=ALU.mult))
            chain.join()
            for t, (t0, w) in enumerate(TILES):
                dve.wait_ge(proj_evac, 3 * NT + t + 1)
                chain.link(nc.vector.tensor_tensor(out=tmp1[0:w, :], in0=qk[0:w, t, :], in1=qk[0:w, t, :], op=ALU.mult))
                chain.link(nc.vector.tensor_reduce(ropes[0:w, t, :], tmp1[0:w, :].rearrange("p (h e) -> p h e", e=AD),
                                                   axis=AX.X, op=ALU.add))
                chain.link(nc.vector.tensor_scalar(ropes[0:w, t, :], ropes[0:w, t, :], 1.0 / AD, EPS, ALU.mult, ALU.add))
                nc.vector.reciprocal(ropes[0:w, t, :], ropes[0:w, t, :]).then_inc(rope_var, 1)
            dve.wait_ge(rope_rs, 1)
            chain.link(nc.vector.tensor_scalar(ropes[:, :, 0:8], ropes[:, :, 0:8], AD ** -0.5, None, ALU.mult))
            for t, (t0, w) in enumerate(TILES):
                q4 = qk[0:w, t, :].rearrange("p (j h e) -> p j h e", j=2, e=AD)
                q3 = qk[0:w, t, :].rearrange("p (h e) -> p h e", e=AD)
                t4 = tmp1[0:w, :].rearrange("p (j h e) -> p j h e", j=2, e=AD)
                u4 = tmp2[0:w, :].rearrange("p (j h e) -> p j h e", j=2, e=AD)
                chain.link(nc.vector.tensor_tensor(out=q3, in0=q3, in1=bc(ropes[0:w, t, :], 2, AD), op=ALU.mult))
                H = AD // 2
                chain.mark(nc.vector.tensor_tensor(out=t4, in0=q4, in1=bc(cw[0:w, t], 2, AH), op=ALU.mult))
                chain.mark(nc.vector.tensor_tensor(out=u4[:, :, :, 0:H], in0=q4[:, :, :, H:AD], in1=bc(sw[0:w, t, :, 0:H], 2, AH), op=ALU.mult))
                chain.link(nc.vector.tensor_tensor(out=u4[:, :, :, H:AD], in0=q4[:, :, :, 0:H], in1=bc(sw[0:w, t, :, H:AD], 2, AH), op=ALU.mult))
                nc.vector.tensor_tensor(out=qk[0:w, t, :], in0=tmp1[0:w, :], in1=tmp2[0:w, :], op=ALU.add).then_inc(rope_done, 1)
                if t < NT - 1:
                    dve.wait_ge(rope_done, t + 1)
            for m in range(2 * NT):
                t0, w = TILES[m // 2]
                dve.wait_ge(qk_turned, m + 1)
                nc.vector.tensor_copy(qkt[:, 4 * (m % 2):4 * (m % 2) + 4, t0:t0 + w], quad(m % 2, w)).then_inc(qkt_ready, 1)
            dve.wait_ge(proj_evac, 8 * NT)
            bz4 = bz[:, 0:NT - 1, :].rearrange("p t (h e) -> p (t h) e", e=BD)
            chain.mark(nc.vector.tensor_tensor(out=bz4, in0=bz4, in1=bc(dnw_b[:], 1, (NT - 1) * BH), op=ALU.mult))
            bz1 = bz[0:NB * NL, NT - 1, :].rearrange("p (h e) -> p h e", e=BD)
            chain.mark(nc.vector.tensor_tensor(out=bz1, in0=bz1, in1=bc(dnw_b[0:NB * NL], 1, BH), op=ALU.mult))
            dve.wait_ge(logits_done, 2)
            logits = bank[7][:, 0:2 * BH * NT].rearrange("p (t c) -> p t c", t=NT)
            chain.mark(nc.vector.tensor_copy(g8[:, 0:NT - 1, :], logits[:, 0:NT - 1, :]))
            chain.link(nc.vector.tensor_copy(g8[0:NB * NL, NT - 1, :], logits[0:NB * NL, NT - 1, :]))
            chain.link(nc.vector.tensor_tensor(out=gz[:], in0=g8[:, :, BH:2 * BH], in1=bc(gconst[:, 1, :], 1, NT), op=ALU.add))
            chain.link(nc.vector.scalar_tensor_tensor(out=gl[:], in0=gz[:], scalar=-1.0, in1=gz[:], op0=ALU.mult, op1=ALU.max))
            dve.sem_inc(gates_dve, 1)
            chain.mark(nc.vector.tensor_scalar(gz[:], gz[:], 0.0, None, ALU.max))
            dve.wait_ge(gates_act, 1)
            chain.link(nc.vector.tensor_scalar(gl[:], gl[:], 1.0, None, ALU.add))
            dve.sem_inc(gates_dve, 1)
            dve.wait_ge(gates_act, 2)
            chain.link(nc.vector.tensor_tensor(out=gl[:], in0=gl[:], in1=gz[:], op=ALU.add))
            chain.link(nc.vector.scalar_tensor_tensor(out=gate_g[:], in0=gl[:], scalar=-1.0, in1=bc(nega[:], 1, NT), op0=ALU.mult, op1=ALU.mult))
            dve.sem_inc(gates_dve, 1)
            dve.wait_ge(qkt_ready, 2 * NT)
            E0 = 3 + SEQ
            for s in range(2):
                chain.link(nc.vector.memset(ext[:, s, 0:3], 0.0))
            for c in range(3 * BH):
                dve.wait_ge(ext_ready, c + 1)
                dve.wait_ge(ext_state, c + 1)
                if c >= 2:
                    dve.wait_ge(silu_done, c - 1)
                slot = ext[:, c % 2, :]
                es = slot[:, E0:E0 + NB * 7].rearrange("p (b j) -> p b j", b=NB)
                yp_, ys_ = cy[:, c % 2, 0:SEQ], cy[:, c % 2, SEQ:TOK].rearrange("p (b j) -> p b j", b=NB)
                chain.mark(nc.vector.tensor_scalar(yp_, slot[:, 0:SEQ], convw_t[:, c, 0:1], None, ALU.mult))
                chain.link(nc.vector.tensor_scalar(ys_, es[:, :, 0:NL], convw_t[:, c, 0:1], None, ALU.mult))
                for j in range(1, CONV):
                    chain.mark(nc.vector.scalar_tensor_tensor(out=yp_, in0=slot[:, j:j + SEQ], scalar=convw_t[:, c, j:j + 1],
                                                              in1=yp_, op0=ALU.mult, op1=ALU.add))
                    chain.link(nc.vector.scalar_tensor_tensor(out=ys_, in0=es[:, :, j:j + NL], scalar=convw_t[:, c, j:j + 1],
                                                              in1=ys_, op0=ALU.mult, op1=ALU.add))
                dve.sem_inc(conv_done, 1)
            dve.wait_ge(l2_sum, 1)
            sums = bank[0][:, 0:2 * BH * NT].rearrange("p (c t) -> p c t", t=NT)
            chain.mark(nc.vector.tensor_scalar(l2r[:, :, 0:NT - 1], sums[:, :, 0:NT - 1], EPS, None, ALU.add))
            chain.link(nc.vector.tensor_scalar(l2r[0:NB * NL, :, NT - 1], sums[0:NB * NL, :, NT - 1], EPS, None, ALU.add))
            nc.vector.reciprocal(l2r[:], l2r[:]).then_inc(l2_inv, 1)
            for c in range(2 * BH):
                dve.wait_ge(l2_rows, c + 1)
                nc.vector.tensor_tensor(out=co[:, c, 0:SEQ], in0=co[:, c, 0:SEQ], in1=bank[L2_BANKS[c % 4]][:], op=ALU.mult).then_inc(l2_done, 1)
            rows_s = bank[4][:, 0:2 * BH * NB * NL].rearrange("p (c t) -> p c t", t=NB * NL)
            nc.vector.tensor_tensor(out=co[:, 0:2 * BH, SEQ:TOK], in0=co[:, 0:2 * BH, SEQ:TOK], in1=rows_s, op=ALU.mult).then_inc(l2_done, 1)
            dve_attend(dve, chain)
            dve_delta(dve, chain)
            dve_sample(dve, chain)
            dve_ffn(dve, chain)

        @block.gpsimd
        def _(pool):
            chain = Chain(pool, pool_chain)

            def split_lo(k):
                pool.wait_ge(w_hi_ready, k + 1)
                if k >= 2:
                    pool.wait_ge(w_used, k - 1)
                nc.gpsimd.tensor_tensor(out=w_lo[:, k % 2], in0=w_raw[k % 2][:], in1=w_hi[:, k % 2].bitcast(F32),
                                        op=ALU.subtract).then_inc(w_lo_ready, 1)
            pool.wait_ge(consts_in, 16 * NCONST)
            chain.link(nc.gpsimd.tensor_copy(wg8_hi[:], wg8_raw[:]))
            nc.gpsimd.tensor_tensor(out=wg8_lo[:], in0=wg8_raw[:], in1=wg8_hi[:].bitcast(F32), op=ALU.subtract).then_inc(logits_done, 1)
            split_lo(0)
            split_lo(1)
            for k in range(8):
                split_lo(k + 2)
            pool.wait_ge(small_in, 16 * 9)
            pool.wait_ge(rope_done, NT)
            E0 = 3 + SEQ
            for c in range(3 * BH):
                slot = ext[:, c % 2, :]
                es = slot[:, E0:E0 + NB * 7].rearrange("p (b j) -> p b j", b=NB)
                if c >= 2:
                    pool.wait_ge(conv_done, c - 1)
                nc.gpsimd.tensor_copy(es[:, :, 0:3], cst[:, c]).then_inc(ext_state, 1)
                pool.wait_ge(ext_ready, c + 1)
                chain.mark(nc.gpsimd.tensor_copy(cso[:, c, 0:3], slot[:, SEQ:SEQ + 3]))
                chain.link(nc.gpsimd.tensor_copy(cso[:, c, 3:27].rearrange("p (b j) -> p b j", b=NB), es[:, :, 4:7]))
                pool.sem_inc(cso_done, 1)
                if 2 <= c < 2 + 2 * BH:
                    pool.wait_ge(silu_done, c - 1)
                    nc.gpsimd.tensor_tensor(out=l2s[:, c - 2, :], in0=co[:, c - 2, :], in1=co[:, c - 2, :], op=ALU.mult).then_inc(l2_sq, 1)
                if c % 2 and 8 + c // 2 + 2 < NW1:
                    split_lo(8 + c // 2 + 2)
            pool_mix(pool, chain)

        @block.tensor
        def _(pe):
            def product(out, pairs):
                n = len(pairs)
                for i, (ah, al, bh, bl) in enumerate(pairs):
                    nc.tensor.matmul(out, ah, bh, start=i == 0, stop=False)
                    nc.tensor.matmul(out, ah, bl, start=False, stop=False)
                    last = nc.tensor.matmul(out, al, bh, start=False, stop=i == n - 1)
                return last

            pe.wait_ge(consts_in, 16 * NCONST)
            for m in range(2 * NT):
                t0, w = TILES[m // 2]
                pe.wait_ge(xs_ready, m // 2 + 1)
                if m >= 2:
                    pe.wait_ge(xn_lo_ready, m - 1)
                for j in range(4):
                    c = 4 * (m % 2) + j
                    last = nc.tensor.transpose(quad(m % 2, w)[:, j, :], xs[0:w, (m // 2) % 2, c * P:(c + 1) * P], ident[0:w, 0:w])
                last.then_inc(xs_turned, 1)
            pe.wait_ge(xn_lo_ready, 2 * NT)
            uses = 0
            for k in range(8):
                pe.wait_ge(w_lo_ready, k + 1)
                for t in range(NT):
                    if uses >= 4:
                        pe.wait_ge(proj_evac, uses - 3)
                    tok = token_columns(t)
                    last = product(bank[2 + uses % 4][:, 0:WC],
                                   [(xn_hi[:, c, tok], xn_lo[:, c, tok], w_hi[:, k % 2, c, :], w_lo[:, k % 2, c, :])
                                    for c in range(CH)])
                    last.then_inc(proj_ready, 1)
                    uses += 1
                pe.wait_ge(proj_ready, uses)
                pe.sem_inc(w_used, 1)
            pe.wait_ge(logits_done, 1)
            for h in range(2):
                pe.wait_ge(proj_evac, uses - 3)
                cols = slice(h * HALF, (h + 1) * HALF)
                product(bank[2 + uses % 4][0:2 * BH, 0:HALF],
                        [(wg8_hi[:, c, :], wg8_lo[:, c, :], xn_hi[:, c, cols], xn_lo[:, c, cols])
                         for c in range(CH)]).then_inc(proj_ready, 1)
                uses += 1
            for m in range(2 * NT):
                t0, w = TILES[m // 2]
                pe.wait_ge(rope_done, m // 2 + 1)
                if m >= 2:
                    pe.wait_ge(qkt_ready, m - 1)
                for j in range(4):
                    c = 4 * (m % 2) + j
                    last = nc.tensor.transpose(quad(m % 2, w)[:, j, :], qk[0:w, m // 2, c * P:(c + 1) * P], ident[0:w, 0:w])
                last.then_inc(qk_turned, 1)
            pe.wait_ge(proj_evac, uses)
            for t, (t0, w) in enumerate(TILES):
                last = nc.tensor.transpose(bank[7][0:w, 2 * BH * t:2 * BH * (t + 1)], g8t[:, t0:t0 + w], ident[0:2 * BH, 0:2 * BH])
            last.then_inc(logits_done, 1)
            for c in range(3 * BH):
                k = 8 + c // 2
                pe.wait_ge(w_lo_ready, k + 1)
                wcols = slice((c % 2) * P, (c % 2) * P + P)
                for h in range(2):
                    pe.wait_ge(proj_evac, uses - 3)
                    cols = slice(h * HALF, (h + 1) * HALF)
                    product(bank[2 + uses % 4][:, 0:HALF],
                            [(w_hi[:, k % 2, i, wcols], w_lo[:, k % 2, i, wcols], xn_hi[:, i, cols], xn_lo[:, i, cols])
                             for i in range(CH)]).then_inc(proj_ready, 1)
                    uses += 1
                if c % 2:
                    pe.wait_ge(proj_ready, uses)
                    pe.sem_inc(w_used, 1)
            pe.wait_ge(proj_evac, uses)
            pe.wait_ge(qkt_ready, 2 * NT)
            for c in range(2 * BH):
                pe.wait_ge(l2_sq, c + 1)
                for t, (t0, w) in enumerate(TILES):
                    last = nc.tensor.matmul(bank[0][0:w, c * NT + t:c * NT + t + 1], l2s[:, c, t0:t0 + w], ones[:, 0:1], start=True, stop=True)
            last.then_inc(l2_sum, 1)
            pe.wait_ge(l2_rt, 1)
            for c in range(2 * BH):
                if c >= 4:
                    pe.wait_ge(l2_done, c - 3)
                for t, (t0, w) in enumerate(TILES):
                    out = bank[L2_BANKS[c % 4]][:, t0:t0 + w] if t < NT - 1 else bank[4][:, c * w:(c + 1) * w]
                    last = nc.tensor.matmul(out, l2r[0:w, c, t:t + 1].broadcast_to([w, P]), ident[0:w, 0:w], start=True, stop=True)
                last.then_inc(l2_rows, 1)
            pe_attend(pe)
            pe_delta(pe)
            pe_sample(pe)
            pe_ffn(pe, product)


def kernel(**inputs):
    import concourse.bacc as bacc
    from concourse.bass_utils import run_bass_kernel_spmd as run

    a = {k: np.asarray(v) for k, v in inputs.items()}

    def tiles(w, cols):
        d, n = w.shape
        return np.ascontiguousarray(w.reshape(CH, P, n // cols, cols).transpose(2, 1, 0, 3))

    w_in = a["w_in"][0]
    eu = tiles(a["expert_u"][0].T, P)
    main = 14 * WC
    qkw = np.stack([a["q_norm_w"][0], a["k_norm_w"][0]])
    qkw = np.stack([qkw, np.roll(qkw, AD // 2, axis=1)], 1)
    arrays = {
        "x_p": a["x_prompt"].reshape(SEQ, D),
        "x_s": a["x_sample"].reshape(NB * NL, D),
        "kc": a["cache_k_win"].reshape(NB, PAST, AH * AD),
        "vc": a["cache_v_win"].reshape(NB, PAST, AH * AD),
        "conv_state": a["state_conv"][0].transpose(2, 0, 1).reshape(3 * BH, P, NB, 3).transpose(1, 0, 2, 3),
        "s0": a["state_delta"].reshape(NB, BH, BD, BD),
        "nmix": a["norm_mix_w"].reshape(D),
        "win": tiles(w_in[:, :main], WC),
        "wg8": tiles(w_in[:, main:], 8)[0],
        "qkw": qkw,
        "convw": a["conv_w"][0].reshape(CONV, 3 * BH, P).transpose(2, 1, 0),
        "alog": a["a_log"].reshape(BH),
        "dtb": a["dt_bias"].reshape(BH),
        "dnw": a["delta_norm_w"].reshape(BD),
        "wout": tiles(a["w_out"][0], WC),
        "nffn": a["norm_ffn_w"].reshape(D),
        "wpq": tiles(a["w_pq"][0], WC),
        "skt": a["sub_keys"][0].transpose(2, 0, 1),
        "eu": np.concatenate([eu[0::2], eu[1::2]]),
        "ev": a["expert_v"][0].reshape(PK, PK, D),
        "pos_t": position_tables(),
        "lnc_p": prompt_log_counts(),
        "lnc_s": sample_log_counts(),
        "squares": square_tables(),
    }
    outs = {
        "y_p": (SEQ, D), "y_s": (NB * NL, D), "k_p": (SEQ, AH * AD), "v_p": (SEQ, AH * AD),
        "conv_out": (P, 3 * BH, (NB + 1) * 3), "s_p": (BH, BD, BD),
        "k_s": (NB, PAST, AH * AD), "v_s": (NB, PAST, AH * AD), "s_s": (NB, BH, BD, BD),
    }
    nc = bacc.Bacc("TRN2", target_bir_lowering=False, num_devices=1)
    args = []
    for name, v in arrays.items():
        arrays[name] = np.ascontiguousarray(v)
        args.append(nc.dram_tensor(name, v.shape, F32, kind="ExternalInput").ap())
    for name, shape in outs.items():
        args.append(nc.dram_tensor(name, shape, F32, kind="ExternalOutput").ap())
    args.append(nc.dram_tensor("gates_dram", (GBLOCKS, P, PK, GT), F32, kind="Internal").ap())
    args.append(nc.dram_tensor("acts_dram", (AHEAD, P, TOK), F32, kind="Internal").ap())
    hybrid_step(nc, *args)
    r = run(nc, [arrays], core_ids=[0]).results[0]
    conv = r["conv_out"].transpose(1, 0, 2).reshape(3 * BH * P, NB + 1, 3).transpose(1, 2, 0)
    return (
        r["y_p"].reshape(1, SEQ, D), r["y_s"].reshape(NB, NL, D),
        r["k_p"].reshape(1, 1, SEQ, AH, AD), r["v_p"].reshape(1, 1, SEQ, AH, AD),
        np.ascontiguousarray(conv[0:1])[None], r["s_p"][None, None],
        r["k_s"].reshape(1, NB, PAST, AH, AD), r["v_s"].reshape(1, NB, PAST, AH, AD),
        np.ascontiguousarray(conv[1:])[None], r["s_s"][None],
    )
```
